# Optimizing a Trainium2 kernel written in Bass

```python
import math
import jax
import jax.numpy as jnp
from jax import lax
import numpy as np

D_MODEL = 1024
BATCH = 1
SEQ = 256
DEPTH = 4
DEC_BATCH = 8
DEC_SEQ = 8
PAST_LEN = 1024
PAGE_SIZE = 128

N_MIXERS = 3
N_RWKV = (DEPTH + 2) // 3
N_MLA = (DEPTH + 1) // 3
N_MAMBA = DEPTH // 3

RW_HEAD = 64
RW_HEADS = D_MODEL // RW_HEAD
RW_DECAY_LORA = 64
RW_AAA_LORA = 64
RW_MV_LORA = 32
RW_GATE_LORA = 160
RW_LNX_EPS = 64e-5

MLA_HEADS = 16
MLA_Q_LORA = 512
MLA_KV_LORA = 256
MLA_NOPE = 64
MLA_ROPE = 32
MLA_V = 64
MLA_SCALE = 1.0 / math.sqrt(MLA_NOPE + MLA_ROPE)
ROPE_THETA = 10000.0
Q_BLOCK = 128

MB_INNER = 2 * D_MODEL
MB_HEAD = 64
MB_HEADS = MB_INNER // MB_HEAD
MB_GROUPS = 4
MB_STATE = 128
MB_CONV = 4
MB_CONV_DIM = MB_INNER + 2 * MB_GROUPS * MB_STATE
MB_IN_DIM = MB_INNER + MB_CONV_DIM + MB_HEADS
MB_CHUNK = 128

FFN_HIDDEN = 4 * D_MODEL
NORM_EPS = 1e-6
F32 = jnp.float32

kernel_name = 'hybrid_rwkv7_mla_mamba2_decode_step'

def rmsnorm(x, g):
    xf = x.astype(F32)
    y = xf * lax.rsqrt(jnp.mean(xf * xf, axis=-1, keepdims=True) + NORM_EPS)
    return (y * g.astype(F32)).astype(x.dtype)

def rope(x, pos):
    half = MLA_ROPE // 2
    inv = ROPE_THETA ** (-jnp.arange(half, dtype=F32) / half)
    ang = pos.astype(F32)[:, None] * inv[None, :]
    shape = (pos.shape[0],) + (1,) * (x.ndim - 3) + (half,)
    cos = jnp.cos(ang).reshape(shape).astype(x.dtype)
    sin = jnp.sin(ang).reshape(shape).astype(x.dtype)
    x1, x2 = x[..., :half], x[..., half:]
    return jnp.concatenate([x1 * cos - x2 * sin, x2 * cos + x1 * sin], axis=-1)

def sqrelu_ffn(x, w1, w2):
    return jnp.square(jax.nn.relu(x @ w1)) @ w2

def _wkv_step(S, inp):
    r_t, w_t, k_t, v_t, a_t, b_t = inp
    sa = jnp.einsum('bhij,bhj->bhi', S, a_t)
    S = S * w_t[:, :, None, :] + sa[..., None] * b_t[:, :, None, :] + v_t[..., None] * k_t[:, :, None, :]
    return S, jnp.einsum('bhij,bhj->bhi', S, r_t)

def rwkv_mix(x, shift, wkv, v_first, vres, mu, w_rkv, w0, w1, w2, a0, a1, a2,
             g1, g2, k_k, k_a, r_k, lnx_w, lnx_b, w_o):
    b, t, c = x.shape
    hd = (b, t, RW_HEADS, RW_HEAD)
    x_prev = jnp.concatenate([shift[:, None].astype(x.dtype), x[:, :-1]], axis=1)
    xm = x[None] + (x_prev - x)[None] * mu[:, None, None, :]
    rkv = jnp.einsum('pbtc,pcd->pbtd', xm[:3], w_rkv)
    r, k, v = rkv[0], rkv[1], rkv[2]
    w_log = -jax.nn.softplus(-(w0 + jnp.tanh(xm[3] @ w1) @ w2)) - 0.5
    decay = jnp.exp(-jnp.exp(w_log.astype(F32)))
    if vres is None:
        v_first = v
    else:
        v0, v1, v2 = vres
        v = v + (v_first - v) * jax.nn.sigmoid(v0 + (xm[2] @ v1) @ v2)
    a = jax.nn.sigmoid(a0 + (xm[4] @ a1) @ a2)
    g = jax.nn.sigmoid(xm[5] @ g1) @ g2
    kk = (k * k_k).reshape(hd).astype(F32)
    kk = kk / jnp.maximum(jnp.linalg.norm(kk, axis=-1, keepdims=True), 1e-12)
    k = k * (1.0 + (a - 1.0) * k_a)
    rh, kh, vh, ah = [z.reshape(hd).astype(F32) for z in (r, k, v, a)]
    seq = tuple(jnp.moveaxis(z, 1, 0) for z in (rh, decay.reshape(hd), kh, vh, -kk, kk * ah))
    S, y = lax.scan(_wkv_step, wkv.astype(F32), seq)
    y = jnp.moveaxis(y, 0, 1)
    mean = jnp.mean(y, axis=-1, keepdims=True)
    var = jnp.mean(jnp.square(y - mean), axis=-1, keepdims=True)
    y = (y - mean) * lax.rsqrt(var + RW_LNX_EPS) * lnx_w.reshape(RW_HEADS, RW_HEAD) \
        + lnx_b.reshape(RW_HEADS, RW_HEAD)
    y = y + jnp.sum(rh * kh * r_k, axis=-1, keepdims=True) * vh
    out = (y.reshape(b, t, c).astype(x.dtype) * g) @ w_o
    return out, S, x[:, -1], v_first

def mla_project(x, pos, w_in, q_norm, kv_norm, w_uq, qn_norm, qr_norm, kr_norm):
    h = x @ w_in
    q_a = h[..., :MLA_Q_LORA]
    c_raw = h[..., MLA_Q_LORA:MLA_Q_LORA + MLA_KV_LORA]
    kp_raw = h[..., MLA_Q_LORA + MLA_KV_LORA:]
    q = jnp.einsum('btl,lhd->bthd', rmsnorm(q_a, q_norm), w_uq)
    q_nope = rmsnorm(q[..., :MLA_NOPE], qn_norm)
    q_pe = rope(rmsnorm(q[..., MLA_NOPE:], qr_norm), pos)
    c = rmsnorm(c_raw, kv_norm)
    k_pe = rope(rmsnorm(kp_raw, kr_norm), pos)
    return q_nope, q_pe, c, k_pe

def mla_keys(c, w_uk, kn_norm):
    return rmsnorm(jnp.einsum('...r,rhd->...hd', c, w_uk), kn_norm)

def mla_attend(q_nope, q_pe, k_nope, k_pe, c, mask, w_uv):
    s = jnp.einsum('bqhd,bkhd->bhqk', q_nope, k_nope) + jnp.einsum('bqhd,bkd->bhqk', q_pe, k_pe)
    s = jnp.where(mask, s.astype(F32) * MLA_SCALE, -jnp.inf)
    p = jax.nn.softmax(s, axis=-1).astype(c.dtype)
    o_lat = jnp.einsum('bhqk,bkr->bqhr', p, c)
    return jnp.einsum('bqhr,rhd->bqhd', o_lat, w_uv)

def mla_prompt(x, w_in, q_norm, kv_norm, w_uq, w_uk, w_uv, qn_norm, qr_norm, kn_norm, kr_norm, w_o):
    b, t, _ = x.shape
    pos = jnp.arange(t)
    qn, qp, c, kp = mla_project(x, pos, w_in, q_norm, kv_norm, w_uq, qn_norm, qr_norm, kr_norm)
    kn = mla_keys(c, w_uk, kn_norm)
    nb = t // Q_BLOCK
    qn_b = jnp.swapaxes(qn.reshape(b, nb, Q_BLOCK, MLA_HEADS, MLA_NOPE), 0, 1)
    qp_b = jnp.swapaxes(qp.reshape(b, nb, Q_BLOCK, MLA_HEADS, MLA_ROPE), 0, 1)
    kpos = jnp.arange(t)

    def block(args):
        qn_i, qp_i, i = args
        qpos = i * Q_BLOCK + jnp.arange(Q_BLOCK)
        return mla_attend(qn_i, qp_i, kn, kp, c, kpos[None, :] <= qpos[:, None], w_uv)

    o = lax.map(block, (qn_b, qp_b, jnp.arange(nb)))
    o = jnp.swapaxes(o, 0, 1).reshape(b, t, MLA_HEADS * MLA_V)
    return o @ w_o, c, kp

def mla_sample(x, pool_c, pool_kp, page_table, w_in, q_norm, kv_norm, w_uq, w_uk, w_uv,
               qn_norm, qr_norm, kn_norm, kr_norm, w_o):
    b, t, _ = x.shape
    pos = PAST_LEN + jnp.arange(t)
    qn, qp, c, kp = mla_project(x, pos, w_in, q_norm, kv_norm, w_uq, qn_norm, qr_norm, kr_norm)
    n_past = page_table.shape[1] * PAGE_SIZE
    mask = jnp.concatenate([jnp.ones((t, n_past), bool), jnp.tril(jnp.ones((t, t), bool))], axis=1)

    def one_seq(args):
        pt, qn_s, qp_s, c_s, kp_s = args
        c_all = jnp.concatenate([pool_c[pt].reshape(n_past, MLA_KV_LORA), c_s.astype(pool_c.dtype)], axis=0)
        kp_all = jnp.concatenate([pool_kp[pt].reshape(n_past, MLA_ROPE), kp_s.astype(pool_kp.dtype)], axis=0)
        kn_all = mla_keys(c_all, w_uk, kn_norm)
        return mla_attend(qn_s[None], qp_s[None], kn_all[None], kp_all[None], c_all[None], mask, w_uv)[0]

    o = lax.map(one_seq, (page_table, qn, qp, c, kp))
    return o.reshape(b, t, MLA_HEADS * MLA_V) @ w_o, c, kp

def ssd_scan(xh, dt, A, Bm, Cm, h0, chunk):
    b, t = xh.shape[0], xh.shape[1]
    nc = t // chunk
    r = MB_HEADS // MB_GROUPS

    def to_chunks(z):
        return jnp.moveaxis(z.reshape((b, nc, chunk) + z.shape[2:]), 1, 0)

    xc = to_chunks(xh.astype(F32).reshape(b, t, MB_GROUPS, r, MB_HEAD))
    dtc = to_chunks(dt.astype(F32).reshape(b, t, MB_GROUPS, r))
    Bc = to_chunks(Bm.astype(F32))
    Cc = to_chunks(Cm.astype(F32))
    a_gr = A.reshape(MB_GROUPS, r)
    causal = jnp.tril(jnp.ones((chunk, chunk), bool))[None, :, :, None, None]

    def step(h, inp):
        x_q, dt_q, b_q, c_q = inp
        acum = jnp.cumsum(dt_q * a_gr, axis=1)
        seg = acum[:, :, None] - acum[:, None, :]
        lmat = jnp.exp(jnp.where(causal, seg, -jnp.inf))
        xdt = x_q * dt_q[..., None]
        cb = jnp.einsum('bign,bjgn->bijg', c_q, b_q)
        y = jnp.einsum('bijgr,bjgrp->bigrp', cb[..., None] * lmat, xdt)
        y = y + jnp.einsum('bign,bgrpn->bigrp', c_q, h) * jnp.exp(acum)[..., None]
        to_end = jnp.exp(acum[:, -1:] - acum)
        h = h * jnp.exp(acum[:, -1])[..., None, None] \
            + jnp.einsum('bjgn,bjgrp->bgrpn', b_q, xdt * to_end[..., None])
        return h, y

    h, ys = lax.scan(step, h0.astype(F32).reshape(b, MB_GROUPS, r, MB_HEAD, MB_STATE), (xc, dtc, Bc, Cc))
    y = jnp.moveaxis(ys, 0, 1).reshape(b, t, MB_HEADS, MB_HEAD)
    return y, h.reshape(b, MB_HEADS, MB_HEAD, MB_STATE)

def mamba_mix(x, conv_state, ssm_state, w_in, conv_w, conv_b, dt_bias, a_log, d_skip, norm_w, w_o):
    b, t, _ = x.shape
    zxbcdt = x @ w_in
    z = zxbcdt[..., :MB_INNER]
    xbc = zxbcdt[..., MB_INNER:MB_INNER + MB_CONV_DIM]
    dt_raw = zxbcdt[..., MB_INNER + MB_CONV_DIM:]
    xpad = jnp.concatenate([conv_state.astype(xbc.dtype), xbc], axis=1)
    conv = conv_b + sum(xpad[:, j:j + t] * conv_w[j] for j in range(MB_CONV))
    xbc = jax.nn.silu(conv)
    new_conv = xpad[:, t:]
    gn = MB_GROUPS * MB_STATE
    xs = xbc[..., :MB_INNER].reshape(b, t, MB_HEADS, MB_HEAD)
    Bm = xbc[..., MB_INNER:MB_INNER + gn].reshape(b, t, MB_GROUPS, MB_STATE)
    Cm = xbc[..., MB_INNER + gn:].reshape(b, t, MB_GROUPS, MB_STATE)
    dt = jax.nn.softplus(dt_raw.astype(F32) + dt_bias.astype(F32))
    A = -jnp.exp(a_log.astype(F32))
    y, h = ssd_scan(xs, dt, A, Bm, Cm, ssm_state, math.gcd(t, MB_CHUNK))
    y = y + d_skip.astype(F32)[:, None] * xs.astype(F32)
    yz = (y.reshape(b, t, MB_INNER) * jax.nn.silu(z.astype(F32))).reshape(b, t, MB_GROUPS, MB_INNER // MB_GROUPS)
    yz = rmsnorm(yz, norm_w.reshape(MB_GROUPS, MB_INNER // MB_GROUPS)).reshape(b, t, MB_INNER)
    return yz.astype(x.dtype) @ w_o, new_conv, h

def setup_inputs(seed: int = 0) -> dict:
    key = jax.random.key(seed)
    ks = iter(jax.random.split(key, 64))
    C = D_MODEL
    n_pages = PAST_LEN // PAGE_SIZE
    n_pool = (DEC_BATCH * n_pages * 5) // 4
    nv = max(N_RWKV - 1, 0)

    def nrm(shape, scale):
        return scale * jax.random.normal(next(ks), shape, F32)

    def gain(shape):
        return 1.0 + 0.02 * jax.random.normal(next(ks), shape, F32)

    def unif(shape, lo, hi):
        return jax.random.uniform(next(ks), shape, F32, lo, hi)

    dt0 = jnp.exp(unif((N_MAMBA, MB_HEADS), math.log(1e-3), math.log(1e-1)))
    page_table = jax.random.permutation(next(ks), n_pool)[:DEC_BATCH * n_pages]
    page_table = page_table.reshape(DEC_BATCH, n_pages).astype(jnp.int32)
    return {
        'x_prompt': nrm((BATCH, SEQ, C), 1.0),
        'x_sample': nrm((DEC_BATCH, DEC_SEQ, C), 1.0),
        'cache_mla_ckv': nrm((N_MLA, n_pool, PAGE_SIZE, MLA_KV_LORA), 1.0),
        'cache_mla_kpe': nrm((N_MLA, n_pool, PAGE_SIZE, MLA_ROPE), 1.0),
        'state_rwkv_wkv': nrm((N_RWKV, DEC_BATCH, RW_HEADS, RW_HEAD, RW_HEAD), 0.5),
        'state_rwkv_shift': nrm((N_RWKV, DEC_BATCH, C), 1.0),
        'state_ssm': nrm((N_MAMBA, DEC_BATCH, MB_HEADS, MB_HEAD, MB_STATE), 0.5),
        'state_conv': nrm((N_MAMBA, DEC_BATCH, MB_CONV - 1, MB_CONV_DIM), 1.0),
        'page_table': page_table,
        'norm_mix': gain((DEPTH, C)),
        'norm_ffn': gain((DEPTH, C)),
        'ffn_w1': nrm((DEPTH, C, FFN_HIDDEN), C ** -0.5),
        'ffn_w2': nrm((DEPTH, FFN_HIDDEN, C), FFN_HIDDEN ** -0.5),
        'rwkv_mu': unif((N_RWKV, 6, C), 0.0, 1.0),
        'rwkv_w_rkv': nrm((N_RWKV, 3, C, C), C ** -0.5),
        'rwkv_w0': unif((N_RWKV, C), -6.0, 1.0),
        'rwkv_w1': nrm((N_RWKV, C, RW_DECAY_LORA), C ** -0.5),
        'rwkv_w2': nrm((N_RWKV, RW_DECAY_LORA, C), 0.1 * RW_DECAY_LORA ** -0.5),
        'rwkv_a0': nrm((N_RWKV, C), 0.1),
        'rwkv_a1': nrm((N_RWKV, C, RW_AAA_LORA), C ** -0.5),
        'rwkv_a2': nrm((N_RWKV, RW_AAA_LORA, C), 0.1 * RW_AAA_LORA ** -0.5),
        'rwkv_v0': nrm((nv, C), 0.1),
        'rwkv_v1': nrm((nv, C, RW_MV_LORA), C ** -0.5),
        'rwkv_v2': nrm((nv, RW_MV_LORA, C), 0.1 * RW_MV_LORA ** -0.5),
        'rwkv_g1': nrm((N_RWKV, C, RW_GATE_LORA), C ** -0.5),
        'rwkv_g2': nrm((N_RWKV, RW_GATE_LORA, C), RW_GATE_LORA ** -0.5),
        'rwkv_k_k': 0.85 + nrm((N_RWKV, C), 0.05),
        'rwkv_k_a': 1.0 + nrm((N_RWKV, C), 0.05),
        'rwkv_r_k': nrm((N_RWKV, RW_HEADS, RW_HEAD), 0.1),
        'rwkv_lnx_w': gain((N_RWKV, C)),
        'rwkv_lnx_b': nrm((N_RWKV, C), 0.01),
        'rwkv_w_o': nrm((N_RWKV, C, C), C ** -0.5),
        'mla_w_in': nrm((N_MLA, C, MLA_Q_LORA + MLA_KV_LORA + MLA_ROPE), C ** -0.5),
        'mla_q_norm': gain((N_MLA, MLA_Q_LORA)),
        'mla_kv_norm': gain((N_MLA, MLA_KV_LORA)),
        'mla_w_uq': nrm((N_MLA, MLA_Q_LORA, MLA_HEADS, MLA_NOPE + MLA_ROPE), MLA_Q_LORA ** -0.5),
        'mla_w_uk': nrm((N_MLA, MLA_KV_LORA, MLA_HEADS, MLA_NOPE), MLA_KV_LORA ** -0.5),
        'mla_w_uv': nrm((N_MLA, MLA_KV_LORA, MLA_HEADS, MLA_V), MLA_KV_LORA ** -0.5),
        'mla_qn_norm': gain((N_MLA, MLA_NOPE)),
        'mla_qr_norm': gain((N_MLA, MLA_ROPE)),
        'mla_kn_norm': gain((N_MLA, MLA_NOPE)),
        'mla_kr_norm': gain((N_MLA, MLA_ROPE)),
        'mla_w_o': nrm((N_MLA, MLA_HEADS * MLA_V, C), (MLA_HEADS * MLA_V) ** -0.5),
        'mamba_w_in': nrm((N_MAMBA, C, MB_IN_DIM), C ** -0.5),
        'mamba_conv_w': nrm((N_MAMBA, MB_CONV, MB_CONV_DIM), MB_CONV ** -0.5),
        'mamba_conv_b': nrm((N_MAMBA, MB_CONV_DIM), 0.01),
        'mamba_dt_bias': dt0 + jnp.log(-jnp.expm1(-dt0)),
        'mamba_a_log': jnp.log(unif((N_MAMBA, MB_HEADS), 1.0, 16.0)),
        'mamba_d': 1.0 + nrm((N_MAMBA, MB_HEADS), 0.1),
        'mamba_norm': gain((N_MAMBA, MB_INNER)),
        'mamba_w_o': nrm((N_MAMBA, MB_INNER, C), MB_INNER ** -0.5),
    }

def reference(x_prompt, x_sample, cache_mla_ckv, cache_mla_kpe, state_rwkv_wkv, state_rwkv_shift,
              state_ssm, state_conv, page_table, norm_mix, norm_ffn, ffn_w1, ffn_w2,
              rwkv_mu, rwkv_w_rkv, rwkv_w0, rwkv_w1, rwkv_w2, rwkv_a0, rwkv_a1, rwkv_a2,
              rwkv_v0, rwkv_v1, rwkv_v2, rwkv_g1, rwkv_g2, rwkv_k_k, rwkv_k_a, rwkv_r_k,
              rwkv_lnx_w, rwkv_lnx_b, rwkv_w_o, mla_w_in, mla_q_norm, mla_kv_norm, mla_w_uq,
              mla_w_uk, mla_w_uv, mla_qn_norm, mla_qr_norm, mla_kn_norm, mla_kr_norm, mla_w_o,
              mamba_w_in, mamba_conv_w, mamba_conv_b, mamba_dt_bias, mamba_a_log, mamba_d,
              mamba_norm, mamba_w_o):
    bp = x_prompt.shape[0]
    hp, hs = x_prompt, x_sample
    vf_p, vf_s = None, None
    ckv_p, kpe_p, ckv_s, kpe_s = [], [], [], []
    wkv_p, sh_p, wkv_s, sh_s = [], [], [], []
    ssm_p, conv_p, ssm_s, conv_s = [], [], [], []
    for i in range(DEPTH):
        kind, j = i % N_MIXERS, i // N_MIXERS
        xp = rmsnorm(hp, norm_mix[i])
        xs = rmsnorm(hs, norm_mix[i])
        if kind == 0:
            rw = (rwkv_mu[j], rwkv_w_rkv[j], rwkv_w0[j], rwkv_w1[j], rwkv_w2[j], rwkv_a0[j],
                  rwkv_a1[j], rwkv_a2[j], rwkv_g1[j], rwkv_g2[j], rwkv_k_k[j], rwkv_k_a[j],
                  rwkv_r_k[j], rwkv_lnx_w[j], rwkv_lnx_b[j], rwkv_w_o[j])
            vres = None if j == 0 else (rwkv_v0[j - 1], rwkv_v1[j - 1], rwkv_v2[j - 1])
            op, s_p, l_p, vf_p = rwkv_mix(xp, jnp.zeros((bp, D_MODEL), xp.dtype),
                                          jnp.zeros((bp, RW_HEADS, RW_HEAD, RW_HEAD), F32),
                                          vf_p, vres, *rw)
            os_, s_s, l_s, vf_s = rwkv_mix(xs, state_rwkv_shift[j], state_rwkv_wkv[j], vf_s, vres, *rw)
            wkv_p.append(s_p); sh_p.append(l_p); wkv_s.append(s_s); sh_s.append(l_s)
        elif kind == 1:
            ml = (mla_w_in[j], mla_q_norm[j], mla_kv_norm[j], mla_w_uq[j], mla_w_uk[j], mla_w_uv[j],
                  mla_qn_norm[j], mla_qr_norm[j], mla_kn_norm[j], mla_kr_norm[j], mla_w_o[j])
            op, c_p, k_p = mla_prompt(xp, *ml)
            os_, c_s, k_s = mla_sample(xs, cache_mla_ckv[j], cache_mla_kpe[j], page_table, *ml)
            ckv_p.append(c_p); kpe_p.append(k_p); ckv_s.append(c_s); kpe_s.append(k_s)
        else:
            mb = (mamba_w_in[j], mamba_conv_w[j], mamba_conv_b[j], mamba_dt_bias[j],
                  mamba_a_log[j], mamba_d[j], mamba_norm[j], mamba_w_o[j])
            op, cv_p, h_p = mamba_mix(xp, jnp.zeros((bp, MB_CONV - 1, MB_CONV_DIM), xp.dtype),
                                      jnp.zeros((bp, MB_HEADS, MB_HEAD, MB_STATE), F32), *mb)
            os_, cv_s, h_s = mamba_mix(xs, state_conv[j], state_ssm[j], *mb)
            ssm_p.append(h_p); conv_p.append(cv_p); ssm_s.append(h_s); conv_s.append(cv_s)
        hp = hp + op.astype(hp.dtype)
        hs = hs + os_.astype(hs.dtype)
        hp = hp + sqrelu_ffn(rmsnorm(hp, norm_ffn[i]), ffn_w1[i], ffn_w2[i]).astype(hp.dtype)
        hs = hs + sqrelu_ffn(rmsnorm(hs, norm_ffn[i]), ffn_w1[i], ffn_w2[i]).astype(hs.dtype)
    return (hp, hs,
            jnp.stack(ckv_p), jnp.stack(kpe_p), jnp.stack(ckv_s), jnp.stack(kpe_s),
            jnp.stack(wkv_p), jnp.stack(sh_p), jnp.stack(wkv_s), jnp.stack(sh_s),
            jnp.stack(ssm_p), jnp.stack(conv_p), jnp.stack(ssm_s), jnp.stack(conv_s))


_drawn_inputs = setup_inputs


def setup_inputs(seed=0):
    import zlib

    import numpy as np

    out = dict(_drawn_inputs(seed))
    spreads = {}
    factors = {'cache_mla_kpe': 2.849,
     'rwkv_w1': 7.512,
     'rwkv_w2': 7.446,
     'rwkv_lnx_w': 3.102,
     'rwkv_lnx_b': 5.062,
     'mla_q_norm': 8.0,
     'mla_kv_norm': 2.878,
     'mla_qn_norm': 8.0,
     'mla_qr_norm': 8.0,
     'mla_kn_norm': 8.0,
     'mla_kr_norm': 2.812,
     'mamba_conv_b': 3.499,
     'mamba_norm': 5.787}
    for name, (base, spread) in spreads.items():
        noise = np.random.default_rng([zlib.crc32(name.encode()), seed]).standard_normal(out[name].shape)
        drawn = base * np.exp(spread * noise) if base else spread * noise
        out[name] = jnp.asarray(drawn.astype(out[name].dtype))
    for name, factor in factors.items():
        out[name] = (out[name] * factor).astype(out[name].dtype)
    return out
```

```python
from contextlib import ExitStack

import numpy as np
import concourse.bass as bass
from concourse import mybir
from concourse.alu_op_type import AluOpType as ALU

F32 = mybir.dt.float32
I32 = mybir.dt.int32
ACT = mybir.ActivationFunctionType
AX = mybir.AxisListType.X

P = 128
C = 1024
KT = C // P
TP, NB, TS = 256, 8, 8
T = TP + NB * TS
DEPTH = 4
PAST, PAGE, POOL = 1024, 128, 80
NPG = PAST // PAGE
CK = 64
NCK = T // CK
HID = 4 * C
MLA_SCALE = 96.0 ** -0.5
EPS = 1e-6
DECAY = float(np.exp(-0.5))
NEG = -1.0e30
RING = 4

CONST_COLS = {}


def make_constants():
    out, col = [], 0

    def add(name, a):
        nonlocal col
        a = np.asarray(a, np.float32)
        full = np.zeros((P, a.shape[1]), np.float32)
        full[:a.shape[0]] = a
        CONST_COLS[name] = (col, a.shape[1])
        out.append(full)
        col += a.shape[1]

    p = np.arange(P)
    add("ident", np.eye(P))
    add("ones", np.ones((P, P)))
    for n in (1024, 512, 256):
        add(f"mean{n}", np.full((P, P), 1.0 / n))
    same = lambda w: (p[:, None] // w == p[None] // w).astype(np.float32)
    add("mean64", same(64) / 64)
    add("mean32", same(32) / 32)
    perm = np.zeros((P, P))
    for i in range(P):
        perm[i + 16 if i % 32 < 16 else i - 16, i] = -1.0 if i % 32 < 16 else 1.0
    add("perm", perm)
    half = 16
    inv = (np.float32(10000.0) ** (-np.arange(half, dtype=np.float32) / np.float32(half))).astype(np.float32)
    pos = np.concatenate([np.arange(TP), np.tile(PAST + np.arange(TS), NB)]).astype(np.float32)
    ang = (pos[None] * inv[p % 16][:, None]).astype(np.float32)
    add("cos", np.cos(ang.astype(np.float64)))
    add("sin", np.sin(ang.astype(np.float64)))
    s, t = p[:, None] % 64, np.arange(64)[None]
    add("att_p", np.concatenate([s < t, s <= t], 1))
    b8 = s // 8 == t // 8
    add("att_s", np.concatenate([(s < t) & b8, (s <= t) & b8], 1))
    r = s
    blk = lambda w: r // w == t // w
    add("dA_p", (t < r) & blk(16))
    add("dG_p", (r < t) & blk(16))
    add("eA", (t < r) & blk(32) & ~blk(16))
    add("eG", (r < t) & blk(32) & ~blk(16))
    add("fA", (t < r) & ~blk(32))
    add("dA_s", (t < r) & b8)
    add("dG_s", (r < t) & b8)
    add("eye64", r == t)
    add("seq", (s // 8 == np.arange(8)[None]))
    reset = np.ones(T)
    reset[0:TP:CK] = 0
    reset[TP::TS] = 0
    add("reset", np.tile(reset, (P, 1)))
    reset = np.ones(T)
    reset[0:TP:P] = 0
    reset[TP::TS] = 0
    add("reset_m", np.tile(reset, (32, 1)))
    add("causal", np.where(p[None] <= p[:, None], 0.0, NEG))
    add("tril_p", (p[:, None] <= p[None]))
    k, q = np.arange(64)[:, None], np.arange(64)[None]
    add("tril_s", (k <= q) & (k // 8 == q // 8))
    add("eps", np.tile(np.float32([EPS, 64e-5, 64 * EPS]), (P, 1)))
    add("new8", np.where(np.arange(8)[:, None] <= np.arange(8)[None], 0.0, NEG))
    return np.concatenate(out, 1)


CONSTS = make_constants()

PARAM_COLS = {}


def param_layout():
    col = 0

    def add(name, n):
        nonlocal col
        PARAM_COLS[name] = (col, n)
        col += n

    for l in range(DEPTH):
        add(f"norm_mix{l}", KT)
        add(f"norm_ffn{l}", KT)
    for j in range(2):
        add(f"mu{j}", 6 * KT)
        for n in ("w0", "a0", "v0", "k_k", "k_a", "r_k", "lnx_w", "lnx_b"):
            add(f"{n}{j}", KT)
    add("q_norm", 4)
    add("kv_norm", 2)
    add("qn", 1)
    add("kn", 1)
    add("qr", 1)
    add("kr", 1)
    add("conv_w", 4 * 24)
    add("conv_b", 24)
    add("dt_bias", 1)
    add("a_log", 1)
    add("d_skip", 16)
    add("m_norm", 16)
    return col


NPARAM = param_layout()

PANELS_FFN = 32
PANELS_RWKV = 19
PANELS_MLA = 2 + 1 + 1 + 2 + 1 + 4
PANELS_MAMBA = 8 + 12 + 1 + 8
PANELS = 4 * PANELS_FFN + 2 * PANELS_RWKV + PANELS_MLA + PANELS_MAMBA


class Tally:

    def __init__(self, sem, key, old, new):
        self.sem, self.key, self.old, self.new, self.n = sem, key, old, new, 0

    def tick(self, *name, also=None):
        self.n += 1
        self.new[(self.key, name)] = self.n
        if also is not None:
            self.new[(self.key, also)] = self.n
        return self.sem, 1

    def at(self, *name):
        if self.old is None:
            return self.sem, 1
        return self.sem, self.old[(self.key, name)]


class Kit:

    def __init__(self, nc, ctx, io, old):
        self.nc, self.ctx, self.io, self.old, self.new = nc, ctx, io, old, {}
        sb = lambda name, shape, dt=F32: ctx.enter_context(nc.sbuf_tensor(name, shape, dt))
        self.consts = sb("consts", [P, CONSTS.shape[1]])
        self.params = sb("params", [P, NPARAM])
        self.hidden = sb("residual", [P, KT, T])
        self.normed = sb("normed", [P, KT * T])
        self.v_first = sb("v_first", [P, KT, T])
        self.ring = sb("weight_ring", [P, RING, 16, P])
        self.table = sb("page_table", [1, NB * NPG], I32)
        self.arena_size = 33400
        self.arena = sb("arena", [P, self.arena_size])
        self.ps = ctx.enter_context(nc.psum_tensor("banks", [P, 8, 512], F32))
        self.loaded = [ctx.enter_context(nc.semaphore(f"panel_landed{i}")) for i in range(RING)]
        self.issued = 0
        self.panel = 0
        self.stage = 0

    def const(self, name, rows=slice(0, P)):
        c, n = CONST_COLS[name]
        return self.consts[rows, c:c + n]

    def eps(self, i, rows=slice(0, P)):
        return self.const("eps", rows)[:, i:i + 1]

    def param(self, name, i=0, n=1):
        c, _ = PARAM_COLS[name]
        return self.params[:, c + i:c + i + n]

    def tallies(self, *names):
        self.stage += 1
        return [Tally(self.ctx.enter_context(self.nc.semaphore(f"{n}{self.stage}")), (n, self.stage), self.old, self.new)
                for n in names]

    def sem(self, name):
        self.stage += 1
        return self.ctx.enter_context(self.nc.semaphore(f"{name}{self.stage}"))

    def at(self, offset, *shape, rows=P):
        n = int(np.prod(shape))
        assert offset + n <= self.arena_size, (offset, shape)
        a = self.arena[0:rows, offset:offset + n]
        if len(shape) == 2:
            a = a.rearrange("p (a b) -> p a b", a=shape[0])
        elif len(shape) == 3:
            a = a.rearrange("p (a b c) -> p a b c", a=shape[0], b=shape[1])
        return a

    def bank(self, i, n=512):
        return self.ps[:, i, 0:n]

    def load_panels(self, sp, pe_did, first, count):
        for p in range(self.issued, min(first + count + RING, PANELS)):
            if p - RING >= first:
                sp.wait_ge(*pe_did.at("panel", p - RING))
            sp.dma_start(self.ring[:, p % RING, :, :].rearrange("p a b -> p (a b)"),
                         self.io["panels"][p]).then_inc(self.loaded[p % RING], 16)
            self.issued = p + 1

    def wait_panel(self, pe, p):
        pe.wait_ge(self.loaded[p % RING], 16 * (p // RING + 1))

    def tile(self, p, i):
        return self.ring[:, p % RING, i, :]


def bc(ap, n):
    return ap.unsqueeze(2).to_broadcast([ap.shape[0], ap.shape[1], n])


def bcm(ap, n):
    return ap.unsqueeze(1).to_broadcast([ap.shape[0], n, ap.shape[1]])


def norm_act(k, act, act_did, pe_did, sq, rs):
    k.nc.scalar.activation(sq, k.hidden[:, :, :].rearrange("p a b -> p (a b)"), ACT.Square).then_inc(*act_did.tick("sq"))
    act.wait_ge(*pe_did.at("mean"))
    k.nc.scalar.activation(rs, k.bank(7, T), ACT.Sqrt, bias=k.eps(0)).then_inc(*act_did.tick("root"))


def norm_pe(k, pe, act_did, pe_did, sq):
    pe.wait_ge(*act_did.at("sq"))
    for i in range(KT):
        ins = k.nc.tensor.matmul(k.bank(7, T), k.const("mean1024"), sq[:, i * T:(i + 1) * T], start=i == 0, stop=i == KT - 1)
    ins.then_inc(*pe_did.tick("mean"))


def norm_vec(k, vec, act_did, vec_did, rs, gain):
    vec.wait_ge(*act_did.at("root"))
    k.nc.vector.reciprocal(rs, rs).then_inc(*vec_did.tick("rs"))
    vec.wait_ge(*vec_did.at("rs"))
    for i in range(KT):
        k.nc.vector.scalar_tensor_tensor(k.normed[:, i * T:(i + 1) * T], k.hidden[:, i, :], k.param(gain, i), rs,
                                         ALU.mult, ALU.mult).then_inc(*vec_did.tick("x", i))


def stage_load(k):
    nc, io = k.nc, k.io
    first_loads = k.sem("first_loads")
    with nc.Block() as block:
        @block.gpsimd
        def _(pool):
            nc.gpsimd.dma_start(k.hidden[:, :, :].rearrange("p a b -> p (a b)"), io["x"]).then_inc(first_loads, 16)
            nc.gpsimd.dma_start(k.consts[:, :], io["consts"]).then_inc(first_loads, 16)
            nc.gpsimd.dma_start(k.params[:, :], io["params"]).then_inc(first_loads, 16)
            nc.gpsimd.dma_start(k.table[:, :], io["page_table"]).then_inc(first_loads, 16)
            pool.wait_ge(first_loads, 64)

        @block.sync
        def _(sp):
            k.load_panels(sp, None, 0, 0)


def stage_ffn(k, l):
    nc = k.nc
    act_did, pe_did, vec_did = k.tallies("act", "pe", "vec")
    p0 = k.panel
    k.panel += PANELS_FFN
    hid = k.at(0, 32, T)
    sq = k.arena[:, 32 * T:40 * T]
    rs = k.arena[:, 40 * T:41 * T]
    x = k.normed

    with nc.Block() as block:
        @block.sync
        def _(sp):
            k.load_panels(sp, pe_did, p0, PANELS_FFN)

        @block.tensor
        def _(pe):
            norm_pe(k, pe, act_did, pe_did, sq)
            for m in range(32):
                if m % 2 == 0:
                    k.wait_panel(pe, p0 + m // 2)
                if m >= 4:
                    pe.wait_ge(*act_did.at("relu", m - 4))
                for i in range(KT):
                    if m == 0:
                        pe.wait_ge(*vec_did.at("x", i))
                    ins = nc.tensor.matmul(k.bank(m % 4, T), k.tile(p0 + m // 2, (m % 2) * 8 + i), x[:, i * T:(i + 1) * T],
                                           start=i == 0, stop=i == KT - 1)
                ins.then_inc(*pe_did.tick("up", m, also=("panel", p0 + m // 2)))
            for m in range(KT):
                if m == 0:
                    for j in range(28, 32):
                        pe.wait_ge(*act_did.at("relu", j))
                if m >= 4:
                    pe.wait_ge(*vec_did.at("res", m - 4))
                for q in range(4):
                    p = p0 + 16 + (m // 2) * 4 + q
                    if m % 2 == 1:
                        continue
                    k.wait_panel(pe, p)
                    for mm in (m, m + 1):
                        if mm == m + 1 and q == 0 and mm >= 4:
                            pe.wait_ge(*vec_did.at("res", mm - 4))
                        for i in range(8):
                            if m == 0 and mm == 0:
                                pe.wait_ge(*vec_did.at("hid", 8 * q + i))
                            ins = nc.tensor.matmul(k.bank(mm % 4, T), k.tile(p, (mm % 2) * 8 + i), hid[:, 8 * q + i, :],
                                                   start=q == 0 and i == 0, stop=q == 3 and i == 7)
                        if mm == m + 1:
                            ins.then_inc(*pe_did.tick("down", mm, q, also=("panel", p)))
                        elif q == 3:
                            ins.then_inc(*pe_did.tick("down", mm, q))

        @block.scalar
        def _(act):
            norm_act(k, act, act_did, pe_did, sq, rs)
            for m in range(32):
                act.wait_ge(*pe_did.at("up", m))
                nc.scalar.activation(hid[:, m, :], k.bank(m % 4, T), ACT.Relu).then_inc(*act_did.tick("relu", m))

        @block.vector
        def _(vec):
            norm_vec(k, vec, act_did, vec_did, rs, f"norm_ffn{l}")
            for m in range(32):
                vec.wait_ge(*act_did.at("relu", m))
                nc.vector.tensor_tensor(hid[:, m, :], hid[:, m, :], hid[:, m, :], ALU.mult).then_inc(*vec_did.tick("hid", m))
            for m in range(KT):
                vec.wait_ge(*pe_did.at("down", m, 3))
                nc.vector.tensor_tensor(k.hidden[:, m, :], k.hidden[:, m, :], k.bank(m % 4, T), ALU.add)\
                    .then_inc(*vec_did.tick("res", m))


def out_project_pe(k, pe, pe_did, vec_did, p0, src, nk, ready):
    per = 16 // nk
    for m in range(KT):
        p = p0 + m // per
        if m % per == 0:
            k.wait_panel(pe, p)
        if m >= 4:
            pe.wait_ge(*vec_did.at("res", m - 4))
        for i in range(nk):
            if m == 0:
                ready(pe, i)
            ins = k.nc.tensor.matmul(k.bank(m % 4, T), k.tile(p, (m % per) * nk + i), src(i), start=i == 0, stop=i == nk - 1)
        ins.then_inc(*pe_did.tick("out", m, also=("panel", p)))


def out_project_vec(k, vec, pe_did, vec_did):
    for m in range(KT):
        vec.wait_ge(*pe_did.at("out", m))
        k.nc.vector.tensor_tensor(k.hidden[:, m, :], k.hidden[:, m, :], k.bank(m % 4, T), ALU.add)\
            .then_inc(*vec_did.tick("res", m))


W = KT * T
RW = dict(R=0, K=W, V=2 * W, LW=3 * W, A=4 * W, G=5 * W, DX=6 * W, XM=7 * W, SG=9 * W, LH=10 * W,
          AR=6 * W, BK=8 * W, TMP=10 * W)


def stage_rwkv_project(k, l, j):
    nc, io = k.nc, k.io
    act_did, pe_did, vec_did = k.tallies("act", "pe", "vec")
    moved = k.sem("shift_moved")
    stored = k.sem("shift_stored")
    p0 = k.panel
    used = PANELS_RWKV - 4
    k.panel += used
    res = j > 0
    arr = {n: k.at(RW[n], KT, T) for n in ("R", "K", "V", "LW", "A", "G", "DX", "SG")}
    arr["XM"] = k.at(RW["XM"], 2 * KT, T)
    hw, hg, hb = (k.arena[:, RW["LH"] + i * T:RW["LH"] + (i + 1) * T] for i in range(3))
    rs = k.arena[:, RW["LH"] + 3 * T:RW["LH"] + 4 * T]
    small = RW["LH"] + 4 * T
    shift_in = k.at(small, KT, NB)
    last = k.at(small + 64, KT, 9)
    sq = k.arena[:, RW["G"]:RW["G"] + W]
    x = k.normed[:, :].rearrange("p (a b) -> p a b", a=KT)
    dx, xm = arr["DX"], arr["XM"]
    la, lb, lc = p0 + 12, p0 + 13, p0 + 14

    plan = [("R", m) for m in range(KT)] + [("K", m) for m in range(KT)] + [("V", m) for m in range(KT)]
    if res:
        plan += [("hv", 0)] + [("SG", m) for m in range(KT)]
    plan += [("hw", 0)] + [("LW", m) for m in range(KT)]
    plan += [("ha", 0)] + [("A", m) for m in range(KT)]
    plan += [("hg", 0), ("hb", 0)] + [("G", m) for m in range(KT)]
    mix_of = {"R": 0, "K": 1, "V": 2, "hv": 2, "hw": 3, "ha": 4, "hg": 5, "hb": 5}
    last_of_mix = {mix_of[what]: n for n, (what, _) in enumerate(plan) if what in mix_of}

    with nc.Block() as block:
        @block.sync
        def _(sp):
            sp.dma_start(shift_in.rearrange("p a b -> p (a b)"), io["shift"][j]).then_inc(moved, 16)
            k.load_panels(sp, pe_did, p0, used)

        @block.gpsimd
        def _(pool):
            pool.wait_ge(*vec_did.at("last"))
            nc.gpsimd.dma_start(io["shift_out"][j], last.rearrange("p a b -> p (a b)")).then_inc(stored, 16)
            pool.wait_ge(stored, 16)

        @block.vector
        def _(vec):
            norm_vec(k, vec, act_did, vec_did, rs, f"norm_mix{l}")
            vec.wait_ge(*vec_did.at("x", KT - 1))
            nc.vector.tensor_copy(last[:, :, 0:1], x[:, :, TP - 1:TP])
            nc.vector.tensor_copy(last[:, :, 1:9], x[:, :, TP + TS - 1::TS]).then_inc(*vec_did.tick("last"))
            nc.vector.tensor_tensor(dx[:, :, 1:TP], x[:, :, 0:TP - 1], x[:, :, 1:TP], ALU.subtract)
            nc.vector.tensor_scalar(dx[:, :, 0:1], x[:, :, 0:1], -1.0, None, ALU.mult)
            nc.vector.tensor_tensor(dx[:, :, TP + 1:T], x[:, :, TP:T - 1], x[:, :, TP + 1:T], ALU.subtract)\
                .then_inc(*vec_did.tick("dx0"))
            vec.wait_ge(moved, 16)
            vec.wait_ge(*vec_did.at("dx0"))
            nc.vector.tensor_tensor(dx[:, :, TP::TS], shift_in, x[:, :, TP::TS], ALU.subtract).then_inc(*vec_did.tick("dx"))
            vec.wait_ge(*vec_did.at("dx"))
            for p in range(6):
                if p >= 2:
                    vec.wait_ge(*pe_did.at("tile", last_of_mix[p - 2]))
                for i in range(KT):
                    nc.vector.scalar_tensor_tensor(xm[:, (p % 2) * KT + i, :], dx[:, i, :], k.param(f"mu{j}", p * KT + i),
                                                   x[:, i, :], ALU.mult, ALU.add).then_inc(*vec_did.tick("mix", p, i))
            if res:
                vec.wait_ge(*act_did.at("tile", plan.index(("SG", KT - 1))))
                vec.wait_ge(*vec_did.at("mix", 5, KT - 1))
                nc.vector.tensor_tensor(dx, k.v_first[:, :, :], arr["V"], ALU.subtract).then_inc(*vec_did.tick("vd"))
                vec.wait_ge(*vec_did.at("vd"))
                nc.vector.tensor_tensor(dx, dx, arr["SG"], ALU.mult).then_inc(*vec_did.tick("vg"))
                vec.wait_ge(*vec_did.at("vg"))
                nc.vector.tensor_tensor(arr["V"], arr["V"], dx, ALU.add).then_inc(*vec_did.tick("v"))
            else:
                vec.wait_ge(*act_did.at("tile", plan.index(("V", KT - 1))))
                nc.vector.tensor_copy(k.v_first[:, :, :], arr["V"]).then_inc(*vec_did.tick("v"))

        @block.tensor
        def _(pe):
            norm_pe(k, pe, act_did, pe_did, sq)
            for n, (what, m) in enumerate(plan):
                if n >= 4:
                    pe.wait_ge(*act_did.at("tile", n - 4))
                out = k.bank(n % 4, T)
                if what in mix_of:
                    rhs = lambda i, b=(mix_of[what] % 2) * KT: xm[:, b + i, :]
                    for i in range(KT):
                        pe.wait_ge(*vec_did.at("mix", mix_of[what], i))
                        if what in "RKV":
                            p = p0 + 4 * "RKV".index(what) + m // 2
                            if i == 0 and m % 2 == 0:
                                k.wait_panel(pe, p)
                            o, lhs = out, k.tile(p, (m % 2) * 8 + i)
                        elif what == "hv":
                            if i == 0:
                                k.wait_panel(pe, lb)
                            o, lhs = out[32:64, :], k.tile(lb, i)[:, 32:64]
                        elif what == "hw":
                            if i == 0:
                                k.wait_panel(pe, la)
                            o, lhs = out[0:64, :], k.tile(la, i)[:, 0:64]
                        elif what == "ha":
                            o, lhs = out[64:128, :], k.tile(la, i)[:, 64:128]
                        elif what == "hg":
                            o, lhs = out, k.tile(la, 8 + i)
                        else:
                            o, lhs = out[0:32, :], k.tile(lb, i)[:, 0:32]
                        ins = nc.tensor.matmul(o, lhs, rhs(i), start=i == 0, stop=i == KT - 1)
                    also = ("panel", p0 + 4 * "RKV".index(what) + m // 2) if what in "RKV" else None
                    ins.then_inc(*pe_did.tick("tile", n, also=also))
                    continue
                pe.wait_ge(*act_did.at("tile", plan.index(({"SG": "hv", "LW": "hw", "A": "ha", "G": "hb"}[what], 0))))
                k.wait_panel(pe, lb)
                k.wait_panel(pe, lc)
                if what == "SG":
                    ins = nc.tensor.matmul(out, k.tile(lc, 8 + m)[32:64, :], hb[32:64, :], start=True, stop=True)
                elif what == "LW":
                    ins = nc.tensor.matmul(out, k.tile(lb, 8 + m)[0:64, :], hw[0:64, :], start=True, stop=True)
                elif what == "A":
                    ins = nc.tensor.matmul(out, k.tile(lb, 8 + m)[64:128, :], hw[64:128, :], start=True, stop=True)
                else:
                    nc.tensor.matmul(out, k.tile(lc, m), hg, start=True, stop=False)
                    ins = nc.tensor.matmul(out, k.tile(lc, 8 + m)[0:32, :], hb[0:32, :], start=False, stop=True)
                ins.then_inc(*pe_did.tick("tile", n))
            for p in (la, lb, lc):
                k.new[(pe_did.key, ("panel", p))] = pe_did.n

        @block.scalar
        def _(act):
            norm_act(k, act, act_did, pe_did, sq, rs)
            for n, (what, m) in enumerate(plan):
                act.wait_ge(*pe_did.at("tile", n))
                b = k.bank(n % 4, T)
                if what in ("R", "K", "V", "G"):
                    ins = nc.scalar.activation(arr[what][:, m, :], b, ACT.Copy)
                elif what == "hv":
                    ins = nc.scalar.activation(hb[32:64, :], b[32:64, :], ACT.Copy)
                elif what == "hw":
                    ins = nc.scalar.activation(hw[0:64, :], b[0:64, :], ACT.Tanh)
                elif what == "ha":
                    ins = nc.scalar.activation(hw[64:128, :], b[64:128, :], ACT.Copy)
                elif what == "hg":
                    ins = nc.scalar.activation(hg, b, ACT.Sigmoid)
                elif what == "hb":
                    ins = nc.scalar.activation(hb[0:32, :], b[0:32, :], ACT.Sigmoid)
                else:
                    bias = {"SG": "v0", "LW": "w0", "A": "a0"}[what]
                    ins = nc.scalar.activation(arr[what][:, m, :], b, ACT.Sigmoid, bias=k.param(f"{bias}{j}", m))
                ins.then_inc(*act_did.tick("tile", n))


def stage_rwkv_prepare(k, j):
    nc = k.nc
    act_did, pe_did, vec_did, pool_did = k.tallies("act", "pe", "vec", "pool")
    R, K, V, LW, A = (k.arena[:, RW[n]:RW[n] + W] for n in ("R", "K", "V", "LW", "A"))
    T1, T2, T3 = (k.arena[:, RW["TMP"] + i * W:RW["TMP"] + (i + 1) * W] for i in range(3))
    T4 = k.normed[:, :]
    AR = k.at(RW["AR"], KT * NCK, P)
    BK = k.at(RW["BK"], KT * NCK, P)
    g3 = lambda a: a.rearrange("p (a b) -> p a b", a=KT)
    c3 = lambda a: a.rearrange("p (a b) -> p a b", b=CK)
    par = lambda n: bc(k.param(f"{n}{j}", 0, KT), T)
    pc = k.at(k.arena_size - 96, KT, 12)
    allbanks = k.ps[:, :, 0:T]

    with nc.Block() as block:
        @block.vector
        def _(vec):
            v = nc.vector
            v.tensor_tensor(g3(T1), g3(K), par("k_k"), ALU.mult).then_inc(*vec_did.tick("kk0"))
            for i in range(KT):
                ins = v.tensor_tensor_scan(T3[:, i * T:(i + 1) * T], k.const("reset"), LW[:, i * T:(i + 1) * T], 0.0,
                                           ALU.mult, ALU.add)
            ins.then_inc(*vec_did.tick("cum"))
            vec.wait_ge(*pe_did.at("norm", KT - 1))
            v.tensor_scalar(g3(T2), allbanks, 1e-24 / 64, None, ALU.max).then_inc(*vec_did.tick("clamp"))
            vec.wait_ge(*act_did.at("root"))
            v.reciprocal(T2, T2).then_inc(*vec_did.tick("inv"))
            vec.wait_ge(*vec_did.at("inv"))
            v.scalar_tensor_tensor(T1, T1, 0.125, T2, ALU.mult, ALU.mult).then_inc(*vec_did.tick("kk"))
            vec.wait_ge(*vec_did.at("kk"))
            v.scalar_tensor_tensor(g3(T2), g3(A), -1.0, par("k_a"), ALU.add, ALU.mult).then_inc(*vec_did.tick("ka"))
            vec.wait_ge(*act_did.at("px"))
            v.scalar_tensor_tensor(AR[:, :, 0:CK], c3(T1), -1.0, c3(LW), ALU.mult, ALU.mult).then_inc(*vec_did.tick("a_hat"))
            vec.wait_ge(*vec_did.at("ka"))
            v.scalar_tensor_tensor(K, T2, 1.0, K, ALU.add, ALU.mult).then_inc(*vec_did.tick("k"))
            vec.wait_ge(*vec_did.at("a_hat"))
            v.tensor_tensor(T1, T1, A, ALU.mult).then_inc(*vec_did.tick("b"))
            vec.wait_ge(*act_did.at("p"))
            v.tensor_tensor(AR[:, :, CK:P], c3(R), c3(T4), ALU.mult).then_inc(*vec_did.tick("r_hat"))
            p3 = g3(T4)
            v.tensor_copy(pc[:, :, 0:4], p3[:, :, CK - 1:TP:CK])
            v.tensor_copy(pc[:, :, 4:12], p3[:, :, TP + TS - 1::TS]).then_inc(*vec_did.tick("pc"))
            vec.wait_ge(*act_did.at("pi"))
            vec.wait_ge(*vec_did.at("b"))
            v.tensor_tensor(BK[64:128, :, 0:CK], c3(T1)[64:128], c3(T3)[64:128], ALU.mult)
            v.tensor_tensor(BK[0:64, :, CK:P], c3(T1)[0:64], c3(T3)[0:64], ALU.mult)
            v.tensor_tensor(BK[0:64, :, 0:CK], c3(K)[0:64], c3(T3)[0:64], ALU.mult)
            v.tensor_tensor(BK[64:128, :, CK:P], c3(K)[64:128], c3(T3)[64:128], ALU.mult).then_inc(*vec_did.tick("k_hat"))
            vec.wait_ge(*pool_did.at("rr"))
            vec.wait_ge(*vec_did.at("k"))
            v.tensor_tensor(T2, LW, K, ALU.mult).then_inc(*vec_did.tick("rk"))
            vec.wait_ge(*pe_did.at("bonus", KT - 1))
            v.scalar_tensor_tensor(g3(R), g3(V), 64.0, allbanks, ALU.mult, ALU.mult).then_inc(*vec_did.tick("bon"))

        @block.gpsimd
        def _(pool):
            pool.wait_ge(*vec_did.at("cum"))
            nc.gpsimd.tensor_tensor(T4, T3, LW, ALU.subtract).then_inc(*pool_did.tick("before"))
            pool.wait_ge(*vec_did.at("a_hat"))
            nc.gpsimd.tensor_tensor(g3(LW), g3(R), par("r_k"), ALU.mult).then_inc(*pool_did.tick("rr"))

        @block.scalar
        def _(act):
            s = nc.scalar
            act.wait_ge(*vec_did.at("kk0"))
            s.activation(T2, T1, ACT.Square).then_inc(*act_did.tick("sq"))
            act.wait_ge(*vec_did.at("clamp"))
            s.activation(T2, T2, ACT.Sqrt).then_inc(*act_did.tick("root"))
            act.wait_ge(*pool_did.at("before"))
            s.activation(LW, T4, ACT.Exp, scale=-DECAY).then_inc(*act_did.tick("px"))
            act.wait_ge(*act_did.at("px"))
            s.activation(T4, T3, ACT.Exp, scale=-DECAY).then_inc(*act_did.tick("p"))
            act.wait_ge(*act_did.at("p"))
            s.activation(T3, T3, ACT.Exp, scale=DECAY).then_inc(*act_did.tick("pi"))

        @block.tensor
        def _(pe):
            pe.wait_ge(*act_did.at("sq"))
            for i in range(KT):
                nc.tensor.matmul(k.bank(i, T), k.const("mean64"), T2[:, i * T:(i + 1) * T], start=True, stop=True)\
                    .then_inc(*pe_did.tick("norm", i))
            pe.wait_ge(*vec_did.at("rk"))
            for i in range(KT):
                nc.tensor.matmul(k.bank(i, T), k.const("mean64"), T2[:, i * T:(i + 1) * T], start=True, stop=True)\
                    .then_inc(*pe_did.tick("bonus", i))


def stage_rwkv_scan(k, j):
    nc, io = k.nc, k.io
    act_did, pe_did, vec_did, pool_did = k.tallies("act", "pe", "vec", "pool")
    state_in = k.sem("state_in")
    stored = k.sem("state_stored")
    V = k.at(RW["V"], KT, T)
    AR = k.at(RW["AR"], KT * NCK, P)
    BK = k.at(RW["BK"], KT * NCK, P)
    Y = k.at(RW["K"], KT, T)
    SS = k.at(RW["LW"], KT * NB, CK)
    bktok = k.at(RW["LW"] + KT * NB * CK, KT, P)
    o = RW["TMP"]
    att = k.at(o, 16, P)
    o += 16 * P
    par = []
    for _ in range(9):
        par.append(k.at(o, KT, CK))
        o += KT * CK
    D, Gm, T_, TT, D1, G1, E_, Et, F_ = par
    assert o <= k.arena_size - 96, o
    z = k.normed[:, 0:1024].rearrange("p (a b) -> p a b", a=16)
    x0, S, Y1 = (k.normed[:, 1024 + 512 * i:1536 + 512 * i].rearrange("p (a b) -> p a b", a=KT) for i in range(3))
    Y2 = D1
    pc = k.at(k.arena_size - 96, KT, 12)
    b3 = lambda i: k.ps[:, i, :].rearrange("p (a b) -> p a b", a=KT)
    bcols = [slice(CK, P), slice(0, CK)]
    half = [slice(0, 64), slice(64, 128)]
    heads = [(2 * f + h, f, slice(64 * h, 64 * h + 64)) for f in range(KT) for h in range(2)]
    zmask = [G1, Et]

    with nc.Block() as block:
        @block.sync
        def _(sp):
            sp.dma_start(SS.rearrange("p a b -> p (a b)"), io["wkv"][j]).then_inc(state_in, 16)
            sp.wait_ge(*vec_did.at("S", 3))
            sp.dma_start(io["wkv_prompt"][j], S.rearrange("p a b -> p (a b)")).then_inc(stored, 16)
            sp.wait_ge(*vec_did.at("SS", KT - 1))
            sp.dma_start(io["wkv_sample"][j], SS.rearrange("p a b -> p (a b)")).then_inc(stored, 16)
            sp.wait_ge(stored, 32)

        @block.tensor
        def _(pe):
            mm = nc.tensor.matmul
            for c in range(NCK):
                smp = c == NCK - 1
                if c:
                    pe.wait_ge(*act_did.at("y", c - 1))
                    pe.wait_ge(*vec_did.at("S", c - 1))
                for f in range(KT):
                    ins = nc.tensor.transpose(k.ps[:, f // 4, (f % 4) * P:(f % 4 + 1) * P], BK[:, f * NCK + c, :], k.const("ident"))
                ins.then_inc(*pe_did.tick("bkt", c))
                for h, f, r in heads:
                    ins = mm(b3(2)[r, f, :], V[r, f, c * CK:(c + 1) * CK], k.const("eye64")[r, :], start=True, stop=True)
                ins.then_inc(*pe_did.tick("vt", c))
                for h, f, r in heads:
                    ins = mm(k.ps[:, 4 + 2 * (h % 2) + f // 4, (f % 4) * P:(f % 4 + 1) * P], BK[r, f * NCK + c, :], AR[r, f * NCK + c, :],
                             start=True, stop=True)
                ins.then_inc(*pe_did.tick("att", c))
                pe.wait_ge(*act_did.at("bkt", c))
                for h, f, r in heads:
                    mm(b3(0)[r, f, :], AR[r, f * NCK + c, 0:CK], BK[r, f * NCK + c, bcols[h % 2]], start=True, stop=True)
                for h, f, r in heads:
                    ins = mm(b3(1)[r, f, :], BK[r, f * NCK + c, bcols[h % 2]], AR[r, f * NCK + c, 0:CK], start=True, stop=True)
                ins.then_inc(*pe_did.tick("A", c))
                levels = 2 if smp else 3
                pe.wait_ge(*act_did.at("vt", c))
                for lev in range(levels):
                    Dp, Gp = (D, Gm) if lev % 2 == 0 else (D1, G1)
                    Dn, Gn = (D1, G1) if lev % 2 == 0 else (D, Gm)
                    if lev == 0:
                        pe.wait_ge(*vec_did.at("TT0", c))
                    for h, f, r in heads:
                        mm(b3(2)[r, f, :], Gp[r, f, :], Dp[r, f, :], start=True, stop=True)
                    for h, f, r in heads:
                        ins = mm(b3(3)[r, f, :], Dp[r, f, :], Gp[r, f, :], start=True, stop=True)
                    ins.then_inc(*pe_did.tick("sq", c, lev))
                    pe.wait_ge(*vec_did.at("D", c, lev))
                    pe.wait_ge(*act_did.at("G", c, lev))
                    if lev:
                        pe.wait_ge(*vec_did.at("T", c, lev - 1))
                    for h, f, r in heads:
                        mm(b3(4)[r, f, :], Gn[r, f, :], T_[r, f, :], start=True, stop=True)
                    for h, f, r in heads:
                        ins = mm(b3(5)[r, f, :], Dn[r, f, :], TT[r, f, :], start=True, stop=True)
                    ins.then_inc(*pe_did.tick("T", c, lev))
                pe.wait_ge(*vec_did.at("T", c, levels - 1))
                if not smp:
                    for h, f, r in heads:
                        mm(b3(6)[r, f, :], Et[r, f, :], T_[r, f, :], start=True, stop=True)
                    for h, f, r in heads:
                        ins = mm(b3(7)[r, f, :], E_[r, f, :], TT[r, f, :], start=True, stop=True)
                    ins.then_inc(*pe_did.tick("m1", c))
                    pe.wait_ge(*vec_did.at("Y1", c))
                    pe.wait_ge(*act_did.at("Y2", c))
                    for h, f, r in heads:
                        mm(b3(4)[r, f, :], TT[r, f, :], Y1[r, f, :], start=True, stop=True)
                    for h, f, r in heads:
                        ins = mm(b3(5)[r, f, :], T_[r, f, :], Y2[r, f, :], start=True, stop=True)
                    ins.then_inc(*pe_did.tick("m2", c))
                    pe.wait_ge(*vec_did.at("T32", c))
                    for h, f, r in heads:
                        ins = mm(b3(6)[r, f, :], F_[r, f, :], TT[r, f, :], start=True, stop=True)
                    ins.then_inc(*pe_did.tick("m3", c))
                    pe.wait_ge(*act_did.at("Y3", c))
                    for h, f, r in heads:
                        ins = mm(b3(4)[r, f, :], T_[r, f, :], Y1[r, f, :], start=True, stop=True)
                    ins.then_inc(*pe_did.tick("m4", c))
                    pe.wait_ge(*vec_did.at("T64", c))
                else:
                    pe.wait_ge(state_in, 16)
                    for h, f, r in heads:
                        for b in range(NB):
                            ins = mm(b3(6)[r, f, TS * b:TS * b + TS], SS[r, f * NB + b, :], AR[r, f * NCK + c, TS * b:TS * b + TS],
                                     start=True, stop=True)
                    ins.then_inc(*pe_did.tick("xs", c))
                    pe.wait_ge(*act_did.at("xs", c))
                for h, f, r in heads:
                    if smp:
                        mm(b3(5)[r, f, :], E_[r, f, :], k.const("eye64")[r, :], start=True, stop=False)
                    elif c:
                        mm(b3(5)[r, f, :], AR[r, f * NCK + c, 0:CK], S[r, f, :], start=True, stop=False)
                    ins = mm(b3(5)[r, f, :], att[r, h, 0:CK], z[r, h, :], start=c == 0, stop=True)
                ins.then_inc(*pe_did.tick("x0", c))
                pe.wait_ge(*act_did.at("x0", c))
                for h, f, r in heads:
                    ins = mm(b3(6)[half[1 - h % 2], f, :], TT[r, f, :], x0[r, f, :], start=True, stop=True)
                ins.then_inc(*pe_did.tick("u", c))
                pe.wait_ge(*vec_did.at("u", c))
                if not smp:
                    for h, f, r in heads:
                        ins = mm(b3(5)[r, f, :], bktok[:, f, r], z[:, h, :], start=True, stop=True)
                    ins.then_inc(*pe_did.tick("ds", c))
                for h, f, r in heads:
                    ins = mm(b3(4)[r, f, :], z[:, h, :], att[:, h, CK:P], start=True, stop=c == 0 or smp)
                    if smp:
                        for b in range(NB):
                            ins = mm(b3(4)[r, f, TS * b:TS * b + TS], SS[r, f * NB + b, :],
                                     AR[r, f * NCK + c, CK + TS * b:CK + TS * b + TS], start=False, stop=True,
                                     skip_group_check=True)
                    elif c:
                        ins = mm(b3(4)[r, f, :], S[r, f, :], AR[r, f * NCK + c, CK:P], start=False, stop=True)
                ins.then_inc(*pe_did.tick("y", c))
            for h, f, r in heads:
                pe.wait_ge(*(pool_did if h % 2 else vec_did).at("zm", h))
                if h % 2 == 0 and f >= 2:
                    pe.wait_ge(*vec_did.at("SS", f - 2))
                mm(k.ps[r, 2 + f % 2, :], bktok[:, f, r], zmask[h % 2].rearrange("p a b -> p (a b)"), start=True, stop=True)\
                    .then_inc(*pe_did.tick("dss", h))

        @block.scalar
        def _(act):
            s = nc.scalar
            for c in range(NCK):
                smp = c == NCK - 1
                act.wait_ge(*pe_did.at("bkt", c))
                s.activation(bktok.rearrange("p a b -> p (a b)"), k.ps[:, 0:2, :].rearrange("p a b -> p (a b)"), ACT.Copy)\
                    .then_inc(*act_did.tick("bkt", c))
                act.wait_ge(*pe_did.at("vt", c))
                s.activation(z[half[0], 0::2, :], b3(2)[half[0]], ACT.Copy)
                s.activation(z[half[1], 1::2, :], b3(2)[half[1]], ACT.Copy).then_inc(*act_did.tick("vt", c))
                levels = 2 if smp else 3
                for lev in range(levels):
                    act.wait_ge(*pe_did.at("sq", c, lev))
                    s.activation(G1 if lev % 2 == 0 else Gm, b3(3), ACT.Copy).then_inc(*act_did.tick("G", c, lev))
                if not smp:
                    act.wait_ge(*pe_did.at("m1", c))
                    s.activation(Y2, b3(7), ACT.Copy).then_inc(*act_did.tick("Y2", c))
                    act.wait_ge(*pe_did.at("m3", c))
                    s.activation(Y1, b3(6), ACT.Copy).then_inc(*act_did.tick("Y3", c))
                else:
                    act.wait_ge(*pe_did.at("xs", c))
                    s.activation(E_, b3(6), ACT.Copy).then_inc(*act_did.tick("xs", c))
                act.wait_ge(*pe_did.at("x0", c))
                s.activation(x0, b3(5), ACT.Copy).then_inc(*act_did.tick("x0", c))
                act.wait_ge(*pe_did.at("y", c))
                s.activation(Y[:, :, c * CK:(c + 1) * CK], b3(4), ACT.Copy).then_inc(*act_did.tick("y", c))

        @block.vector
        def _(vec):
            v = nc.vector
            m8 = lambda name: bcm(k.const(name), KT)
            for c in range(NCK):
                smp = c == NCK - 1
                sfx = "s" if smp else "p"
                vec.wait_ge(*pe_did.at("att", c))
                for q in range(4):
                    h0 = q // 2 + 8 * (q % 2)
                    v.tensor_tensor(att[:, h0:h0 + 7:2, :], k.ps[:, 4 + q, :].rearrange("p (a b) -> p a b", a=4),
                                    bcm(k.const(f"att_{sfx}"), 4), ALU.mult).then_inc(*vec_did.tick("att", c, q))
                vec.wait_ge(*pe_did.at("A", c))
                v.tensor_tensor(D, b3(0), m8(f"dA_{sfx}"), ALU.mult).then_inc(*vec_did.tick("D0", c))
                v.tensor_tensor(Gm, b3(1), m8(f"dG_{sfx}"), ALU.mult).then_inc(*vec_did.tick("G0", c))
                if not smp:
                    v.tensor_tensor(E_, b3(0), m8("eA"), ALU.mult)
                    v.tensor_tensor(Et, b3(1), m8("eG"), ALU.mult)
                    v.tensor_tensor(F_, b3(0), m8("fA"), ALU.mult)
                vec.wait_ge(*vec_did.at("G0", c))
                v.tensor_tensor(T_, D, m8("eye64"), ALU.add)
                v.tensor_tensor(TT, Gm, m8("eye64"), ALU.add).then_inc(*vec_did.tick("TT0", c))
                for lev in range(2 if smp else 3):
                    vec.wait_ge(*pe_did.at("sq", c, lev))
                    v.tensor_copy(D1 if lev % 2 == 0 else D, b3(2)).then_inc(*vec_did.tick("D", c, lev))
                    vec.wait_ge(*pe_did.at("T", c, lev))
                    v.tensor_tensor(T_, T_, b3(4), ALU.add)
                    v.tensor_tensor(TT, TT, b3(5), ALU.add).then_inc(*vec_did.tick("T", c, lev))
                if not smp:
                    vec.wait_ge(*pe_did.at("m1", c))
                    v.tensor_copy(Y1, b3(6)).then_inc(*vec_did.tick("Y1", c))
                    vec.wait_ge(*pe_did.at("m2", c))
                    v.tensor_tensor(T_, T_, b3(4), ALU.add)
                    v.tensor_tensor(TT, TT, b3(5), ALU.add).then_inc(*vec_did.tick("T32", c))
                    vec.wait_ge(*vec_did.at("T32", c))
                    vec.wait_ge(*pe_did.at("m4", c))
                    v.tensor_tensor(TT, TT, b3(4), ALU.add).then_inc(*vec_did.tick("T64", c))
                vec.wait_ge(*pe_did.at("u", c))
                v.tensor_copy(z[half[1], 0::2, :], b3(6)[half[1]])
                v.tensor_copy(z[half[0], 1::2, :], b3(6)[half[0]]).then_inc(*vec_did.tick("u", c))
                if not smp:
                    vec.wait_ge(*pe_did.at("y", c))
                    if c:
                        v.tensor_tensor(S, S, b3(5), ALU.add).then_inc(*vec_did.tick("S0", c))
                        vec.wait_ge(*vec_did.at("S0", c))
                        v.tensor_tensor(S, S, bc(pc[:, :, c], CK), ALU.mult).then_inc(*vec_did.tick("S", c))
                    else:
                        v.tensor_tensor(S, b3(5), bc(pc[:, :, c], CK), ALU.mult).then_inc(*vec_did.tick("S", c))
            vec.wait_ge(*vec_did.at("u", NCK - 1))
            vec.wait_ge(*pe_did.at("y", NCK - 1))
            for f in range(KT):
                if f:
                    vec.wait_ge(*pe_did.at("dss", 2 * f - 2))
                v.tensor_tensor(zmask[0], bcm(z[:, 2 * f, :], NB), bc(k.const("seq"), CK), ALU.mult).then_inc(*vec_did.tick("zm", 2 * f))
                vec.wait_ge(*pe_did.at("dss", 2 * f + 1))
                sf = SS[:, f * NB:(f + 1) * NB, :]
                v.tensor_tensor(sf, sf, k.ps[:, 2 + f % 2, :].rearrange("p (a b) -> p a b", a=NB), ALU.add)\
                    .then_inc(*vec_did.tick("SS0", f))
                vec.wait_ge(*vec_did.at("SS0", f))
                v.tensor_tensor(sf, sf, bc(pc[:, f, 4:12], CK), ALU.mult).then_inc(*vec_did.tick("SS", f))

        @block.gpsimd
        def _(pool):
            pool.wait_ge(*vec_did.at("u", NCK - 1))
            pool.wait_ge(*pe_did.at("y", NCK - 1))
            for f in range(KT):
                if f:
                    pool.wait_ge(*pe_did.at("dss", 2 * f - 1))
                nc.gpsimd.tensor_tensor(zmask[1], bcm(z[:, 2 * f + 1, :], NB), bc(k.const("seq"), CK), ALU.mult)\
                    .then_inc(*pool_did.tick("zm", 2 * f + 1))


def stage_rwkv_output(k, j):
    nc = k.nc
    act_did, pe_did, vec_did, pool_did = k.tallies("act", "pe", "vec", "pool")
    p0 = k.panel
    k.panel += 4
    Y, BON, G = (k.at(RW[n], KT, T) for n in ("K", "R", "G"))
    flat = lambda a: a.rearrange("p a b -> p (a b)")
    SQ, RS = k.at(RW["AR"], KT, T), k.at(RW["BK"], KT, T)
    par = lambda n: bc(k.param(f"{n}{j}", 0, KT), T)
    allbanks = k.ps[:, :, 0:T]
    with nc.Block() as block:
        @block.sync
        def _(sp):
            k.load_panels(sp, pe_did, p0, 4)

        @block.tensor
        def _(pe):
            for i in range(KT):
                ins = nc.tensor.matmul(k.bank(i, T), k.const("mean64"), Y[:, i, :], start=True, stop=True)
            ins.then_inc(*pe_did.tick("mean"))
            pe.wait_ge(*act_did.at("sq"))
            for i in range(KT):
                ins = nc.tensor.matmul(k.bank(i, T), k.const("mean64"), SQ[:, i, :], start=True, stop=True)
            ins.then_inc(*pe_did.tick("var"))
            pe.wait_ge(*act_did.at("root"))
            out_project_pe(k, pe, pe_did, vec_did, p0, lambda i: Y[:, i, :], KT, lambda e, i: e.wait_ge(*vec_did.at("gated", i)))

        @block.scalar
        def _(act):
            act.wait_ge(*vec_did.at("centred"))
            nc.scalar.activation(flat(SQ), flat(Y), ACT.Square).then_inc(*act_did.tick("sq"))
            act.wait_ge(*pe_did.at("var"))
            nc.scalar.activation(RS, allbanks, ACT.Sqrt, bias=k.eps(1)).then_inc(*act_did.tick("root"))

        @block.vector
        def _(vec):
            v = nc.vector
            vec.wait_ge(*pe_did.at("mean"))
            v.tensor_tensor(Y, Y, allbanks, ALU.subtract).then_inc(*vec_did.tick("centred"))
            vec.wait_ge(*act_did.at("root"))
            v.reciprocal(RS, RS).then_inc(*vec_did.tick("rs"))
            vec.wait_ge(*vec_did.at("rs"))
            v.tensor_tensor(Y, Y, RS, ALU.mult).then_inc(*vec_did.tick("n"))
            vec.wait_ge(*vec_did.at("n"))
            for i in range(KT):
                v.tensor_scalar(Y[:, i, :], Y[:, i, :], k.param(f"lnx_w{j}", i), k.param(f"lnx_b{j}", i), ALU.mult, ALU.add)\
                    .then_inc(*vec_did.tick("w", i))
            for i in range(KT):
                vec.wait_ge(*vec_did.at("w", i))
                v.tensor_tensor(Y[:, i, :], Y[:, i, :], BON[:, i, :], ALU.add).then_inc(*vec_did.tick("b", i))
            for i in range(KT):
                vec.wait_ge(*vec_did.at("b", i))
                v.tensor_tensor(Y[:, i, :], Y[:, i, :], G[:, i, :], ALU.mult).then_inc(*vec_did.tick("gated", i))
            out_project_vec(k, vec, pe_did, vec_did)


HEADS = 16
ML, _o = {}, 0
for _n, _s in (("WUK", 2048), ("WUKT", 2048), ("WUV", 2048), ("CN", 2 * T), ("KPE", T), ("QN", KT * T), ("QP", 4 * T),
               ("OT", KT * T), ("KN", KT * TP), ("VT", 2 * C), ("REST", 0)):
    ML[_n] = _o
    _o += _s
ML_END = _o
HEAD_ROWS = [(h, h // 2, slice(64 * (h % 2), 64 * (h % 2) + 64)) for h in range(HEADS)]


def stage_mla_project(k, l):
    nc, io = k.nc, k.io
    act_did, pe_did, vec_did = k.tallies("act", "pe", "vec")
    landed = k.sem("mla_weights")
    stored = k.sem("mla_stored")
    p0 = k.panel
    k.panel += 7
    wuk, wuv = k.at(ML["WUK"], 2, C), k.at(ML["WUV"], 2, C)
    CN, KPE, QN, QP = k.at(ML["CN"], 2, T), k.at(ML["KPE"], T), k.at(ML["QN"], KT, T), k.at(ML["QP"], 4, T)
    KN, VT = k.at(ML["KN"], KT, TP), k.at(ML["VT"], 2, C)
    o = ML["REST"]
    QA = k.at(o, 4, T)
    CA = k.at(o + 4 * T, 2, T)
    KA = k.at(o + 6 * T, T)
    SQ = k.at(o + 7 * T, KT, T)
    RQ = k.at(o + 15 * T, KT, T)
    RP = k.at(o + 23 * T, 4, T)
    SK = k.at(o + 27 * T, KT, TP)
    RK = k.at(o + 27 * T + 2048, KT, TP)
    r3 = k.at(o + 27 * T + 4096, 3, T)
    SP4 = k.at(ML["OT"], 4, T)
    sw = k.at(ML["OT"] + 4 * T, 4, T)
    flat = lambda a: a.rearrange("p a b -> p (a b)")
    x = k.normed
    kinds = [("qa", m) for m in range(4)] + [("c", m) for m in range(2)] + [("kp", 0)]
    kinds += [("qn", m) for m in range(8)] + [("qp", m) for m in range(4)] + [("kn", m) for m in range(8)]
    kinds += [("v", m) for m in range(4)]

    with nc.Block() as block:
        @block.sync
        def _(sp):
            sp.dma_start(flat(wuk), io["w_uk"]).then_inc(landed, 16)
            sp.dma_start(flat(k.at(ML["WUKT"], 8, 256)), io["w_ukT"]).then_inc(landed, 16)
            sp.dma_start(flat(wuv), io["w_uv"]).then_inc(landed, 16)
            k.load_panels(sp, pe_did, p0, 7)
            sp.wait_ge(*vec_did.at("cn", 1))
            sp.dma_start(io["ckv"], flat(CN)).then_inc(stored, 16)
            sp.wait_ge(*vec_did.at("kpe"))
            sp.dma_start(io["kpe"], KPE[0:32, :]).then_inc(stored, 16)
            sp.wait_ge(stored, 32)

        @block.tensor
        def _(pe):
            mm = nc.tensor.matmul
            norm_pe(k, pe, act_did, pe_did, flat(SQ))
            pe.wait_ge(*vec_did.at("rs"))
            for n, (what, m) in enumerate(kinds):
                if what == "qn" and m == 0:
                    pe.wait_ge(*act_did.at("sqa"))
                    for i in range(4):
                        mm(k.bank(4, T), k.const("mean512"), SQ[:, i, :], start=i == 0, stop=i == 3)
                    for i in range(2):
                        mm(k.bank(5, T), k.const("mean256"), SQ[:, 4 + i, :], start=i == 0, stop=i == 1)
                    mm(k.bank(6, T), k.const("mean32"), SQ[:, 6, :], start=True, stop=True).then_inc(*pe_did.tick("lat"))
                    pe.wait_ge(*vec_did.at("kpn"))
                    mm(k.bank(7, T), k.const("perm"), KA, start=True, stop=True).then_inc(*pe_did.tick("kperm"))
                    pe.wait_ge(*vec_did.at("qan", 3))
                    pe.wait_ge(landed, 48)
                if n >= 4:
                    pe.wait_ge(*act_did.at("t", n - 4))
                out = k.bank(n % 4, T)
                also = None
                if what in ("qa", "c", "kp"):
                    p = p0 + {"qa": m // 2, "c": 2, "kp": 3}[what]
                    if m % 2 == 0:
                        k.wait_panel(pe, p)
                    for i in range(8):
                        if n == 0:
                            pe.wait_ge(*vec_did.at("x", i))
                        ins = mm(out, k.tile(p, (m % 2) * 8 + i), x[:, i * T:(i + 1) * T], start=i == 0, stop=i == 7)
                    also = ("panel", p)
                elif what in ("qn", "qp"):
                    p = p0 + (4 + m // 4 if what == "qn" else 6)
                    if m % 4 == 0:
                        k.wait_panel(pe, p)
                    for i in range(4):
                        ins = mm(out, k.tile(p, (m % 4) * 4 + i), QA[:, i, :], start=i == 0, stop=i == 3)
                    also = ("panel", p)
                elif what == "kn":
                    if m == 0:
                        pe.wait_ge(*vec_did.at("cn", 1))
                    for i in range(2):
                        ins = mm(out[:, 0:TP], wuk[:, i, m * P:(m + 1) * P], CN[:, i, 0:TP], start=i == 0, stop=i == 1)
                else:
                    t, half = m // 2, m % 2
                    for i in range(2):
                        ins = mm(k.bank(n % 4), CN[:, i, t * P:(t + 1) * P], wuv[:, i, half * 512:half * 512 + 512],
                                 start=i == 0, stop=i == 1)
                ins.then_inc(*pe_did.tick("t", n, also=also))
            pe.wait_ge(*act_did.at("sqn"))
            pe.wait_ge(*vec_did.at("kpe"))
            for i in range(KT):
                ins = mm(k.bank(i, T), k.const("mean64"), SQ[:, i, :], start=True, stop=True)
            ins.then_inc(*pe_did.tick("qstat"))
            pe.wait_ge(*act_did.at("sqp"))
            pe.wait_ge(*act_did.at("rootq"))
            for i in range(4):
                mm(k.bank(i, T), k.const("mean32"), SP4[:, i, :], start=True, stop=True)
            for i in range(KT):
                ins = mm(k.ps[:, 4 + i // 2, (i % 2) * TP:(i % 2 + 1) * TP], k.const("mean64"), SK[:, i, :], start=True, stop=True)
            ins.then_inc(*pe_did.tick("kstat"))
            pe.wait_ge(*vec_did.at("qpn"))
            for i in range(4):
                ins = mm(k.bank(i, T), k.const("perm"), QP[:, i, :], start=True, stop=True)
            ins.then_inc(*pe_did.tick("qperm"))

        @block.scalar
        def _(act):
            s = nc.scalar
            norm_act(k, act, act_did, pe_did, flat(SQ), r3[:, 0, :])
            for n, (what, m) in enumerate(kinds):
                act.wait_ge(*pe_did.at("t", n))
                b = k.bank(n % 4, T)
                dst = {"qa": lambda: QA[:, m, :], "c": lambda: CA[:, m, :], "kp": lambda: KA, "qn": lambda: QN[:, m, :],
                       "qp": lambda: QP[:, m, :], "kn": lambda: KN[:, m, :],
                       "v": lambda: VT[:, m // 2, (m % 2) * 512:(m % 2) * 512 + 512]}[what]()
                src = b[:, 0:TP] if what == "kn" else k.bank(n % 4) if what == "v" else b
                s.activation(dst, src, ACT.Copy).then_inc(*act_did.tick("t", n))
                if what == "kp":
                    act.wait_ge(*act_did.at("t", n))
                    s.activation(SQ[:, 0:4, :], QA, ACT.Square)
                    s.activation(SQ[:, 4:6, :], CA, ACT.Square)
                    s.activation(SQ[:, 6, :], KA, ACT.Square).then_inc(*act_did.tick("sqa"))
                    act.wait_ge(*pe_did.at("lat"))
                    act.wait_ge(*vec_did.at("x", KT - 1))
                    s.activation(r3, k.ps[:, 4:7, 0:T], ACT.Sqrt, bias=k.eps(0)).then_inc(*act_did.tick("rlat"))
            act.wait_ge(*act_did.at("t", len(kinds) - 1))
            s.activation(flat(SQ), flat(QN), ACT.Square).then_inc(*act_did.tick("sqn"))
            s.activation(flat(SP4), flat(QP), ACT.Square)
            s.activation(flat(SK), flat(KN), ACT.Square).then_inc(*act_did.tick("sqp"))
            act.wait_ge(*pe_did.at("qstat"))
            s.activation(RQ, k.ps[:, :, 0:T], ACT.Sqrt, bias=k.eps(0)).then_inc(*act_did.tick("rootq"))
            act.wait_ge(*pe_did.at("kstat"))
            s.activation(RP, k.ps[:, 0:4, 0:T], ACT.Sqrt, bias=k.eps(0))
            s.activation(flat(RK), k.ps[:, 4:8, :].rearrange("p a b -> p (a b)"), ACT.Sqrt, bias=k.eps(0))\
                .then_inc(*act_did.tick("rootk"))

        @block.vector
        def _(vec):
            v = nc.vector
            norm_vec(k, vec, act_did, vec_did, r3[:, 0, :], f"norm_mix{l}")
            vec.wait_ge(*act_did.at("rlat"))
            v.reciprocal(r3, r3).then_inc(*vec_did.tick("r3"))
            vec.wait_ge(*vec_did.at("r3"))
            v.scalar_tensor_tensor(KA, KA, k.param("kr"), r3[:, 2, :], ALU.mult, ALU.mult).then_inc(*vec_did.tick("kpn"))
            for i in range(4):
                v.scalar_tensor_tensor(QA[:, i, :], QA[:, i, :], k.param("q_norm", i), r3[:, 0, :], ALU.mult, ALU.mult)\
                    .then_inc(*vec_did.tick("qan", i))
            for i in range(2):
                v.scalar_tensor_tensor(CN[:, i, :], CA[:, i, :], k.param("kv_norm", i), r3[:, 1, :], ALU.mult, ALU.mult)\
                    .then_inc(*vec_did.tick("cn", i))
            vec.wait_ge(*vec_did.at("kpn"))
            v.tensor_tensor(KPE, KA, k.const("cos"), ALU.mult).then_inc(*vec_did.tick("kc"))
            vec.wait_ge(*pe_did.at("kperm"))
            v.tensor_tensor(sw[:, 0, :], k.bank(7, T), k.const("sin"), ALU.mult).then_inc(*vec_did.tick("ks"))
            vec.wait_ge(*vec_did.at("ks"))
            v.tensor_tensor(KPE, KPE, sw[:, 0, :], ALU.add).then_inc(*vec_did.tick("kpe"))
            vec.wait_ge(*act_did.at("rootq"))
            v.reciprocal(RQ, RQ).then_inc(*vec_did.tick("rq"))
            vec.wait_ge(*vec_did.at("rq"))
            v.tensor_tensor(QN, QN, RQ, ALU.mult).then_inc(*vec_did.tick("qn0"))
            vec.wait_ge(*act_did.at("rootk"))
            v.reciprocal(RP, RP).then_inc(*vec_did.tick("rp"))
            vec.wait_ge(*vec_did.at("rp"))
            v.scalar_tensor_tensor(QP, QP, k.param("qr"), RP, ALU.mult, ALU.mult).then_inc(*vec_did.tick("qpn"))
            v.reciprocal(RK, RK).then_inc(*vec_did.tick("rk"))
            vec.wait_ge(*vec_did.at("rk"))
            v.tensor_tensor(KN, KN, RK, ALU.mult).then_inc(*vec_did.tick("kn"))
            v.tensor_scalar(flat(QN), flat(QN), k.param("qn"), k.param("kn"), ALU.mult, ALU.mult).then_inc(*vec_did.tick("qn"))
            vec.wait_ge(*pe_did.at("qperm"))
            v.tensor_tensor(sw, k.ps[:, 0:4, 0:T], bcm(k.const("sin"), 4), ALU.mult).then_inc(*vec_did.tick("qs"))
            v.tensor_tensor(QP, QP, bcm(k.const("cos"), 4), ALU.mult).then_inc(*vec_did.tick("qc"))
            vec.wait_ge(*vec_did.at("qc"))
            v.tensor_tensor(QP, QP, sw, ALU.add).then_inc(*vec_did.tick("qp"))


def stage_mla_prompt(k):
    nc = k.nc
    act_did, pe_did, vec_did, pool_did = k.tallies("act", "pe", "vec", "pool")
    KPE, QN, QP = k.at(ML["KPE"], T), k.at(ML["QN"], KT, T), k.at(ML["QP"], 4, T)
    KN, VT, OT = k.at(ML["KN"], KT, TP), k.at(ML["VT"], 2, C), k.at(ML["OT"], KT, T)
    o = ML["REST"]
    S = [k.at(o + 1024 * i, 4, 256) for i in range(2)]
    PT = [k.at(o + 2048 + 1024 * i, 8, P) for i in range(2)]
    st = k.at(o + 4096, 8, 16)
    QM = [k.at(o + 4096 + 128 + 512 * i, 4, P) for i in range(2)]
    NG = 8

    def head(g, i):
        h = (g % 4) * 4 + (i % 2) * 2 + i // 2
        return h, h // 2, slice(64 * (h % 2), 64 * (h % 2) + 64)

    with nc.Block() as block:
        @block.tensor
        def _(pe):
            mm = nc.tensor.matmul

            def scores(g):
                qt = g // 4
                nk = (qt + 1) * P
                if g >= 2:
                    pe.wait_ge(*vec_did.at("s", g - 2))
                pe.wait_ge(*pool_did.at("qm", g))
                for i in range(4):
                    h, f, r = head(g, i)
                    out = k.ps[:, (g % 2) * 2 + i // 2, (i % 2) * 256:(i % 2) * 256 + nk]
                    mm(out, QN[r, f, qt * P:(qt + 1) * P], KN[r, f, 0:nk], start=True, stop=False)
                    ins = mm(out, QM[g % 2][:, h % 4, :], KPE[:, 0:nk], start=False, stop=True)
                ins.then_inc(*pe_did.tick("s", g))

            def values(g):
                qt = g // 4
                pe.wait_ge(*vec_did.at("p", g))
                if g:
                    pe.wait_ge(*act_did.at("pt", g - 1))
                for i in range(4):
                    for kt in range(qt + 1):
                        ins = nc.tensor.transpose(k.ps[:, 4 + i // 2, ((i % 2) * 2 + kt) * P:((i % 2) * 2 + kt + 1) * P],
                                                  S[g % 2][:, i, kt * P:(kt + 1) * P], k.const("ident"))
                ins.then_inc(*pe_did.tick("pt", g))
                pe.wait_ge(*act_did.at("pt", g))
                if g >= 2:
                    pe.wait_ge(*act_did.at("o", g - 2))
                for i in range(4):
                    h, f, r = head(g, i)
                    for kt in range(qt + 1):
                        ins = mm(k.ps[r, 6 + g % 2, (i % 2) * P:(i % 2 + 1) * P], VT[:, kt, h * 64:h * 64 + 64],
                                 PT[g % 2][:, 2 * i + kt, :], start=kt == 0, stop=kt == qt)
                ins.then_inc(*pe_did.tick("o", g))

            for g in range(NG + 1):
                if g < NG:
                    scores(g)
                if g:
                    values(g - 1)

        @block.gpsimd
        def _(pool):
            nc.gpsimd.memset(QM[0], 0.0)
            nc.gpsimd.memset(QM[1], 0.0).then_inc(*pool_did.tick("zero"))
            pool.wait_ge(*pool_did.at("zero"))
            for g in range(NG):
                if g >= 2:
                    pool.wait_ge(*pe_did.at("s", g - 2))
                for a in range(4):
                    rows = slice(32 * a, 32 * a + 32)
                    ins = nc.gpsimd.tensor_copy(QM[g % 2][rows, a, :], QP[rows, g % 4, (g // 4) * P:(g // 4 + 1) * P])
                ins.then_inc(*pool_did.tick("qm", g))

        @block.vector
        def _(vec):
            v = nc.vector
            for g in range(NG):
                qt = g // 4
                Sg = S[g % 2]
                ps = k.ps[:, (g % 2) * 2:(g % 2) * 2 + 2, :].rearrange("p a b -> p (a b)").rearrange("p (a b) -> p a b", a=4)
                vec.wait_ge(*pe_did.at("s", g))
                if g >= 2:
                    vec.wait_ge(*pe_did.at("pt", g - 2))
                v.tensor_tensor(Sg[:, :, qt * P:(qt + 1) * P], ps[:, :, qt * P:(qt + 1) * P], bcm(k.const("causal"), 4), ALU.add)
                if qt:
                    v.tensor_copy(Sg[:, :, 0:P], ps[:, :, 0:P])
                v.tensor_copy(st[:, g, 12:13], ps[:, 0, 0:1]).then_inc(*vec_did.tick("s", g))
                vec.wait_ge(*vec_did.at("s", g))
                v.tensor_reduce(st[:, g, 0:4], Sg[:, :, 0:(qt + 1) * P], AX, ALU.max).then_inc(*vec_did.tick("m", g))
                vec.wait_ge(*vec_did.at("m", g))
                v.tensor_scalar(st[:, g, 4:8], st[:, g, 0:4], -MLA_SCALE, None, ALU.mult).then_inc(*vec_did.tick("nm", g))
                vec.wait_ge(*act_did.at("e", g, 3))
                v.reciprocal(st[:, g, 12:16], st[:, g, 8:12]).then_inc(*vec_did.tick("rd", g))
                vec.wait_ge(*vec_did.at("rd", g))
                v.tensor_tensor(Sg[:, :, 0:(qt + 1) * P], Sg[:, :, 0:(qt + 1) * P], bc(st[:, g, 12:16], (qt + 1) * P), ALU.mult)\
                    .then_inc(*vec_did.tick("p", g))

        @block.scalar
        def _(act):
            s = nc.scalar

            def exps(g):
                n = (g // 4 + 1) * P
                act.wait_ge(*vec_did.at("nm", g))
                for i in range(4):
                    s.activation(S[g % 2][:, i, 0:n], S[g % 2][:, i, 0:n], ACT.Exp, bias=st[:, g, 4 + i:5 + i], scale=MLA_SCALE,
                                 accum_out=st[:, g, 8 + i:9 + i]).then_inc(*act_did.tick("e", g, i))

            def out(g):
                act.wait_ge(*pe_did.at("pt", g))
                if g >= 2:
                    act.wait_ge(*pe_did.at("o", g - 2))
                for kt in range(g // 4 + 1):
                    ins = s.activation(PT[g % 2][:, kt::2, :],
                                       k.ps[:, 4:6, :].rearrange("p a b -> p (a b)").rearrange("p (a b) -> p a b", a=8)[:, kt::2, :],
                                       ACT.Copy)
                ins.then_inc(*act_did.tick("pt", g))
                act.wait_ge(*pe_did.at("o", g))
                f = (g % 4) * 2
                s.activation(OT[:, f:f + 2, (g // 4) * P:(g // 4 + 1) * P],
                             k.ps[:, 6 + g % 2, 0:256].rearrange("p (a b) -> p a b", a=2), ACT.Copy).then_inc(*act_did.tick("o", g))

            for g in range(NG + 1):
                if g < NG:
                    exps(g)
                if g:
                    out(g - 1)


def stage_mla_sample(k):
    nc, io = k.nc, k.io
    act_did, pe_did, vec_did, pool_did = k.tallies("act", "pe", "vec", "pool")
    landed = [k.sem("pages_a"), k.sem("pages_b")]
    wuk, wukT = k.at(ML["WUK"], 2, C), k.at(ML["WUKT"], KT, 256)
    CN, KPE, QN, QP = k.at(ML["CN"], 2, T), k.at(ML["KPE"], T), k.at(ML["QN"], KT, T), k.at(ML["QP"], 4, T)
    o = ML["KN"]
    pages = k.at(o, 16, 640)
    o += 16 * 640
    SQ = [k.at(o + 1024 * i, HEADS, 64) for i in range(2)]
    o += 2048
    QL = k.at(o, 2, NB, P)
    o += 2048
    QX = k.at(o, NB, P)
    o += 1024
    OL = k.at(ML_OL, 2, HEADS, 64)
    o = ML_SMALL
    mx, diag, rden, cnew_a, cnew_b, ss = (k.at(o + 256 * i, 256) for i in range(6))
    m1 = ss[:, 128:129]
    cnew = [cnew_a, cnew_b]
    S = [k.normed[:, 1152 * i:1152 * (i + 1)].rearrange("p (a b) -> p a b", a=9) for i in range(2)]

    with nc.Block() as block:
        @block.sync
        def _(sp):
            for b in range(NB):
                if b >= 2:
                    sp.wait_ge(*pe_did.at("pv", b - 2))
                for kt in range(NPG):
                    page = sp.value_load(k.table[0:1, b * NPG + kt:b * NPG + kt + 1], min_val=0, max_val=POOL - 1)
                    sp.dma_start(pages[:, (b % 2) * NPG + kt, :],
                                 io["pages"][bass.ds(page, 1), :, :].rearrange("a p n -> (a p) n")).then_inc(landed[b % 2], 16)

        @block.gpsimd
        def _(pool):
            nc.gpsimd.memset(QX, 0.0).then_inc(*pool_did.tick("zero"))
            for i in range(2):
                nc.gpsimd.memset(S[i][:, 8, :], NEG).then_inc(*pool_did.tick("neg", i))

        @block.tensor
        def _(pe):
            mm = nc.tensor.matmul
            for rc in range(2):
                for h, f, r in HEAD_ROWS:
                    ins = mm(k.ps[:, 2 * rc + h % 2, f * 64:(f + 1) * 64], wukT[r, f, rc * P:(rc + 1) * P],
                             QN[r, f, TP:T], start=True, stop=True)
            ins.then_inc(*pe_did.tick("ql"))
            pe.wait_ge(*act_did.at("ql"))
            pe.wait_ge(*vec_did.at("qx"))

            def tile(b, kt):
                n = b * 9 + kt
                if kt == 0:
                    pe.wait_ge(landed[b % 2], 16 * NPG * (b // 2 + 1))
                if kt < NPG:
                    pg = pages[:, (b % 2) * NPG + kt, :]
                    ct, kp, m = [pg[:, 256:384], pg[:, 384:512]], pg[:, 512:640], P
                else:
                    cs = slice(TP + TS * b, TP + TS * b + TS)
                    ct, kp, m = [CN[:, 0, cs], CN[:, 1, cs]], KPE[:, cs], TS
                if n >= 2:
                    pe.wait_ge(*act_did.at("sq", n - 2))
                    pe.wait_ge(*vec_did.at("s", n - 2))
                for half in range(2):
                    for rc in range(2):
                        ins = mm(k.ps[0:m, 2 * (n % 2) + half, :], ct[rc], wuk[:, rc, half * 512:half * 512 + 512],
                                 start=rc == 0, stop=rc == 1)
                ins.then_inc(*pe_did.tick("kraw", n))
                sc = k.ps[0:m, 4 + n % 2, :]
                for rc in range(2):
                    mm(sc[:, 0:P], ct[rc], QL[:, rc, b, :], start=rc == 0, stop=rc == 1)
                mm(sc[:, P:2 * P], kp, QX[:, b, :], start=True, stop=True).then_inc(*pe_did.tick("s", n))

            def turn(b):
                pe.wait_ge(*vec_did.at("mx", b))
                pe.wait_ge(*act_did.at("cn", b))
                nc.tensor.transpose(k.ps[:, 6, 0:P], mx[:, 0:P], k.const("ident")).then_inc(*pe_did.tick("mt", b))

            def turn_new(b):
                if b:
                    pe.wait_ge(*vec_did.at("sub", b - 1))
                for rc in range(2):
                    ins = nc.tensor.transpose(k.ps[0:TS, 6, 256 + P * rc:256 + P * rc + P],
                                              CN[:, rc, TP + TS * b:TP + TS * b + TS], k.const("ident"))
                ins.then_inc(*pe_did.tick("cn", b))

            def spread(b):
                pe.wait_ge(*vec_did.at("diag", b))
                mm(k.ps[:, 6, P:2 * P], k.const("ones"), diag[:, 0:P], start=True, stop=True).then_inc(*pe_did.tick("mb", b))

            def values(b):
                pe.wait_ge(*act_did.at("e", b))
                if b:
                    pe.wait_ge(*vec_did.at("ol", b - 1))
                s = S[b % 2]
                for part in range(3):
                    for kt in range(9):
                        rows = slice(0, P if kt < 8 else TS)
                        lhs = k.const("ones") if part == 2 else \
                            pages[:, (b % 2) * NPG + kt, part * P:(part + 1) * P] if kt < 8 else cnew[b % 2][:, part * P:(part + 1) * P]
                        ins = mm(k.ps[:, 7, part * P:(part + 1) * P], lhs[rows, :], s[rows, kt, :], start=kt == 0, stop=kt == 8)
                ins.then_inc(*pe_did.tick("pv", b))

            for b in range(NB + 1):
                for kt in range(9):
                    if b < NB:
                        tile(b, kt)
                    if b < NB and kt == 5:
                        turn_new(b)
                    if b and kt == 1:
                        turn(b - 1)
                    if b and kt == 3:
                        spread(b - 1)
                    if b and kt == 6:
                        values(b - 1)

        @block.scalar
        def _(act):
            s = nc.scalar
            act.wait_ge(*pe_did.at("ql"))
            for rc in range(2):
                for par in range(2):
                    ins = s.activation(QL[:, rc, :, :].rearrange("p b (h q) -> p h b q", h=HEADS)[:, par::2, :, :],
                                       k.ps[:, 2 * rc + par, :].rearrange("p (f b q) -> p f b q", f=KT, b=NB), ACT.Copy)
            ins.then_inc(*act_did.tick("ql"))

            def root(n):
                m = P if n % 9 < NPG else TS
                act.wait_ge(*vec_did.at("ss", n))
                s.activation(ss[0:m, 32 + 16 * (n % 2):48 + 16 * (n % 2)], ss[0:m, 16 * (n % 2):16 * (n % 2) + 16], ACT.Sqrt,
                             bias=k.eps(2, slice(0, m))).then_inc(*act_did.tick("root", n))

            for b in range(NB + 1):
                for kt in range(9):
                    if b == NB and kt == 0:
                        root(NB * 9 - 1)
                    if b < NB:
                        n = b * 9 + kt
                        m = P if kt < NPG else TS
                        act.wait_ge(*pe_did.at("kraw", n))
                        if n >= 2:
                            act.wait_ge(*vec_did.at("ss", n - 2))
                        s.activation(SQ[n % 2][0:m, :, :].rearrange("p a b -> p (a b)"),
                                     k.ps[0:m, 2 * (n % 2):2 * (n % 2) + 2, :].rearrange("p a b -> p (a b)"), ACT.Square)\
                            .then_inc(*act_did.tick("sq", n))
                        if n:
                            root(n - 1)
                    if b < NB and kt == 6:
                        act.wait_ge(*pe_did.at("cn", b))
                        s.activation(cnew[b % 2][0:TS, :], k.ps[0:TS, 6, 256:512], ACT.Copy).then_inc(*act_did.tick("cn", b))
                    if b and kt == 4:
                        act.wait_ge(*vec_did.at("sub", b - 1))
                        sb = S[(b - 1) % 2]
                        s.activation(sb.rearrange("p a b -> p (a b)"), sb.rearrange("p a b -> p (a b)"), ACT.Exp, scale=MLA_SCALE)\
                            .then_inc(*act_did.tick("e", b - 1))

        @block.vector
        def _(vec):
            v = nc.vector
            vec.wait_ge(*pool_did.at("zero"))
            for a in range(4):
                rows = slice(32 * a, 32 * a + 32)
                ins = v.tensor_copy(QX[rows, :, :].rearrange("p b (g a q) -> p g a b q", g=4, a=4)[:, :, a, :, :],
                                    QP[rows, :, TP:T].rearrange("p g (b q) -> p g b q", b=NB))
            ins.then_inc(*vec_did.tick("qx"))
            vec.wait_ge(*pool_did.at("neg", 1))
            for b in range(NB + 1):
                for kt in range(9):
                    if b < NB:
                        n = b * 9 + kt
                        m = P if kt < NPG else TS
                        s1, rk = ss[0:m, 16 * (n % 2):16 * (n % 2) + 16], ss[0:m, 32 + 16 * (n % 2):48 + 16 * (n % 2)]
                        vec.wait_ge(*act_did.at("sq", n))
                        v.tensor_reduce(s1, SQ[n % 2][0:m, :, :], AX, ALU.add).then_inc(*vec_did.tick("ss", n))
                        vec.wait_ge(*act_did.at("root", n))
                        v.reciprocal(rk, rk).then_inc(*vec_did.tick("rk", n))
                        vec.wait_ge(*vec_did.at("rk", n))
                        vec.wait_ge(*pe_did.at("s", n))
                        if kt == 0 and b >= 2:
                            vec.wait_ge(*pe_did.at("pv", b - 2))
                        d = S[b % 2][0:m, kt, :]
                        v.scalar_tensor_tensor(d.rearrange("p (h q) -> p h q", h=HEADS),
                                               k.ps[0:m, 4 + n % 2, 0:P].rearrange("p (h q) -> p h q", h=HEADS), 8.0,
                                               bc(rk, TS), ALU.mult, ALU.mult).then_inc(*vec_did.tick("s0", n))
                        vec.wait_ge(*vec_did.at("s0", n))
                        v.tensor_tensor(d, d, k.ps[0:m, 4 + n % 2, P:2 * P], ALU.add).then_inc(*vec_did.tick("s", n))
                        if kt == 8:
                            vec.wait_ge(*vec_did.at("s", n))
                            dh = d.rearrange("p (h q) -> p h q", h=HEADS)
                            v.tensor_tensor(dh, dh, bcm(k.const("new8", slice(0, TS)), HEADS), ALU.add).then_inc(*vec_did.tick("new", b))
                            vec.wait_ge(*vec_did.at("new", b))
                            v.tensor_reduce(mx[:, 0:P], S[b % 2].rearrange("p k c -> p c k"), AX, ALU.max)\
                                .then_inc(*vec_did.tick("mx", b))
                    if b and kt == 1:
                        vec.wait_ge(*pe_did.at("mt", b - 1))
                        v.tensor_reduce(m1[:, 0:1], k.ps[:, 6, 0:P], AX, ALU.max).then_inc(*vec_did.tick("m1", b - 1))
                        vec.wait_ge(*vec_did.at("m1", b - 1))
                        v.tensor_scalar(diag[:, 0:P], k.const("ident"), m1[:, 0:1], None, ALU.mult).then_inc(*vec_did.tick("diag", b - 1))
                    if b and kt == 3:
                        vec.wait_ge(*pe_did.at("mb", b - 1))
                        sb = S[(b - 1) % 2]
                        v.tensor_tensor(sb, sb, bcm(k.ps[:, 6, P:2 * P], 9), ALU.subtract).then_inc(*vec_did.tick("sub", b - 1))
                    if b and kt == 7:
                        vec.wait_ge(*pe_did.at("pv", b - 1))
                        v.reciprocal(rden[:, 0:P], k.ps[:, 7, 256:384]).then_inc(*vec_did.tick("rd", b - 1))
                        vec.wait_ge(*vec_did.at("rd", b - 1))
                        for rc in range(2):
                            ins = v.tensor_tensor(OL[:, rc, :, (b - 1) * TS:b * TS],
                                                  k.ps[:, 7, rc * P:(rc + 1) * P].rearrange("p (h q) -> p h q", h=HEADS),
                                                  rden[:, 0:P].rearrange("p (h q) -> p h q", h=HEADS), ALU.mult)
                        ins.then_inc(*vec_did.tick("ol", b - 1))


ML_OL = ML["KN"] + 16 * 640 + 2048 + 2048 + 1024
ML_SMALL = ML_OL + 2048
assert ML_SMALL + 6 * 256 <= 33400, ML_SMALL


def stage_mla_output(k):
    nc = k.nc
    act_did, pe_did, vec_did = k.tallies("act", "pe", "vec")
    p0 = k.panel
    k.panel += 4
    wuv, OL, OT = k.at(ML["WUV"], 2, C), k.at(ML_OL, 2, HEADS, 64), k.at(ML["OT"], KT, T)
    with nc.Block() as block:
        @block.sync
        def _(sp):
            k.load_panels(sp, pe_did, p0, 4)

        @block.tensor
        def _(pe):
            for h, f, r in HEAD_ROWS:
                for rc in range(2):
                    ins = nc.tensor.matmul(k.ps[r, 7, f * 64:(f + 1) * 64], wuv[:, rc, h * 64:(h + 1) * 64], OL[:, rc, h, :],
                                           start=rc == 0, stop=rc == 1)
            ins.then_inc(*pe_did.tick("uv"))
            out_project_pe(k, pe, pe_did, vec_did, p0, lambda i: OT[:, i, :], KT, lambda e, i: e.wait_ge(*act_did.at("uv")))

        @block.scalar
        def _(act):
            act.wait_ge(*pe_did.at("uv"))
            nc.scalar.activation(OT[:, :, TP:T], k.ps[:, 7, :].rearrange("p (a b) -> p a b", a=KT), ACT.Copy)\
                .then_inc(*act_did.tick("uv"))

        @block.vector
        def _(vec):
            out_project_vec(k, vec, pe_did, vec_did)


MH = 32
MT = 16
MB, _o = {}, 0
for _n, _s in (("XBC", 24 * T), ("ZS", MT * T), ("Y", MT * T), ("AC", T), ("DT", T), ("EA", T), ("TE", T), ("TM", 9 * MH),
               ("EE", 10 * MH), ("REST", 0)):
    MB[_n] = _o
    _o += _s


def stage_mamba_project(k, l):
    nc, io = k.nc, k.io
    act_did, pe_did, vec_did, pool_did = k.tallies("act", "pe", "vec", "pool")
    landed = k.sem("conv_in")
    stored = k.sem("conv_stored")
    p0 = k.panel
    k.panel += 21
    XBC, ZS, DT = k.at(MB["XBC"], 24, T), k.at(MB["ZS"], MT, T), k.at(MB["DT"], T)
    o = MB["REST"]
    NS = 3
    rw = TP + 3 + NB * 11
    raw = [k.at(o + rw * i, rw) for i in range(NS)]
    o += rw * NS
    acc = [k.at(o + T * i, T) for i in range(NS)]
    o += T * NS
    cin = k.at(o, 24, 24)
    o += 576
    cout = k.at(o, 24, 27)
    o += 648
    SQ = k.at(o, KT * T)
    o += KT * T
    rs = k.at(o, T)
    x = k.normed
    rawp = lambda i: raw[i % NS][:, 0:TP + 3]
    raws = lambda i: raw[i % NS][:, TP + 3:rw].rearrange("p (b t) -> p b t", b=NB)
    accs = lambda i: acc[i % NS][:, TP:T].rearrange("p (b t) -> p b t", b=NB)
    ntile = 16 + 24 + 1

    with nc.Block() as block:
        @block.sync
        def _(sp):
            sp.dma_start(cin.rearrange("p a b -> p (a b)"), io["conv_in"]).then_inc(landed, 16)
            k.load_panels(sp, pe_did, p0, 21)

        @block.tensor
        def _(pe):
            norm_pe(k, pe, act_did, pe_did, SQ)
            for n in range(ntile):
                p = p0 + n // 2
                if n % 2 == 0:
                    k.wait_panel(pe, p)
                if n >= 4:
                    pe.wait_ge(*act_did.at("t", n - 4))
                m = P if n < 40 else MH
                for i in range(KT):
                    if n == 0:
                        pe.wait_ge(*vec_did.at("x", i))
                    ins = nc.tensor.matmul(k.bank(n % 4, T)[0:m, :], k.tile(p, (n % 2) * 8 + i)[:, 0:m], x[:, i * T:(i + 1) * T],
                                           start=i == 0, stop=i == KT - 1)
                ins.then_inc(*pe_did.tick("t", n, also=("panel", p)))

        @block.scalar
        def _(act):
            s = nc.scalar
            norm_act(k, act, act_did, pe_did, SQ, rs)
            for n in range(ntile):
                act.wait_ge(*pe_did.at("t", n))
                b = k.bank(n % 4, T)
                if n < 16:
                    s.activation(ZS[:, n, :], b, ACT.Silu).then_inc(*act_did.tick("t", n))
                elif n < 40:
                    i = n - 16
                    if i >= NS:
                        act.wait_ge(*vec_did.at("conv", i - NS))
                        act.wait_ge(*pool_did.at("out", i - NS))
                    s.activation(rawp(i)[:, 3:TP + 3], b[:, 0:TP], ACT.Copy)
                    s.activation(raws(i)[:, :, 3:11], b[:, TP:T].rearrange("p (b t) -> p b t", b=NB), ACT.Copy)\
                        .then_inc(*act_did.tick("t", n))
                else:
                    s.activation(DT[0:MH, :], b[0:MH, :], ACT.Identity, bias=k.param("dt_bias")[0:MH, :]).then_inc(*act_did.tick("t", n))
                if n >= 17:
                    i = n - 17
                    act.wait_ge(*vec_did.at("conv", i))
                    s.activation(XBC[:, i, :], acc[i % NS], ACT.Silu, bias=k.param("conv_b", i)).then_inc(*act_did.tick("xbc", i))

        @block.gpsimd
        def _(pool):
            for i in range(NS):
                nc.gpsimd.memset(raw[i][:, 0:3], 0.0).then_inc(*pool_did.tick("zero", i))
            for i in range(24):
                pool.wait_ge(*act_did.at("t", 16 + i))
                nc.gpsimd.tensor_copy(cout[:, i, 0:3], rawp(i)[:, TP:TP + 3])
                nc.gpsimd.tensor_copy(cout[:, i, 3:27].rearrange("p (b t) -> p b t", b=NB), raws(i)[:, :, 8:11])\
                    .then_inc(*pool_did.tick("out", i))
            pool.wait_ge(*pool_did.at("out", 23))
            nc.gpsimd.dma_start(io["conv_out"], cout.rearrange("p a b -> p (a b)")).then_inc(stored, 16)
            pool.wait_ge(stored, 16)

        @block.vector
        def _(vec):
            v = nc.vector
            norm_vec(k, vec, act_did, vec_did, rs, f"norm_mix{l}")
            vec.wait_ge(landed, 16)
            vec.wait_ge(*pool_did.at("zero", NS - 1))
            for i in range(24):
                if i >= NS:
                    vec.wait_ge(*act_did.at("xbc", i - NS))
                    vec.wait_ge(*vec_did.at("conv", i - NS))
                v.tensor_copy(raws(i)[:, :, 0:3], cin[:, i, :].rearrange("p (b t) -> p b t", b=NB)).then_inc(*vec_did.tick("pad", i))
                vec.wait_ge(*vec_did.at("pad", i))
                vec.wait_ge(*act_did.at("t", 16 + i))
                for j in range(4):
                    w = k.param("conv_w", j * 24 + i)
                    if j:
                        vec.wait_ge(*vec_did.at("tap", i, j - 1))
                        v.scalar_tensor_tensor(acc[i % NS][:, 0:TP], rawp(i)[:, j:j + TP], w, acc[i % NS][:, 0:TP], ALU.mult, ALU.add)
                        ins = v.scalar_tensor_tensor(accs(i), raws(i)[:, :, j:j + TS], w, accs(i), ALU.mult, ALU.add)
                    else:
                        v.tensor_scalar(acc[i % NS][:, 0:TP], rawp(i)[:, 0:TP], w, None, ALU.mult)
                        ins = v.tensor_scalar(accs(i), raws(i)[:, :, 0:TS], w, None, ALU.mult)
                    ins.then_inc(*vec_did.tick("tap", i, j, also=("conv", i) if j == 3 else None))


def stage_mamba_decay(k):
    nc = k.nc
    act_did, pe_did, vec_did = k.tallies("act", "pe", "vec")
    AC, DT, EA, TE = (k.at(MB[n], T, rows=MH) for n in ("AC", "DT", "EA", "TE"))
    TM = k.at(MB["TM"], 9, MH)
    EE = k.at(MB["EE"], 10, MH)
    EAB = k.at(MB["Y"], MT, T)
    o = MB["REST"]
    t1, ends, dg, A = k.at(o, T, rows=MH), k.at(o + T, 10, rows=MH), k.at(o + T + 16, 10, MH, rows=MH), k.at(o + 2 * T + 64, 1, rows=MH)
    t2 = k.at(o + 3 * T, T, rows=MH)
    with nc.Block() as block:
        @block.scalar
        def _(act):
            s = nc.scalar
            s.activation(A, k.param("a_log")[0:MH, :], ACT.Exp)
            s.activation(t1, DT, ACT.Abs).then_inc(*act_did.tick("abs"))
            act.wait_ge(*act_did.at("abs"))
            s.activation(t2, t1, ACT.Exp, scale=-1.0).then_inc(*act_did.tick("e"))
            act.wait_ge(*act_did.at("e"))
            s.activation(t1, t2, ACT.Ln, bias=1.0).then_inc(*act_did.tick("ln"))
            act.wait_ge(*vec_did.at("ac"))
            s.activation(EA, AC, ACT.Exp).then_inc(*act_did.tick("ea"))
            act.wait_ge(*vec_did.at("te"))
            s.activation(TE, TE, ACT.Exp).then_inc(*act_did.tick("te"))
            act.wait_ge(*pe_did.at("ee"))
            s.activation(EE, k.ps[:, 7, 0:10 * MH].rearrange("p (a b) -> p a b", a=10), ACT.Exp).then_inc(*act_did.tick("ee"))
            for f in range(MT):
                act.wait_ge(*pe_did.at("eab", f))
                s.activation(EAB[:, f, :], k.bank(f % 4, T), ACT.Copy).then_inc(*act_did.tick("eab", f))

        @block.vector
        def _(vec):
            v = nc.vector
            vec.wait_ge(*act_did.at("ln"))
            v.scalar_tensor_tensor(DT, DT, 0.0, t1, ALU.max, ALU.add).then_inc(*vec_did.tick("dt"))
            vec.wait_ge(*vec_did.at("dt"))
            v.tensor_scalar(t2, DT, A, -1.0, ALU.mult, ALU.mult).then_inc(*vec_did.tick("da"))
            vec.wait_ge(*vec_did.at("da"))
            v.tensor_tensor_scan(AC, k.const("reset_m", slice(0, MH)), t2, 0.0, ALU.mult, ALU.add).then_inc(*vec_did.tick("ac"))
            vec.wait_ge(*vec_did.at("ac"))
            v.tensor_copy(ends[:, 0:2], AC[:, P - 1:TP:P])
            v.tensor_copy(ends[:, 2:10], AC[:, TP + TS - 1::TS]).then_inc(*vec_did.tick("ends"))
            vec.wait_ge(*vec_did.at("ends"))
            v.tensor_tensor(dg, bcm(k.const("ident", slice(0, MH))[:, 0:MH], 10), bc(ends, MH), ALU.mult).then_inc(*vec_did.tick("dg"))
            v.tensor_tensor(TE[:, 0:TP].rearrange("p (a b) -> p a b", a=2), bc(ends[:, 0:2], P),
                            AC[:, 0:TP].rearrange("p (a b) -> p a b", a=2), ALU.subtract)
            v.tensor_tensor(TE[:, TP:T].rearrange("p (a b) -> p a b", a=NB), bc(ends[:, 2:10], TS),
                            AC[:, TP:T].rearrange("p (a b) -> p a b", a=NB), ALU.subtract).then_inc(*vec_did.tick("te"))
            vec.wait_ge(*pe_did.at("tm"))
            for i in range(3):
                v.tensor_copy(TM[:, 3 * i:3 * i + 2, :], k.ps[:, 6, 96 * i:96 * i + 64].rearrange("p (a b) -> p a b", a=2))
                ins = v.tensor_copy(TM[0:64, 3 * i + 2, :], k.ps[0:64, 6, 96 * i + 64:96 * i + 96])
            ins.then_inc(*vec_did.tick("tm"))

        @block.tensor
        def _(pe):
            mm = nc.tensor.matmul
            pe.wait_ge(*vec_did.at("dg"))
            mm(k.bank(7, T), k.const("ones")[0:MH, :], dg.rearrange("p a b -> p (a b)"), start=True, stop=True)\
                .then_inc(*pe_did.tick("ee"))
            pe.wait_ge(*act_did.at("te"))
            for i, src in enumerate((DT, AC, TE)):
                for c in range(3):
                    n = P if c < 2 else 64
                    ins = nc.tensor.transpose(k.ps[0:n, 6, 96 * i + 32 * c:96 * i + 32 * c + 32], src[:, c * P:c * P + n],
                                              k.const("ident")[0:MH, 0:MH])
            ins.then_inc(*pe_did.tick("tm"))
            for f in range(MT):
                if f >= 4:
                    pe.wait_ge(*act_did.at("eab", f - 4))
                for h in (2 * f, 2 * f + 1):
                    r = slice(64 * (h % 2), 64 * (h % 2) + 64)
                    ins = mm(k.bank(f % 4, T)[r, :], k.const("ident")[0:MH, h:h + 1].to_broadcast([MH, 64]), EA, start=True, stop=True)
                ins.then_inc(*pe_did.tick("eab", f))


def stage_mamba_scan(k):
    nc, io = k.nc, k.io
    act_did, pe_did, vec_did, pool_did = k.tallies("act", "pe", "vec", "pool")
    state_in = [k.sem("ssm_in_a"), k.sem("ssm_in_b")]
    state_out = [k.sem("ssm_out_a"), k.sem("ssm_out_b")]
    prompt_out = k.sem("ssm_prompt_out")
    XBC, Y, AC = k.at(MB["XBC"], 24, T), k.at(MB["Y"], MT, T), k.at(MB["AC"], T, rows=MH)
    TM, EE = k.at(MB["TM"], 9, MH), k.at(MB["EE"], 10, MH)
    o = MB["REST"]
    XDT, XDW, HT = (k.at(o + 2048 * i, MH, 64) for i in range(3))
    HB = [k.at(o + 2048 * (3 + i), MH, 64) for i in range(2)]
    o += 2048 * 5
    SEG = [k.at(o + 512 * i, 4, P) for i in range(2)]
    CB, BT = k.at(o + 1024, 4, P), k.at(o + 1536, 4, P)
    YT = k.at(o + 2048, 2, P)
    YI = k.normed[:, 0:1024].rearrange("p (a b) -> p a b", a=MT)
    BM = [k.normed[:, 1024 + 512 * i:1536 + 512 * i].rearrange("p (a b) -> p a b", a=4) for i in range(2)]
    flat = lambda a: a.rearrange("p a b -> p (a b)")
    span = [(0, P), (P, P), (TP, 64)]

    with nc.Block() as block:
        @block.sync
        def _(sp):
            for b in range(2):
                sp.dma_start(flat(HB[b]), io["ssm"][b]).then_inc(state_in[b], 16)
            sp.wait_ge(*vec_did.at("HT", 1))
            sp.dma_start(io["ssm_prompt"], flat(HT)).then_inc(prompt_out, 16)
            for b in range(NB):
                sp.wait_ge(*vec_did.at("HB", b))
                sp.dma_start(io["ssm_sample"][b], flat(HB[b % 2])).then_inc(state_out[b % 2], 16)
                if b + 2 < NB:
                    sp.wait_ge(state_out[b % 2], 16 * (b // 2 + 1))
                    sp.dma_start(flat(HB[b % 2]), io["ssm"][b + 2]).then_inc(state_in[b % 2], 16)
            sp.wait_ge(prompt_out, 16)
            for q in state_out:
                sp.wait_ge(q, 16 * NB // 2)

        @block.tensor
        def _(pe):
            mm = nc.tensor.matmul
            for c in range(3):
                t0, n = span[c]
                tok = slice(t0, t0 + n)
                if c:
                    pe.wait_ge(*vec_did.at("y", c - 1, 7))
                    if c < 3:
                        pe.wait_ge(*vec_did.at("HT", c - 1))
                for f in range(MT):
                    ins = nc.tensor.transpose(k.ps[0:n, f // 4, (f % 4) * P:(f % 4 + 1) * P], XBC[:, f, tok], k.const("ident"))
                ins.then_inc(*pe_did.tick("xt", c))
                for g in range(4):
                    ins = nc.tensor.transpose(k.ps[0:n, 4, g * P:(g + 1) * P], XBC[:, 16 + g, tok], k.const("ident"))
                ins.then_inc(*pe_did.tick("bt", c))
                for g in range(4):
                    ins = mm(k.ps[0:n, 5, g * P:g * P + n], XBC[:, 16 + g, tok], XBC[:, 20 + g, tok], start=True, stop=True)
                ins.then_inc(*pe_did.tick("cb", c))

                def seg(q):
                    if q >= 2:
                        pe.wait_ge(*vec_did.at("seg", c, q - 2))
                    for i in range(4):
                        h = 4 * q + i
                        ins = mm(k.ps[0:n, 6 + q % 2, i * P:i * P + n], k.const("ident")[0:MH, h:h + 1].to_broadcast([MH, n]),
                                 AC[:, tok], start=True, stop=True)
                    ins.then_inc(*pe_did.tick("seg", c, q))

                def outputs(q):
                    if q == 0:
                        pe.wait_ge(*vec_did.at("xdt", c))
                    if q >= 2:
                        pe.wait_ge(*vec_did.at("y", c, q - 2))
                    if c == 1:
                        for i in range(2):
                            f = 2 * q + i
                            mm(k.ps[:, 2 + q % 2, i * P:i * P + n], flat(HT)[:, f * P:(f + 1) * P], XBC[:, 20 + q // 2, tok],
                               start=True, stop=True)
                    pe.wait_ge(*pool_did.at("m", c, q))
                    for i in range(4):
                        r = slice(64 * (i % 2), 64 * (i % 2) + 64)
                        ins = mm(k.ps[r, q % 2, (i // 2) * P:(i // 2) * P + n], XDT[0:n, 4 * q + i, :], SEG[q % 2][0:n, i, 0:n],
                                 start=True, stop=True)
                    ins.then_inc(*pe_did.tick("y", c, q))

                for q in range(9):
                    if q < 8:
                        seg(q)
                    if q:
                        outputs(q - 1)
                if c < 2:
                    pe.wait_ge(*pool_did.at("xdw", c))
                    pe.wait_ge(*act_did.at("bt", c))
                    pe.wait_ge(*vec_did.at("seg", c, 7))
                    for g in range(4):
                        ins = mm(k.bank(4 + g), BT[0:n, g, :], flat(XDW)[0:n, 512 * g:512 * (g + 1)], start=True, stop=True)
                    ins.then_inc(*pe_did.tick("h", c))
            pe.wait_ge(*pool_did.at("xdw", 2))
            pe.wait_ge(*act_did.at("bt", 2))
            pe.wait_ge(*vec_did.at("y", 2, 7))
            pe.wait_ge(*vec_did.at("cb", 2))
            for b in range(NB):
                cols = slice(TP + TS * b, TP + TS * b + TS)
                pe.wait_ge(state_in[b % 2], 16 * (b // 2 + 1))
                for f in range(MT):
                    ins = mm(k.ps[:, 4 + f // 8, (f % 8) * 64 + TS * b:(f % 8) * 64 + TS * b + TS], flat(HB[b % 2])[:, f * P:(f + 1) * P],
                             XBC[:, 20 + f // 4, cols], start=True, stop=True)
                ins.then_inc(*pe_did.tick("ys", b))
                pe.wait_ge(*vec_did.at("bm", b))
                if b:
                    pe.wait_ge(*vec_did.at("HB", b - 1))
                for g in range(4):
                    ins = mm(k.bank(g), BM[b % 2][0:64, g, :], flat(XDW)[0:64, 512 * g:512 * (g + 1)], start=True, stop=True)
                ins.then_inc(*pe_did.tick("hb", b))

        @block.scalar
        def _(act):
            s = nc.scalar
            for c in range(3):
                _, n = span[c]
                act.wait_ge(*pe_did.at("bt", c))
                s.activation(flat(BT)[0:n, :], k.bank(4)[0:n, :], ACT.Copy).then_inc(*act_did.tick("bt", c))
                for q in range(8):
                    act.wait_ge(*vec_did.at("seg", c, q))
                    s.activation(SEG[q % 2][0:n, :, 0:n], SEG[q % 2][0:n, :, 0:n], ACT.Exp).then_inc(*act_did.tick("e", c, q))

        @block.gpsimd
        def _(pool):
            g_ = nc.gpsimd
            for c in range(3):
                _, n = span[c]
                pool.wait_ge(*vec_did.at("xdt", c))
                g_.tensor_tensor(XDW[0:n], XDT[0:n], bc(TM[0:n, 6 + c, :], 64), ALU.mult).then_inc(*pool_did.tick("xdw", c))
                pool.wait_ge(*vec_did.at("cb", c))
                for q in range(8):
                    pool.wait_ge(*act_did.at("e", c, q))
                    m = SEG[q % 2][0:n, :, 0:n]
                    g_.tensor_tensor(m, m, bcm(CB[0:n, q // 2, 0:n], 4), ALU.mult).then_inc(*pool_did.tick("m", c, q))
            for b in range(NB):
                pool.wait_ge(*pe_did.at("ys", b))
                g_.tensor_tensor(HB[b % 2], HB[b % 2], bc(EE[:, 2 + b, :], 64), ALU.mult).then_inc(*pool_did.tick("hb", b))

        @block.vector
        def _(vec):
            v = nc.vector
            for c in range(3):
                t0, n = span[c]
                vec.wait_ge(*pe_did.at("xt", c))
                if c:
                    vec.wait_ge(*pe_did.at("h", c - 1))
                v.tensor_tensor(XDT[0:n], k.ps[0:n, 0:4, :].rearrange("p a (h d) -> p (a h) d", d=64), bc(TM[0:n, c, :], 64), ALU.mult)\
                    .then_inc(*vec_did.tick("xdt", c))
                vec.wait_ge(*pe_did.at("cb", c))
                v.tensor_tensor(CB[0:n, :, 0:n], k.ps[0:n, 5, :].rearrange("p (g i) -> p g i", g=4)[:, :, 0:n],
                                bcm(k.const("tril_p" if c < 2 else "tril_s", slice(0, n)), 4), ALU.mult).then_inc(*vec_did.tick("cb", c))

                def seg(q):
                    vec.wait_ge(*pe_did.at("seg", c, q))
                    if q >= 2:
                        vec.wait_ge(*pe_did.at("y", c, q - 2))
                    for i in range(4):
                        ins = v.tensor_scalar(SEG[q % 2][0:n, i, 0:n], k.ps[0:n, 6 + q % 2, i * P:i * P + n],
                                              TM[0:n, 3 + c, 4 * q + i:4 * q + i + 1], 0.0, ALU.subtract, ALU.min)
                    ins.then_inc(*vec_did.tick("seg", c, q))

                def outputs(q):
                    vec.wait_ge(*pe_did.at("y", c, q))
                    tok = slice(t0, t0 + n)
                    if c == 1:
                        if q:
                            vec.wait_ge(*vec_did.at("y", c, q - 1))
                        v.tensor_tensor(YT, Y[:, 2 * q:2 * q + 2, tok], k.ps[:, 2 + q % 2, 0:256].rearrange("p (a b) -> p a b", a=2),
                                        ALU.mult).then_inc(*vec_did.tick("yt", q))
                        vec.wait_ge(*vec_did.at("yt", q))
                    for i in range(2):
                        f = 2 * q + i
                        dst = YI[:, f, :] if c == 2 else Y[:, f, tok]
                        ins = v.scalar_tensor_tensor(dst, XBC[:, f, tok], k.param("d_skip", f), k.ps[:, q % 2, i * P:i * P + n],
                                                     ALU.mult, ALU.add)
                    if c == 1:
                        ins.then_inc(*vec_did.tick("yd", q))
                        vec.wait_ge(*vec_did.at("yd", q))
                        ins = v.tensor_tensor(Y[:, 2 * q:2 * q + 2, tok], Y[:, 2 * q:2 * q + 2, tok], YT, ALU.add)
                    ins.then_inc(*vec_did.tick("y", c, q))

                for q in range(9):
                    if q < 8:
                        seg(q)
                    if q:
                        outputs(q - 1)
                if c < 2:
                    vec.wait_ge(*pe_did.at("h", c))
                    if c:
                        v.tensor_tensor(HT, HT, bc(EE[:, c, :], 64), ALU.mult).then_inc(*vec_did.tick("H0"))
                        vec.wait_ge(*vec_did.at("H0"))
                        v.tensor_tensor(flat(HT), flat(HT), flat(k.ps[:, 4:8, :]), ALU.add).then_inc(*vec_did.tick("HT", c))
                    else:
                        v.tensor_copy(flat(HT), flat(k.ps[:, 4:8, :])).then_inc(*vec_did.tick("HT", c))
            vec.wait_ge(*act_did.at("bt", 2))
            for b in range(NB):
                if b >= 2:
                    vec.wait_ge(*pe_did.at("hb", b - 2))
                v.tensor_scalar(flat(BM[b % 2])[0:64, :], flat(BT)[0:64, :], k.const("seq", slice(0, 64))[:, b:b + 1], None, ALU.mult)\
                    .then_inc(*vec_did.tick("bm", b))
                vec.wait_ge(*pe_did.at("hb", b))
                vec.wait_ge(*pool_did.at("hb", b))
                v.tensor_tensor(flat(HB[b % 2]), flat(HB[b % 2]), flat(k.ps[:, 0:4, :]), ALU.add).then_inc(*vec_did.tick("HB", b))
            ys = k.ps[:, 4:6, :].rearrange("p a (f t) -> p (a f) t", t=64)
            v.tensor_tensor(Y[:, :, TP:T], Y[:, :, TP:T], ys, ALU.mult).then_inc(*vec_did.tick("ysm"))
            vec.wait_ge(*vec_did.at("ysm"))
            v.tensor_tensor(Y[:, :, TP:T], Y[:, :, TP:T], YI, ALU.add).then_inc(*vec_did.tick("yfin"))


def stage_mamba_output(k):
    nc = k.nc
    act_did, pe_did, vec_did = k.tallies("act", "pe", "vec")
    p0 = k.panel
    k.panel += 8
    ZS, Y = k.at(MB["ZS"], MT, T), k.at(MB["Y"], MT, T)
    SQ, RS = k.at(MB["XBC"], MT, T), k.at(MB["REST"], 4, T)
    with nc.Block() as block:
        @block.sync
        def _(sp):
            k.load_panels(sp, pe_did, p0, 8)

        @block.vector
        def _(vec):
            v = nc.vector
            for g in range(4):
                fs = slice(4 * g, 4 * g + 4)
                v.tensor_tensor(Y[:, fs, :], Y[:, fs, :], ZS[:, fs, :], ALU.mult).then_inc(*vec_did.tick("z", g))
            for g in range(4):
                vec.wait_ge(*act_did.at("root", g))
                v.reciprocal(RS[:, g, :], RS[:, g, :]).then_inc(*vec_did.tick("rs", g))
                vec.wait_ge(*vec_did.at("rs", g))
                for f in range(4 * g, 4 * g + 4):
                    v.scalar_tensor_tensor(Y[:, f, :], Y[:, f, :], k.param("m_norm", f), RS[:, g, :], ALU.mult, ALU.mult)\
                        .then_inc(*vec_did.tick("n", f))
            out_project_vec(k, vec, pe_did, vec_did)

        @block.scalar
        def _(act):
            for g in range(4):
                fs = slice(4 * g, 4 * g + 4)
                act.wait_ge(*vec_did.at("z", g))
                nc.scalar.activation(SQ[:, fs, :], Y[:, fs, :], ACT.Square).then_inc(*act_did.tick("sq", g))
            for g in range(4):
                act.wait_ge(*pe_did.at("mean", g))
                nc.scalar.activation(RS[:, g, :], k.bank(4 + g, T), ACT.Sqrt, bias=k.eps(0)).then_inc(*act_did.tick("root", g))

        @block.tensor
        def _(pe):
            for g in range(4):
                pe.wait_ge(*act_did.at("sq", g))
                for i in range(4):
                    ins = nc.tensor.matmul(k.bank(4 + g, T), k.const("mean512"), SQ[:, 4 * g + i, :], start=i == 0, stop=i == 3)
                ins.then_inc(*pe_did.tick("mean", g))
            out_project_pe(k, pe, pe_did, vec_did, p0, lambda i: Y[:, i, :], MT, lambda e, i: e.wait_ge(*vec_did.at("n", i)))


def stage_store(k):
    nc = k.nc
    stored = k.sem("y_stored")
    with nc.Block() as block:
        @block.sync
        def _(sp):
            sp.dma_start(k.io["y"], k.hidden[:, :, :].rearrange("p a b -> p (a b)")).then_inc(stored, 16)
            sp.wait_ge(stored, 16)


INPUTS = {
    "x": (P, KT * T), "consts": CONSTS.shape, "params": (P, NPARAM), "panels": (PANELS, P, 16 * P),
    "shift": (2, P, KT * NB), "wkv": (2, P, KT * NB * CK), "w_uk": (P, 2048), "w_ukT": (P, 2048), "w_uv": (P, 2048),
    "pages": (POOL, P, 640), "conv_in": (P, 576), "ssm": (NB, P, 2048), "page_table": (1, NB * NPG),
}
OUTPUTS = {
    "y": (P, KT * T), "ckv": (P, 2 * T), "kpe": (32, T), "shift_out": (2, P, KT * 9), "wkv_prompt": (2, P, 512),
    "wkv_sample": (2, P, KT * NB * CK), "conv_out": (P, 648), "ssm_prompt": (P, 2048), "ssm_sample": (NB, P, 2048),
}


def build(nc, old):
    io = {}
    for name, shape in INPUTS.items():
        io[name] = nc.dram_tensor(f"in_{name}", list(shape), I32 if name == "page_table" else F32, kind="ExternalInput").ap()
    for name, shape in OUTPUTS.items():
        io[name] = nc.dram_tensor(f"out_{name}", list(shape), F32, kind="ExternalOutput").ap()
    with ExitStack() as ctx:
        k = Kit(nc, ctx, io, old)
        stage_load(k)
        for l in range(DEPTH):
            if l % 3 == 0:
                stage_rwkv_project(k, l, l // 3)
                stage_rwkv_prepare(k, l // 3)
                stage_rwkv_scan(k, l // 3)
                stage_rwkv_output(k, l // 3)
            elif l % 3 == 1:
                stage_mla_project(k, l)
                stage_mla_prompt(k)
                stage_mla_sample(k)
                stage_mla_output(k)
            else:
                stage_mamba_project(k, l)
                stage_mamba_decay(k)
                stage_mamba_scan(k)
                stage_mamba_output(k)
            stage_ffn(k, l)
        stage_store(k)
        assert k.panel == PANELS, (k.panel, PANELS)
    return k.new


def to_tiles(w):
    kk, m = -(-w.shape[0] // P) * P, -(-w.shape[1] // P) * P
    full = np.zeros((kk, m), np.float32)
    full[:w.shape[0], :w.shape[1]] = w
    return full.reshape(kk // P, P, m // P, P).transpose(0, 2, 1, 3)


def pack_panels(d):
    out = []

    def panel(tiles):
        tiles = list(tiles) + [np.zeros((P, P), np.float32)] * (16 - len(tiles))
        out.append(np.stack(tiles).transpose(1, 0, 2).reshape(P, 16 * P))

    def columns(w):
        t = to_tiles(w)
        per = 16 // t.shape[0]
        for m in range(0, t.shape[1], per):
            panel([t[i, mm] for mm in range(m, min(m + per, t.shape[1])) for i in range(t.shape[0])])

    def deep(w):
        t = to_tiles(w)
        for m in range(0, 8, 2):
            for q in range(4):
                panel([t[8 * q + i, m + mm] for mm in range(2) for i in range(8)])

    for l in range(DEPTH):
        if l % 3 == 0:
            j = l // 3
            for p in range(3):
                columns(d["rwkv_w_rkv"][j, p])
            g1, g2 = d["rwkv_g1"][j], d["rwkv_g2"][j]
            v1 = d["rwkv_v1"][j - 1] if j else np.zeros((C, 32), np.float32)
            v2 = d["rwkv_v2"][j - 1] if j else np.zeros((32, C), np.float32)
            wa = to_tiles(np.concatenate([d["rwkv_w1"][j], d["rwkv_a1"][j]], 1))
            ga = to_tiles(np.ascontiguousarray(g1[:, 0:P]))
            gb = to_tiles(np.concatenate([g1[:, P:160], v1], 1))
            wa2 = to_tiles(np.concatenate([d["rwkv_w2"][j], d["rwkv_a2"][j]], 0))
            ga2 = to_tiles(np.ascontiguousarray(g2[0:P]))
            gb2 = to_tiles(np.concatenate([g2[P:160], v2], 0))
            panel([wa[i, 0] for i in range(8)] + [ga[i, 0] for i in range(8)])
            panel([gb[i, 0] for i in range(8)] + [wa2[0, m] for m in range(8)])
            panel([ga2[0, m] for m in range(8)] + [gb2[0, m] for m in range(8)])
            columns(d["rwkv_w_o"][j])
        elif l % 3 == 1:
            w = d["mla_w_in"][0]
            columns(w[:, 0:512])
            columns(w[:, 512:768])
            columns(np.tile(w[:, 768:800], (1, 4)))
            uq = d["mla_w_uq"][0]
            columns(uq[:, :, 0:64].reshape(512, C))
            columns(uq[:, :, 64:96].reshape(512, 512))
            columns(d["mla_w_o"][0])
        else:
            columns(d["mamba_w_in"][0])
            columns(d["mamba_w_o"][0])
        columns(d["ffn_w1"][l])
        deep(d["ffn_w2"][l])
    assert len(out) == PANELS, (len(out), PANELS)
    return np.stack(out)


def feature_major(a):
    return a.T.reshape(-1, P, a.shape[0]).transpose(1, 0, 2)


def pack_params(d):
    out = np.zeros((P, NPARAM), np.float32)

    def put(name, a, i=0):
        a = np.asarray(a).reshape(-1, P).T
        c, _ = PARAM_COLS[name]
        out[:, c + i:c + i + a.shape[1]] = a

    for l in range(DEPTH):
        put(f"norm_mix{l}", d["norm_mix"][l])
        put(f"norm_ffn{l}", d["norm_ffn"][l])
    for j in range(2):
        put(f"mu{j}", d["rwkv_mu"][j])
        for n in ("w0", "a0", "k_k", "k_a", "r_k", "lnx_w", "lnx_b"):
            put(f"{n}{j}", d[f"rwkv_{n}"][j])
    put("v01", d["rwkv_v0"][0])
    put("q_norm", d["mla_q_norm"][0])
    put("kv_norm", d["mla_kv_norm"][0])
    put("qn", np.tile(d["mla_qn_norm"][0], 2))
    put("kn", np.tile(d["mla_kn_norm"][0], 2))
    put("qr", np.tile(d["mla_qr_norm"][0], 4))
    put("kr", np.tile(d["mla_kr_norm"][0], 4))
    put("conv_w", d["mamba_conv_w"][0])
    put("conv_b", d["mamba_conv_b"][0])
    for name in ("dt_bias", "a_log"):
        out[0:MH, PARAM_COLS[name][0]] = d[f"mamba_{name}"][0]
    put("d_skip", np.repeat(d["mamba_d"][0], 64))
    put("m_norm", d["mamba_norm"][0])
    return out


def kernel(**inputs):
    import concourse.bacc as bacc
    from concourse.bass_utils import run_bass_kernel_spmd

    d = {n: np.asarray(a) for n, a in inputs.items()}
    counts = build(bacc.Bacc("TRN2", target_bir_lowering=False, num_devices=1), None)
    nc = bacc.Bacc("TRN2", target_bir_lowering=False, num_devices=1)
    build(nc, counts)

    tokens = np.concatenate([d["x_prompt"].reshape(TP, C), d["x_sample"].reshape(NB * TS, C)], 0)
    ck, kp = d["cache_mla_ckv"][0], d["cache_mla_kpe"][0]
    ckT = ck.transpose(0, 2, 1).reshape(POOL, 2, P, PAGE).transpose(0, 2, 1, 3).reshape(POOL, P, 256)
    uk = d["mla_w_uk"][0].reshape(256, C)
    rows = lambda w: w.reshape(2, P, C).transpose(1, 0, 2).reshape(P, 2 * C)
    a = {
        "x": feature_major(tokens).reshape(P, -1),
        "consts": CONSTS,
        "params": pack_params(d),
        "panels": pack_panels(d),
        "shift": np.stack([feature_major(s).reshape(P, -1) for s in d["state_rwkv_shift"]]),
        "wkv": d["state_rwkv_wkv"].reshape(2, NB, KT, 2, CK, CK).transpose(0, 3, 5, 2, 1, 4).reshape(2, P, -1),
        "w_uk": rows(uk),
        "w_ukT": uk.T.reshape(KT, P, 256).transpose(1, 0, 2).reshape(P, -1),
        "w_uv": rows(d["mla_w_uv"][0].reshape(256, C)),
        "pages": np.concatenate([ck, ckT, np.tile(kp.transpose(0, 2, 1), (1, 4, 1))], 2),
        "conv_in": d["state_conv"][0].reshape(NB, 3, 24, P).transpose(3, 2, 0, 1).reshape(P, -1),
        "ssm": d["state_ssm"][0].transpose(0, 3, 1, 2).reshape(NB, P, -1),
        "page_table": d["page_table"].reshape(1, -1),
    }
    r = run_bass_kernel_spmd(nc, [{f"in_{n}": np.ascontiguousarray(v) for n, v in a.items()}], core_ids=[0]).results[0]
    r = {n[4:]: v for n, v in r.items()}

    token_major = lambda t, n: t.reshape(-1, n, T).transpose(2, 1, 0).reshape(T, -1)
    y = token_major(r["y"], KT)
    ckv = token_major(r["ckv"], 2)
    kpe = r["kpe"].T
    sh = r["shift_out"].reshape(2, P, KT, 9).transpose(0, 3, 2, 1).reshape(2, 9, C)
    wp = r["wkv_prompt"].reshape(2, 2, CK, KT, CK).transpose(0, 3, 1, 4, 2).reshape(2, 1, 16, CK, CK)
    ws = r["wkv_sample"].reshape(2, 2, CK, KT, NB, CK).transpose(0, 4, 3, 1, 5, 2).reshape(2, NB, 16, CK, CK)
    co = r["conv_out"].reshape(P, 24, 9, 3).transpose(2, 3, 1, 0).reshape(9, 3, 24 * P)
    sp = r["ssm_prompt"].reshape(P, MH, 64).transpose(1, 2, 0)
    ss = r["ssm_sample"].reshape(NB, P, MH, 64).transpose(0, 2, 3, 1)
    out = (y[:TP].reshape(1, TP, C), y[TP:].reshape(NB, TS, C),
           ckv[:TP].reshape(1, 1, TP, 256), kpe[:TP].reshape(1, 1, TP, 32),
           ckv[TP:].reshape(1, NB, TS, 256), kpe[TP:].reshape(1, NB, TS, 32),
           wp, sh[:, 0:1], ws, sh[:, 1:9],
           sp[None, None], co[0:1][None], ss[None], co[1:9][None])
    return tuple(np.ascontiguousarray(o) for o in out)
```

```python
from contextlib import ExitStack

import numpy as np
import concourse.bass as bass
from concourse import mybir
from concourse.alu_op_type import AluOpType as ALU

F32 = mybir.dt.float32
F32R = mybir.dt.float32r
I32 = mybir.dt.int32
ACT = mybir.ActivationFunctionType
AX = mybir.AxisListType.X

P = 128
C = 1024
KT = C // P
TP, NB, TS = 256, 8, 8
T = TP + NB * TS
DEPTH = 4
PAST, PAGE, POOL = 1024, 128, 80
NPG = PAST // PAGE
CK = 64
NCK = T // CK
HID = 4 * C
MLA_SCALE = 96.0 ** -0.5
EPS = 1e-6
DECAY = float(np.exp(-0.5))
NEG = -1.0e30
RING = 3
SPLIT = 3
ARENA = 35400
W = KT * T

CONST_COLS = {}


def make_constants():
    out, col = [], 0

    def add(name, a):
        nonlocal col
        a = np.asarray(a, np.float32)
        full = np.zeros((P, a.shape[1]), np.float32)
        full[:a.shape[0]] = a
        CONST_COLS[name] = (col, a.shape[1])
        out.append(full)
        col += a.shape[1]

    p = np.arange(P)
    add("ident", np.eye(P))
    add("ones", np.ones((P, P)))
    for n in (1024, 512, 256):
        add(f"mean{n}", np.full((P, P), 1.0 / n))
    same = lambda w: (p[:, None] // w == p[None] // w).astype(np.float32)
    add("mean64", same(64) / 64)
    add("mean32", same(32) / 32)
    perm = np.zeros((P, P))
    for i in range(P):
        perm[i + 16 if i % 32 < 16 else i - 16, i] = -1.0 if i % 32 < 16 else 1.0
    add("perm", perm)
    half = 16
    inv = (np.float32(10000.0) ** (-np.arange(half, dtype=np.float32) / np.float32(half))).astype(np.float32)
    pos = np.concatenate([np.arange(TP), np.tile(PAST + np.arange(TS), NB)]).astype(np.float32)
    ang = (pos[None] * inv[p % 16][:, None]).astype(np.float32)
    add("cos", np.cos(ang.astype(np.float64)))
    add("sin", np.sin(ang.astype(np.float64)))
    s, t = p[:, None] % 64, np.arange(64)[None]
    add("att_p", np.concatenate([s < t, s <= t], 1))
    b8 = s // 8 == t // 8
    add("att_s", np.concatenate([(s < t) & b8, (s <= t) & b8], 1))
    r = s
    blk = lambda w: r // w == t // w
    add("dA_p", (t < r) & blk(16))
    add("dG_p", (r < t) & blk(16))
    add("eA", (t < r) & blk(32) & ~blk(16))
    add("fA", (t < r) & ~blk(32))
    add("dA_s", (t < r) & b8)
    add("dG_s", (r < t) & b8)
    add("eye64", r == t)
    add("seq", (s // 8 == np.arange(8)[None]))
    reset = np.ones(T)
    reset[0:TP:CK] = 0
    reset[TP::TS] = 0
    add("reset", np.tile(reset, (P, 1)))
    reset = np.ones(T)
    reset[0:TP:P] = 0
    reset[TP::TS] = 0
    add("reset_m", np.tile(reset, (32, 1)))
    add("causal", np.where(p[None] <= p[:, None], 0.0, NEG))
    add("tril_p", (p[:, None] <= p[None]))
    k, q = np.arange(64)[:, None], np.arange(64)[None]
    add("tril_s", (k <= q) & (k // 8 == q // 8))
    add("eps", np.tile(np.float32([EPS, 64e-5, 64 * EPS]), (P, 1)))
    add("new8", np.where(np.arange(8)[:, None] <= np.arange(8)[None], 0.0, NEG))
    return np.concatenate(out, 1)


CONSTS = make_constants()

PARAM_COLS = {}


def param_layout():
    col = 0

    def add(name, n):
        nonlocal col
        PARAM_COLS[name] = (col, n)
        col += n

    for l in range(DEPTH):
        add(f"norm_mix{l}", KT)
        add(f"norm_ffn{l}", KT)
    for j in range(2):
        add(f"mu{j}", 6 * KT)
        for n in ("w0", "a0", "v0", "k_k", "k_a", "r_k", "lnx_w", "lnx_b"):
            add(f"{n}{j}", KT)
    add("q_norm", 4)
    add("kv_norm", 2)
    add("qn", 1)
    add("kn", 1)
    add("qr", 1)
    add("kr", 1)
    add("conv_w", 4 * 24)
    add("conv_b", 24)
    add("dt_bias", 1)
    add("a_log", 1)
    add("d_skip", 16)
    add("m_norm", 16)
    return col


NPARAM = param_layout()

PANELS_FFN = 32
PANELS_RWKV = 19
PANELS_MLA = 2 + 1 + 1 + 2 + 1 + 4
PANELS_MAMBA = 8 + 12 + 1 + 8
PANELS = 4 * PANELS_FFN + 2 * PANELS_RWKV + PANELS_MLA + PANELS_MAMBA


class Tally:

    def __init__(self, sem, key, old, new):
        self.sem, self.key, self.old, self.new, self.n = sem, key, old, new, 0

    def tick(self, *name, also=()):
        self.n += 1
        self.new[(self.key, name)] = self.n
        for other in also:
            self.new[(self.key, other)] = self.n
        return self.sem, 1

    def at(self, *name):
        if self.old is None:
            return self.sem, 1
        return self.sem, self.old[(self.key, name)]


class Kit:

    def __init__(self, nc, ctx, io, old):
        self.nc, self.ctx, self.io, self.old, self.new = nc, ctx, io, old, {}
        sb = lambda name, shape, dt=F32: ctx.enter_context(nc.sbuf_tensor(name, shape, dt))
        self.consts = sb("consts", [P, CONSTS.shape[1]])
        self.params = sb("params", [P, NPARAM])
        self.hidden = sb("residual", [P, KT, T])
        self.normed = sb("normed", [P, KT * T])
        self.v_first = sb("v_first", [P, KT, T])
        self.ring = sb("weight_ring", [P, RING, 16, P])
        self.table = sb("page_table", [1, NB * NPG], I32)
        self.arena_size = ARENA
        self.arena = sb("arena", [P, ARENA])
        self.arena_address = nc.sbuf_base - 4 * ARENA
        self.views = 0
        self.w_hi = self.rounded(ARENA - 2 * SPLIT * C, SPLIT, 8, P)
        self.w_lo = self.rounded(ARENA - SPLIT * C, SPLIT, 8, P)
        self.ps = ctx.enter_context(nc.psum_tensor("banks", [P, 8, 512], F32))
        self.loaded = [ctx.enter_context(nc.semaphore(f"panel_landed{i}")) for i in range(RING)]
        self.issued = 0
        self.panel = 0
        self.stage = 0

    def const(self, name, rows=slice(0, P)):
        c, n = CONST_COLS[name]
        return self.consts[rows, c:c + n]

    def eps(self, i, rows=slice(0, P)):
        return self.const("eps", rows)[:, i:i + 1]

    def param(self, name, i=0, n=1):
        c, _ = PARAM_COLS[name]
        return self.params[:, c + i:c + i + n]

    def tallies(self, *names):
        self.stage += 1
        return [Tally(self.ctx.enter_context(self.nc.semaphore(f"{n}{self.stage}")), (n, self.stage), self.old, self.new)
                for n in names]

    def sem(self, name):
        self.stage += 1
        return self.ctx.enter_context(self.nc.semaphore(f"{name}{self.stage}"))

    def at(self, offset, *shape, rows=P):
        n = int(np.prod(shape))
        assert offset + n <= self.arena_size, (offset, shape)
        a = self.arena[0:rows, offset:offset + n]
        if len(shape) == 2:
            a = a.rearrange("p (a b) -> p a b", a=shape[0])
        elif len(shape) == 3:
            a = a.rearrange("p (a b c) -> p a b c", a=shape[0], b=shape[1])
        return a

    def rounded(self, offset, *shape):
        n = int(np.prod(shape))
        assert offset + n <= self.arena_size and offset % 8 == 0, (offset, shape)
        self.views += 1
        a = self.nc.alloc_sbuf_tensor_at(f"rounded{self.views}", [P, n], F32R, offset=self.arena_address + 4 * offset)[:, :]
        if len(shape) == 2:
            a = a.rearrange("p (a b) -> p a b", a=shape[0])
        elif len(shape) == 3:
            a = a.rearrange("p (a b c) -> p a b c", a=shape[0], b=shape[1])
        return a

    def bank(self, i, n=512):
        return self.ps[:, i, 0:n]

    def load_panels(self, sp, reader, first, count):
        for p in range(self.issued, min(first + count + RING, PANELS)):
            if p - RING >= first:
                sp.wait_ge(*reader.at("panel", p - RING))
            sp.dma_start(self.ring[:, p % RING, :, :].rearrange("p a b -> p (a b)"),
                         self.io["panels"][p]).then_inc(self.loaded[p % RING], 16)
            self.issued = p + 1

    def wait_panel(self, pe, p):
        pe.wait_ge(self.loaded[p % RING], 16 * (p // RING + 1))

    def tile(self, p, i):
        return self.ring[:, p % RING, i, :]


def bc(ap, n):
    return ap.unsqueeze(2).to_broadcast([ap.shape[0], ap.shape[1], n])


def bcm(ap, n):
    return ap.unsqueeze(1).to_broadcast([ap.shape[0], n, ap.shape[1]])


class Split:

    def __init__(self, k, parts, act_did, pe_did, vec_did):
        self.k, self.parts, self.act_did, self.pe_did, self.vec_did = k, parts, act_did, pe_did, vec_did

    def raw(self, i):
        p, half = self.parts[i]
        return self.k.ring[:, p % RING, 8 * half:8 * half + 8, :]

    def hi(self, act, i):
        if i >= len(self.parts):
            return
        if i == 0 or self.parts[i][0] != self.parts[i - 1][0]:
            self.k.wait_panel(act, self.parts[i][0])
        if i >= SPLIT:
            act.wait_ge(*self.pe_did.at("part", i - SPLIT))
        self.k.nc.scalar.activation(self.k.w_hi[:, i % SPLIT], self.raw(i), ACT.Copy).then_inc(*self.act_did.tick("w_hi", i))

    def lo(self, vec, i):
        if i >= len(self.parts):
            return
        vec.wait_ge(*self.act_did.at("w_hi", i))
        last = i + 1 == len(self.parts) or self.parts[i + 1][0] != self.parts[i][0]
        self.k.nc.vector.tensor_tensor(self.k.w_lo[:, i % SPLIT], self.raw(i), self.k.w_hi[:, i % SPLIT].bitcast(F32), ALU.subtract)\
            .then_inc(*self.vec_did.tick("w_lo", i, also=[("panel", self.parts[i][0])] if last else []))

    def ready(self, pe, i):
        pe.wait_ge(*self.vec_did.at("w_lo", i))

    def product(self, out, i, t, x_hi, x_lo, start, stop):
        mm, k = self.k.nc.tensor.matmul, self.k
        hi, lo = k.w_hi[:, i % SPLIT, t, :], k.w_lo[:, i % SPLIT, t, :]
        mm(out, hi, x_hi, start=start, stop=False)
        mm(out, hi, x_lo, start=False, stop=False)
        return mm(out, lo, x_hi, start=False, stop=stop)


def round_act(k, act, act_did, vec_did, src, hi, n, name, step="xh"):
    for i in range(n):
        act.wait_ge(*vec_did.at(name, i))
        k.nc.scalar.activation(hi[:, i, :], src(i), ACT.Copy).then_inc(*act_did.tick(step, i))


def rest_vec(k, vec, act_did, vec_did, src, hi, lo, n, step="xl", of="xh"):
    for i in range(n):
        vec.wait_ge(*act_did.at(of, i))
        k.nc.vector.tensor_tensor(lo[:, i, :], src(i), hi[:, i, :].bitcast(F32), ALU.subtract).then_inc(*vec_did.tick(step, i))


def norm_act(k, act, act_did, pe_did, sq, rs):
    k.nc.scalar.activation(sq, k.hidden[:, :, :].rearrange("p a b -> p (a b)"), ACT.Square).then_inc(*act_did.tick("sq"))
    act.wait_ge(*pe_did.at("mean"))
    k.nc.scalar.activation(rs, k.bank(7, T), ACT.Sqrt, bias=k.eps(0)).then_inc(*act_did.tick("root"))


def norm_pe(k, pe, act_did, pe_did, sq):
    pe.wait_ge(*act_did.at("sq"))
    for i in range(KT):
        ins = k.nc.tensor.matmul(k.bank(7, T), k.const("mean1024"), sq[:, i * T:(i + 1) * T], start=i == 0, stop=i == KT - 1)
    ins.then_inc(*pe_did.tick("mean"))


def norm_vec(k, vec, act_did, vec_did, rs, gain):
    vec.wait_ge(*act_did.at("root"))
    k.nc.vector.reciprocal(rs, rs).then_inc(*vec_did.tick("rs"))
    vec.wait_ge(*vec_did.at("rs"))
    for i in range(KT):
        k.nc.vector.scalar_tensor_tensor(k.normed[:, i * T:(i + 1) * T], k.hidden[:, i, :], k.param(gain, i), rs,
                                         ALU.mult, ALU.mult).then_inc(*vec_did.tick("x", i))


def stage_load(k):
    nc, io = k.nc, k.io
    first_loads = k.sem("first_loads")
    with nc.Block() as block:
        @block.gpsimd
        def _(pool):
            nc.gpsimd.dma_start(k.hidden[:, :, :].rearrange("p a b -> p (a b)"), io["x"]).then_inc(first_loads, 16)
            nc.gpsimd.dma_start(k.consts[:, :], io["consts"]).then_inc(first_loads, 16)
            nc.gpsimd.dma_start(k.params[:, :], io["params"]).then_inc(first_loads, 16)
            nc.gpsimd.dma_start(k.table[:, :], io["page_table"]).then_inc(first_loads, 16)
            pool.wait_ge(first_loads, 64)

        @block.sync
        def _(sp):
            k.load_panels(sp, None, 0, 0)


def stage_ffn(k, l):
    nc = k.nc
    act_did, pe_did, vec_did = k.tallies("act", "pe", "vec")
    p0 = k.panel
    k.panel += PANELS_FFN
    xh, xl = k.rounded(0, KT, T), k.rounded(W, KT, T)
    hh, hl = k.rounded(2 * W, 32, T), k.rounded(2 * W + 32 * T, 32, T)
    act_ring = k.at(2 * W + 64 * T, 4, T)
    sq = k.arena[:, 2 * W:3 * W]
    rs = k.arena[:, 3 * W:3 * W + T]
    x = lambda i: k.normed[:, i * T:(i + 1) * T]
    split = Split(k, [(p0 + i // 2, i % 2) for i in range(2 * PANELS_FFN)], act_did, pe_did, vec_did)
    column_end = lambda i: i >= 32 and (i - 32) % 8 >= 6
    column = lambda i: 2 * ((i - 32) // 8) + i % 2

    with nc.Block() as block:
        @block.sync
        def _(sp):
            k.load_panels(sp, vec_did, p0, PANELS_FFN)

        @block.tensor
        def _(pe):
            norm_pe(k, pe, act_did, pe_did, sq)
            for m in range(32):
                split.ready(pe, m)
                if m >= 4:
                    pe.wait_ge(*act_did.at("relu", m - 4))
                for i in range(KT):
                    if m == 0:
                        pe.wait_ge(*vec_did.at("xl", i))
                    ins = split.product(k.bank(m % 4, T), m, i, xh[:, i, :], xl[:, i, :], i == 0, i == KT - 1)
                ins.then_inc(*pe_did.tick("part", m))
            for i in range(32, 64):
                m, q = column(i), (i - 32) % 8 // 2
                split.ready(pe, i)
                if i < 36:
                    pe.wait_ge(*act_did.at("relu", 28 + i - 32))
                elif q == 0 and m >= 4:
                    pe.wait_ge(*vec_did.at("res", m - 4))
                for t in range(8):
                    if m == 0:
                        pe.wait_ge(*vec_did.at("hl", 8 * q + t))
                    ins = split.product(k.bank(m % 4, T), i, t, hh[:, 8 * q + t, :], hl[:, 8 * q + t, :],
                                        q == 0 and t == 0, q == 3 and t == 7)
                ins.then_inc(*pe_did.tick("part", i))

        @block.scalar
        def _(act):
            s = nc.scalar
            s.activation(sq, k.hidden[:, :, :].rearrange("p a b -> p (a b)"), ACT.Square).then_inc(*act_did.tick("sq"))
            for i in range(SPLIT):
                split.hi(act, i)
            act.wait_ge(*pe_did.at("mean"))
            s.activation(rs, k.bank(7, T), ACT.Sqrt, bias=k.eps(0)).then_inc(*act_did.tick("root"))
            round_act(k, act, act_did, vec_did, x, xh, KT, "x")

            def round_hidden(m):
                act.wait_ge(*vec_did.at("hid", m))
                s.activation(hh[:, m, :], act_ring[:, m % 4, :], ACT.Copy).then_inc(*act_did.tick("hh", m))

            for m in range(32):
                act.wait_ge(*pe_did.at("part", m))
                if m >= 4:
                    act.wait_ge(*vec_did.at("hl", m - 4))
                s.activation(act_ring[:, m % 4, :], k.bank(m % 4, T), ACT.Relu).then_inc(*act_did.tick("relu", m))
                if m:
                    round_hidden(m - 1)
                split.hi(act, m + SPLIT)
            round_hidden(31)
            for i in range(32 + SPLIT, 64):
                split.hi(act, i)

        @block.vector
        def _(vec):
            v = nc.vector
            for i in range(SPLIT):
                split.lo(vec, i)
            norm_vec(k, vec, act_did, vec_did, rs, f"norm_ffn{l}")
            rest_vec(k, vec, act_did, vec_did, x, xh, xl, KT)

            def rest_hidden(m):
                vec.wait_ge(*act_did.at("hh", m))
                v.tensor_tensor(hl[:, m, :], act_ring[:, m % 4, :], hh[:, m, :].bitcast(F32), ALU.subtract)\
                    .then_inc(*vec_did.tick("hl", m))

            for m in range(32):
                vec.wait_ge(*act_did.at("relu", m))
                v.tensor_tensor(act_ring[:, m % 4, :], act_ring[:, m % 4, :], act_ring[:, m % 4, :], ALU.mult)\
                    .then_inc(*vec_did.tick("hid", m))
                if m:
                    rest_hidden(m - 1)
                split.lo(vec, m + SPLIT)
            rest_hidden(31)
            for i in range(32, 64):
                split.lo(vec, i + SPLIT)
                if column_end(i):
                    m = column(i)
                    vec.wait_ge(*pe_did.at("part", i))
                    v.tensor_tensor(k.hidden[:, m, :], k.hidden[:, m, :], k.bank(m % 4, T), ALU.add)\
                        .then_inc(*vec_did.tick("res", m))


def out_project_pe(k, pe, pe_did, vec_did, p0, src, nk, ready):
    per = 16 // nk
    for m in range(KT):
        p = p0 + m // per
        if m % per == 0:
            k.wait_panel(pe, p)
        if m >= 4:
            pe.wait_ge(*vec_did.at("res", m - 4))
        for i in range(nk):
            if m == 0:
                ready(pe, i)
            ins = k.nc.tensor.matmul(k.bank(m % 4, T), k.tile(p, (m % per) * nk + i), src(i), start=i == 0, stop=i == nk - 1)
        ins.then_inc(*pe_did.tick("out", m, also=[("panel", p)]))


def out_project_vec(k, vec, pe_did, vec_did):
    for m in range(KT):
        vec.wait_ge(*pe_did.at("out", m))
        k.nc.vector.tensor_tensor(k.hidden[:, m, :], k.hidden[:, m, :], k.bank(m % 4, T), ALU.add)\
            .then_inc(*vec_did.tick("res", m))


RW = dict(R=0, K=W, V=2 * W, LW=3 * W, A=4 * W, G=5 * W, DX=6 * W, XM=7 * W, SG=9 * W, LH=10 * W,
          AR=6 * W, BK=8 * W, TMP=10 * W)


def stage_rwkv_project(k, l, j):
    nc, io = k.nc, k.io
    act_did, pe_did, vec_did = k.tallies("act", "pe", "vec")
    moved = k.sem("shift_moved")
    stored = k.sem("shift_stored")
    p0 = k.panel
    used = PANELS_RWKV - 4
    k.panel += used
    res = j > 0
    arr = {n: k.at(RW[n], KT, T) for n in ("R", "K", "V", "LW", "A", "G", "DX", "SG")}
    arr["XM"] = k.at(RW["XM"], 2 * KT, T)
    hw, hg, hb = (k.arena[:, RW["LH"] + i * T:RW["LH"] + (i + 1) * T] for i in range(3))
    rs = k.arena[:, RW["LH"] + 3 * T:RW["LH"] + 4 * T]
    small = RW["LH"] + 4 * T
    shift_in = k.at(small, KT, NB)
    last = k.at(small + 64, KT, 9)
    sq = k.arena[:, RW["G"]:RW["G"] + W]
    x = k.normed[:, :].rearrange("p (a b) -> p a b", a=KT)
    dx, xm = arr["DX"], arr["XM"]
    la, lb, lc = p0 + 12, p0 + 13, p0 + 14

    plan = [("R", m) for m in range(KT)] + [("K", m) for m in range(KT)] + [("V", m) for m in range(KT)]
    if res:
        plan += [("hv", 0)] + [("SG", m) for m in range(KT)]
    plan += [("hw", 0)] + [("LW", m) for m in range(KT)]
    plan += [("ha", 0)] + [("A", m) for m in range(KT)]
    plan += [("hg", 0), ("hb", 0)] + [("G", m) for m in range(KT)]
    mix_of = {"R": 0, "K": 1, "V": 2, "hv": 2, "hw": 3, "ha": 4, "hg": 5, "hb": 5}
    last_of_mix = {mix_of[what]: n for n, (what, _) in enumerate(plan) if what in mix_of}

    with nc.Block() as block:
        @block.sync
        def _(sp):
            sp.dma_start(shift_in.rearrange("p a b -> p (a b)"), io["shift"][j]).then_inc(moved, 16)
            k.load_panels(sp, pe_did, p0, used)

        @block.gpsimd
        def _(pool):
            pool.wait_ge(*vec_did.at("last"))
            nc.gpsimd.dma_start(io["shift_out"][j], last.rearrange("p a b -> p (a b)")).then_inc(stored, 16)
            pool.wait_ge(stored, 16)

        @block.vector
        def _(vec):
            norm_vec(k, vec, act_did, vec_did, rs, f"norm_mix{l}")
            vec.wait_ge(*vec_did.at("x", KT - 1))
            nc.vector.tensor_copy(last[:, :, 0:1], x[:, :, TP - 1:TP])
            nc.vector.tensor_copy(last[:, :, 1:9], x[:, :, TP + TS - 1::TS]).then_inc(*vec_did.tick("last"))
            nc.vector.tensor_tensor(dx[:, :, 1:TP], x[:, :, 0:TP - 1], x[:, :, 1:TP], ALU.subtract)
            nc.vector.tensor_scalar(dx[:, :, 0:1], x[:, :, 0:1], -1.0, None, ALU.mult)
            nc.vector.tensor_tensor(dx[:, :, TP + 1:T], x[:, :, TP:T - 1], x[:, :, TP + 1:T], ALU.subtract)\
                .then_inc(*vec_did.tick("dx0"))
            vec.wait_ge(moved, 16)
            vec.wait_ge(*vec_did.at("dx0"))
            nc.vector.tensor_tensor(dx[:, :, TP::TS], shift_in, x[:, :, TP::TS], ALU.subtract).then_inc(*vec_did.tick("dx"))
            vec.wait_ge(*vec_did.at("dx"))
            for p in range(6):
                if p >= 2:
                    vec.wait_ge(*pe_did.at("tile", last_of_mix[p - 2]))
                for i in range(KT):
                    nc.vector.scalar_tensor_tensor(xm[:, (p % 2) * KT + i, :], dx[:, i, :], k.param(f"mu{j}", p * KT + i),
                                                   x[:, i, :], ALU.mult, ALU.add).then_inc(*vec_did.tick("mix", p, i))
            if res:
                vec.wait_ge(*act_did.at("tile", plan.index(("SG", KT - 1))))
                vec.wait_ge(*vec_did.at("mix", 5, KT - 1))
                nc.vector.tensor_tensor(dx, k.v_first[:, :, :], arr["V"], ALU.subtract).then_inc(*vec_did.tick("vd"))
                vec.wait_ge(*vec_did.at("vd"))
                nc.vector.tensor_tensor(dx, dx, arr["SG"], ALU.mult).then_inc(*vec_did.tick("vg"))
                vec.wait_ge(*vec_did.at("vg"))
                nc.vector.tensor_tensor(arr["V"], arr["V"], dx, ALU.add).then_inc(*vec_did.tick("v"))
            else:
                vec.wait_ge(*act_did.at("tile", plan.index(("V", KT - 1))))
                nc.vector.tensor_copy(k.v_first[:, :, :], arr["V"]).then_inc(*vec_did.tick("v"))

        @block.tensor
        def _(pe):
            norm_pe(k, pe, act_did, pe_did, sq)
            for n, (what, m) in enumerate(plan):
                if n >= 4:
                    pe.wait_ge(*act_did.at("tile", n - 4))
                out = k.bank(n % 4, T)
                if what in mix_of:
                    rhs = lambda i, b=(mix_of[what] % 2) * KT: xm[:, b + i, :]
                    for i in range(KT):
                        pe.wait_ge(*vec_did.at("mix", mix_of[what], i))
                        if what in "RKV":
                            p = p0 + 4 * "RKV".index(what) + m // 2
                            if i == 0 and m % 2 == 0:
                                k.wait_panel(pe, p)
                            o, lhs = out, k.tile(p, (m % 2) * 8 + i)
                        elif what == "hv":
                            if i == 0:
                                k.wait_panel(pe, lb)
                            o, lhs = out[32:64, :], k.tile(lb, i)[:, 32:64]
                        elif what == "hw":
                            if i == 0:
                                k.wait_panel(pe, la)
                            o, lhs = out[0:64, :], k.tile(la, i)[:, 0:64]
                        elif what == "ha":
                            o, lhs = out[64:128, :], k.tile(la, i)[:, 64:128]
                        elif what == "hg":
                            o, lhs = out, k.tile(la, 8 + i)
                        else:
                            o, lhs = out[0:32, :], k.tile(lb, i)[:, 0:32]
                        ins = nc.tensor.matmul(o, lhs, rhs(i), start=i == 0, stop=i == KT - 1)
                    also = [("panel", p0 + 4 * "RKV".index(what) + m // 2)] if what in "RKV" else []
                    ins.then_inc(*pe_did.tick("tile", n, also=also))
                    continue
                pe.wait_ge(*act_did.at("tile", plan.index(({"SG": "hv", "LW": "hw", "A": "ha", "G": "hb"}[what], 0))))
                k.wait_panel(pe, lb)
                k.wait_panel(pe, lc)
                if what == "SG":
                    ins = nc.tensor.matmul(out, k.tile(lc, 8 + m)[32:64, :], hb[32:64, :], start=True, stop=True)
                elif what == "LW":
                    ins = nc.tensor.matmul(out, k.tile(lb, 8 + m)[0:64, :], hw[0:64, :], start=True, stop=True)
                elif what == "A":
                    ins = nc.tensor.matmul(out, k.tile(lb, 8 + m)[64:128, :], hw[64:128, :], start=True, stop=True)
                else:
                    nc.tensor.matmul(out, k.tile(lc, m), hg, start=True, stop=False)
                    ins = nc.tensor.matmul(out, k.tile(lc, 8 + m)[0:32, :], hb[0:32, :], start=False, stop=True)
                ins.then_inc(*pe_did.tick("tile", n))
            for p in (la, lb, lc):
                k.new[(pe_did.key, ("panel", p))] = pe_did.n

        @block.scalar
        def _(act):
            norm_act(k, act, act_did, pe_did, sq, rs)
            for n, (what, m) in enumerate(plan):
                act.wait_ge(*pe_did.at("tile", n))
                b = k.bank(n % 4, T)
                if what in ("R", "K", "V", "G"):
                    ins = nc.scalar.activation(arr[what][:, m, :], b, ACT.Copy)
                elif what == "hv":
                    ins = nc.scalar.activation(hb[32:64, :], b[32:64, :], ACT.Copy)
                elif what == "hw":
                    ins = nc.scalar.activation(hw[0:64, :], b[0:64, :], ACT.Tanh)
                elif what == "ha":
                    ins = nc.scalar.activation(hw[64:128, :], b[64:128, :], ACT.Copy)
                elif what == "hg":
                    ins = nc.scalar.activation(hg, b, ACT.Sigmoid)
                elif what == "hb":
                    ins = nc.scalar.activation(hb[0:32, :], b[0:32, :], ACT.Sigmoid)
                else:
                    bias = {"SG": "v0", "LW": "w0", "A": "a0"}[what]
                    ins = nc.scalar.activation(arr[what][:, m, :], b, ACT.Sigmoid, bias=k.param(f"{bias}{j}", m))
                ins.then_inc(*act_did.tick("tile", n))


def stage_rwkv_prepare(k, j):
    nc = k.nc
    act_did, pe_did, vec_did, pool_did = k.tallies("act", "pe", "vec", "pool")
    R, K, V, LW, A = (k.arena[:, RW[n]:RW[n] + W] for n in ("R", "K", "V", "LW", "A"))
    T1, T2, T3 = (k.arena[:, RW["TMP"] + i * W:RW["TMP"] + (i + 1) * W] for i in range(3))
    T4 = k.normed[:, :]
    AR = k.at(RW["AR"], KT * NCK, P)
    BK = k.at(RW["BK"], KT * NCK, P)
    g3 = lambda a: a.rearrange("p (a b) -> p a b", a=KT)
    c3 = lambda a: a.rearrange("p (a b) -> p a b", b=CK)
    par = lambda n: bc(k.param(f"{n}{j}", 0, KT), T)
    pc = k.at(k.arena_size - 96, KT, 12)
    allbanks = k.ps[:, :, 0:T]

    with nc.Block() as block:
        @block.vector
        def _(vec):
            v = nc.vector
            v.tensor_tensor(g3(T1), g3(K), par("k_k"), ALU.mult).then_inc(*vec_did.tick("kk0"))
            for i in range(KT):
                ins = v.tensor_tensor_scan(T3[:, i * T:(i + 1) * T], k.const("reset"), LW[:, i * T:(i + 1) * T], 0.0,
                                           ALU.mult, ALU.add)
            ins.then_inc(*vec_did.tick("cum"))
            vec.wait_ge(*pe_did.at("norm", KT - 1))
            v.tensor_scalar(g3(T2), allbanks, 1e-24 / 64, None, ALU.max).then_inc(*vec_did.tick("clamp"))
            vec.wait_ge(*act_did.at("root"))
            v.reciprocal(T2, T2).then_inc(*vec_did.tick("inv"))
            vec.wait_ge(*vec_did.at("inv"))
            v.scalar_tensor_tensor(T1, T1, 0.125, T2, ALU.mult, ALU.mult).then_inc(*vec_did.tick("kk"))
            vec.wait_ge(*vec_did.at("kk"))
            v.scalar_tensor_tensor(g3(T2), g3(A), -1.0, par("k_a"), ALU.add, ALU.mult).then_inc(*vec_did.tick("ka"))
            vec.wait_ge(*act_did.at("px"))
            v.scalar_tensor_tensor(AR[:, :, 0:CK], c3(T1), -1.0, c3(LW), ALU.mult, ALU.mult).then_inc(*vec_did.tick("a_hat"))
            vec.wait_ge(*vec_did.at("ka"))
            v.scalar_tensor_tensor(K, T2, 1.0, K, ALU.add, ALU.mult).then_inc(*vec_did.tick("k"))
            vec.wait_ge(*vec_did.at("a_hat"))
            v.tensor_tensor(T1, T1, A, ALU.mult).then_inc(*vec_did.tick("b"))
            vec.wait_ge(*act_did.at("p"))
            v.tensor_tensor(AR[:, :, CK:P], c3(R), c3(T4), ALU.mult).then_inc(*vec_did.tick("r_hat"))
            p3 = g3(T4)
            v.tensor_copy(pc[:, :, 0:4], p3[:, :, CK - 1:TP:CK])
            v.tensor_copy(pc[:, :, 4:12], p3[:, :, TP + TS - 1::TS]).then_inc(*vec_did.tick("pc"))
            vec.wait_ge(*act_did.at("pi"))
            vec.wait_ge(*vec_did.at("b"))
            v.tensor_tensor(BK[64:128, :, 0:CK], c3(T1)[64:128], c3(T3)[64:128], ALU.mult)
            v.tensor_tensor(BK[0:64, :, CK:P], c3(T1)[0:64], c3(T3)[0:64], ALU.mult)
            v.tensor_tensor(BK[0:64, :, 0:CK], c3(K)[0:64], c3(T3)[0:64], ALU.mult)
            v.tensor_tensor(BK[64:128, :, CK:P], c3(K)[64:128], c3(T3)[64:128], ALU.mult).then_inc(*vec_did.tick("k_hat"))
            vec.wait_ge(*pool_did.at("rr"))
            vec.wait_ge(*vec_did.at("k"))
            v.tensor_tensor(T2, LW, K, ALU.mult).then_inc(*vec_did.tick("rk"))
            vec.wait_ge(*pe_did.at("bonus", KT - 1))
            v.scalar_tensor_tensor(g3(R), g3(V), 64.0, allbanks, ALU.mult, ALU.mult).then_inc(*vec_did.tick("bon"))

        @block.gpsimd
        def _(pool):
            pool.wait_ge(*vec_did.at("cum"))
            nc.gpsimd.tensor_tensor(T4, T3, LW, ALU.subtract).then_inc(*pool_did.tick("before"))
            pool.wait_ge(*vec_did.at("a_hat"))
            nc.gpsimd.tensor_tensor(g3(LW), g3(R), par("r_k"), ALU.mult).then_inc(*pool_did.tick("rr"))

        @block.scalar
        def _(act):
            s = nc.scalar
            act.wait_ge(*vec_did.at("kk0"))
            s.activation(T2, T1, ACT.Square).then_inc(*act_did.tick("sq"))
            act.wait_ge(*vec_did.at("clamp"))
            s.activation(T2, T2, ACT.Sqrt).then_inc(*act_did.tick("root"))
            act.wait_ge(*pool_did.at("before"))
            s.activation(LW, T4, ACT.Exp, scale=-DECAY).then_inc(*act_did.tick("px"))
            act.wait_ge(*act_did.at("px"))
            s.activation(T4, T3, ACT.Exp, scale=-DECAY).then_inc(*act_did.tick("p"))
            act.wait_ge(*act_did.at("p"))
            s.activation(T3, T3, ACT.Exp, scale=DECAY).then_inc(*act_did.tick("pi"))

        @block.tensor
        def _(pe):
            pe.wait_ge(*act_did.at("sq"))
            for i in range(KT):
                nc.tensor.matmul(k.bank(i, T), k.const("mean64"), T2[:, i * T:(i + 1) * T], start=True, stop=True)\
                    .then_inc(*pe_did.tick("norm", i))
            pe.wait_ge(*vec_did.at("rk"))
            for i in range(KT):
                nc.tensor.matmul(k.bank(i, T), k.const("mean64"), T2[:, i * T:(i + 1) * T], start=True, stop=True)\
                    .then_inc(*pe_did.tick("bonus", i))


def stage_rwkv_scan(k, j):
    nc, io = k.nc, k.io
    act_did, pe_did, vec_did, pool_did = k.tallies("act", "pe", "vec", "pool")
    state_in = k.sem("state_in")
    stored = k.sem("state_stored")
    V = k.at(RW["V"], KT, T)
    AR = k.at(RW["AR"], KT * NCK, P)
    BK = k.at(RW["BK"], KT * NCK, P)
    Y = k.at(RW["K"], KT, T)
    SS = k.at(RW["LW"], KT * NB, CK)
    bktok = k.at(RW["LW"] + KT * NB * CK, KT, P)
    o = RW["TMP"]
    att = k.at(o, 16, P)
    o += 16 * P
    DG, EF, TT, TM, YM = [], [], [], [], []
    for g in range(2):
        DG.append(k.at(o, 8, CK))
        EF.append(k.at(o + 512, 8, CK))
        TT.append(k.at(o + 1024, 4, CK))
        TM.append(k.at(o + 1280, 4, CK))
        YM.append(k.at(o + 1536, 4, CK))
        o += 1792
    zmask = [k.at(o, NB, CK), k.at(o + 512, NB, CK)]
    assert o + 1024 <= k.arena_size - 96, o
    z = k.normed[:, 0:1024].rearrange("p (a b) -> p a b", a=16)
    x0, S = (k.normed[:, 1024 + 512 * i:1536 + 512 * i].rearrange("p (a b) -> p a b", a=KT) for i in range(2))
    pc = k.at(k.arena_size - 96, KT, 12)
    bcols = [slice(CK, P), slice(0, CK)]
    half = [slice(0, 64), slice(64, 128)]
    b3 = lambda g, i: k.ps[:, 4 * g + i, :].rearrange("p (a b) -> p a b", b=CK)
    heads = [[(2 * f + h, f, f % 4, half[h]) for f in range(4 * g, 4 * g + 4) for h in range(2)] for g in range(2)]
    eye = k.const("eye64")
    SMP = NCK - 1

    with nc.Block() as block:
        @block.sync
        def _(sp):
            sp.dma_start(SS.rearrange("p a b -> p (a b)"), io["wkv"][j]).then_inc(state_in, 16)
            sp.wait_ge(*vec_did.at("S", 3, 1))
            sp.dma_start(io["wkv_prompt"][j], S.rearrange("p a b -> p (a b)")).then_inc(stored, 16)
            sp.wait_ge(*vec_did.at("SS", KT - 1))
            sp.dma_start(io["wkv_sample"][j], SS.rearrange("p a b -> p (a b)")).then_inc(stored, 16)
            sp.wait_ge(stored, 32)

        @block.tensor
        def _(pe):
            mm = nc.tensor.matmul

            def each(c, g, name, *jobs):
                for bank, at, lhs, rhs in jobs:
                    for h, f, q, r in heads[g]:
                        ins = mm(b3(g, bank)[r, at + q, :], lhs(h, f, q, r), rhs(h, f, q, r), start=True, stop=True)
                ins.then_inc(*pe_did.tick(name, c, g))

            d = lambda g: lambda h, f, q, r: DG[g][r, q, :]
            dt = lambda g: lambda h, f, q, r: DG[g][r, 4 + q, :]
            e = lambda g: lambda h, f, q, r: EF[g][r, q, :]
            ff = lambda g: lambda h, f, q, r: EF[g][r, 4 + q, :]
            tt = lambda g: lambda h, f, q, r: TT[g][r, q, :]
            tm = lambda g: lambda h, f, q, r: TM[g][r, q, :]
            ym = lambda g: lambda h, f, q, r: YM[g][r, q, :]
            one = lambda h, f, q, r: eye[r, :]

            for c in range(NCK):
                smp = c == SMP
                for g in range(2):
                    if c:
                        pe.wait_ge(*act_did.at("y", c - 1, g))
                        pe.wait_ge(*vec_did.at("S", c - 1, g))
                    a = lambda h, f, q, r: AR[r, f * NCK + c, 0:CK]
                    b = lambda h, f, q, r: BK[r, f * NCK + c, bcols[h % 2]]
                    each(c, g, "A", (1, 0, a, b), (1, 4, b, a))
                    for h, f, q, r in heads[g]:
                        ins = mm(k.ps[:, 4 * g + 2 + h % 2, q * P:(q + 1) * P], BK[r, f * NCK + c, :], AR[r, f * NCK + c, :],
                                 start=True, stop=True)
                    ins.then_inc(*pe_did.tick("att", c, g))
                    for f in range(4 * g, 4 * g + 4):
                        ins = nc.tensor.transpose(k.ps[:, 4 * g, (f % 4) * P:(f % 4 + 1) * P], BK[:, f * NCK + c, :], k.const("ident"))
                    ins.then_inc(*pe_did.tick("bkt", c, g))
                for g in range(2):
                    pe.wait_ge(*vec_did.at("D0", c, g))
                    each(c, g, "sq0", (1, 0, dt(g), d(g)), (1, 4, d(g), dt(g)))
                    pe.wait_ge(*act_did.at("bkt", c, g))
                    each(c, g, "vt", (0, 0, lambda h, f, q, r: V[r, f, c * CK:(c + 1) * CK], one))
                for g in range(2):
                    pe.wait_ge(*vec_did.at("att", c, g))
                    pe.wait_ge(*act_did.at("D", c, g, 0))
                    each(c, g, "T0", (2, 0, d(g), tt(g)))
                    if smp:
                        each(c, g, "sq1", (1, 0, dt(g), d(g)))
                    else:
                        each(c, g, "sq1", (1, 0, dt(g), d(g)), (1, 4, d(g), dt(g)))
                for g in range(2):
                    pe.wait_ge(*act_did.at("D", c, g, 1))
                    pe.wait_ge(*vec_did.at("T", c, g, 0))
                    each(c, g, "T1", (2, 0, d(g), tt(g)))
                    if not smp:
                        each(c, g, "sq2", (1, 0, dt(g), d(g)))
                if not smp:
                    for g in range(2):
                        pe.wait_ge(*act_did.at("D", c, g, 2))
                        pe.wait_ge(*vec_did.at("T", c, g, 1))
                        each(c, g, "T2", (2, 0, d(g), tt(g)))
                    for lev, off in ((2, e), (3, ff)):
                        for g in range(2):
                            pe.wait_ge(*vec_did.at("T", c, g, lev))
                            each(c, g, f"turn{lev}", (3, 0, tt(g), one))
                            each(c, g, f"Y{lev}", (1, 0, off(g), tt(g)))
                        for g in range(2):
                            pe.wait_ge(*act_did.at("turn", c, g, lev))
                            pe.wait_ge(*vec_did.at("Y", c, g, lev))
                            each(c, g, f"T{lev + 1}", (2, 0, tm(g), ym(g)))
                else:
                    pe.wait_ge(state_in, 16)
                    for g in range(2):
                        pe.wait_ge(*act_did.at("vt", c, g))
                        for h, f, q, r in heads[g]:
                            for b in range(NB):
                                ins = mm(b3(g, 0)[r, q, TS * b:TS * b + TS], SS[r, f * NB + b, :],
                                         AR[r, f * NCK + c, TS * b:TS * b + TS], start=True, stop=True)
                        ins.then_inc(*pe_did.tick("xs", c, g))
                for g in range(2):
                    if smp:
                        pe.wait_ge(*act_did.at("xs", c, g))
                    else:
                        pe.wait_ge(*act_did.at("vt", c, g))
                    for h, f, q, r in heads[g]:
                        if smp:
                            mm(b3(g, 3)[r, q, :], YM[g][r, q, :], eye[r, :], start=True, stop=False)
                        elif c:
                            mm(b3(g, 3)[r, q, :], AR[r, f * NCK + c, 0:CK], S[r, f, :], start=True, stop=False)
                        ins = mm(b3(g, 3)[r, q, :], att[r, h, 0:CK], z[r, h, :], start=c == 0, stop=True)
                    ins.then_inc(*pe_did.tick("x0", c, g))
                for g in range(2):
                    pe.wait_ge(*act_did.at("x0", c, g))
                    pe.wait_ge(*vec_did.at("T", c, g, 1 if smp else 4))
                    for h, f, q, r in heads[g]:
                        ins = mm(b3(g, 1)[half[1 - h % 2], q, :], TT[g][r, q, :], x0[r, f, :], start=True, stop=True)
                    ins.then_inc(*pe_did.tick("u", c, g))
                for g in range(2):
                    pe.wait_ge(*vec_did.at("u", c, g))
                    if not smp:
                        for h, f, q, r in heads[g]:
                            ins = mm(b3(g, 2)[r, q, :], bktok[:, f, r], z[:, h, :], start=True, stop=True)
                        ins.then_inc(*pe_did.tick("ds", c, g))
                    for h, f, q, r in heads[g]:
                        ins = mm(b3(g, 3)[r, q, :], z[:, h, :], att[:, h, CK:P], start=True, stop=c == 0 or smp)
                        if smp:
                            for b in range(NB):
                                ins = mm(b3(g, 3)[r, q, TS * b:TS * b + TS], SS[r, f * NB + b, :],
                                         AR[r, f * NCK + c, CK + TS * b:CK + TS * b + TS], start=False, stop=True,
                                         skip_group_check=True)
                        elif c:
                            ins = mm(b3(g, 3)[r, q, :], S[r, f, :], AR[r, f * NCK + c, CK:P], start=False, stop=True)
                    ins.then_inc(*pe_did.tick("y", c, g))
            pe.wait_ge(*act_did.at("y", SMP, 0))
            for f in range(KT):
                for par in range(2):
                    h, r = 2 * f + par, half[par]
                    pe.wait_ge(*(pool_did if par else vec_did).at("zm", h))
                    if par == 0 and f >= 4:
                        pe.wait_ge(*vec_did.at("SS", f - 4))
                    mm(k.ps[r, f % 4, :], bktok[:, f, r], zmask[par].rearrange("p a b -> p (a b)"), start=True, stop=True)\
                        .then_inc(*pe_did.tick("dss", h))

        @block.scalar
        def _(act):
            s = nc.scalar
            for c in range(NCK):
                smp = c == SMP
                for g in range(2):
                    act.wait_ge(*pe_did.at("bkt", c, g))
                    s.activation(bktok[:, 4 * g:4 * g + 4, :].rearrange("p a b -> p (a b)"), k.ps[:, 4 * g, :], ACT.Copy)\
                        .then_inc(*act_did.tick("bkt", c, g))
                for g in range(2):
                    act.wait_ge(*pe_did.at("sq0", c, g))
                    s.activation(DG[g], b3(g, 1), ACT.Copy).then_inc(*act_did.tick("D", c, g, 0))
                    act.wait_ge(*pe_did.at("vt", c, g))
                    s.activation(z[half[0], 8 * g:8 * g + 8:2, :], b3(g, 0)[half[0], 0:4, :], ACT.Copy)
                    s.activation(z[half[1], 8 * g + 1:8 * g + 8:2, :], b3(g, 0)[half[1], 0:4, :], ACT.Copy)\
                        .then_inc(*act_did.tick("vt", c, g))
                for g in range(2):
                    act.wait_ge(*pe_did.at("sq1", c, g))
                    n = 4 if smp else 8
                    s.activation(DG[g][:, 0:n, :], b3(g, 1)[:, 0:n, :], ACT.Copy).then_inc(*act_did.tick("D", c, g, 1))
                if not smp:
                    for g in range(2):
                        act.wait_ge(*pe_did.at("sq2", c, g))
                        s.activation(DG[g][:, 0:4, :], b3(g, 1)[:, 0:4, :], ACT.Copy).then_inc(*act_did.tick("D", c, g, 2))
                    for lev in (2, 3):
                        for g in range(2):
                            act.wait_ge(*pe_did.at(f"turn{lev}", c, g))
                            s.activation(TM[g], b3(g, 3)[:, 0:4, :], ACT.Copy).then_inc(*act_did.tick("turn", c, g, lev))
                else:
                    for g in range(2):
                        act.wait_ge(*pe_did.at("xs", c, g))
                        s.activation(YM[g], b3(g, 0)[:, 0:4, :], ACT.Copy).then_inc(*act_did.tick("xs", c, g))
                for g in range(2):
                    act.wait_ge(*pe_did.at("x0", c, g))
                    s.activation(x0[:, 4 * g:4 * g + 4, :], b3(g, 3)[:, 0:4, :], ACT.Copy).then_inc(*act_did.tick("x0", c, g))
                for g in range(2):
                    act.wait_ge(*pe_did.at("y", c, g))
                    s.activation(Y[:, 4 * g:4 * g + 4, c * CK:(c + 1) * CK], b3(g, 3)[:, 0:4, :], ACT.Copy)\
                        .then_inc(*act_did.tick("y", c, g))

        @block.vector
        def _(vec):
            v = nc.vector

            def masks(first, second):
                col, n = CONST_COLS[first]
                assert CONST_COLS[second][0] == col + CK
                m = k.consts[:, col:col + 2 * CK].rearrange("p (a b) -> p a b", a=2)
                return m.unsqueeze(2).to_broadcast([P, 2, 4, CK])

            four = lambda a: a.rearrange("p (m q) b -> p m q b", m=2)
            for c in range(NCK):
                smp = c == SMP
                sfx = "s" if smp else "p"
                for g in range(2):
                    vec.wait_ge(*pe_did.at("A", c, g))
                    v.tensor_tensor(four(DG[g]), four(b3(g, 1)), masks(f"dA_{sfx}", f"dG_{sfx}"), ALU.mult)\
                        .then_inc(*vec_did.tick("D1", c, g))
                    if not smp:
                        v.tensor_tensor(four(EF[g]), b3(g, 1)[:, 0:4, :].unsqueeze(1).to_broadcast([P, 2, 4, CK]),
                                        masks("eA", "fA"), ALU.mult)
                    vec.wait_ge(*vec_did.at("D1", c, g))
                    v.tensor_tensor(TT[g], DG[g][:, 4:8, :], bcm(eye, 4), ALU.add).then_inc(*vec_did.tick("D0", c, g))
                    vec.wait_ge(*pe_did.at("att", c, g))
                    for par in range(2):
                        ins = v.tensor_tensor(att[:, 8 * g + par:8 * g + 8:2, :], k.ps[:, 4 * g + 2 + par, :].rearrange("p (a b) -> p a b", a=4),
                                              bcm(k.const(f"att_{sfx}"), 4), ALU.mult)
                    ins.then_inc(*vec_did.tick("att", c, g))

                def add_tt(lev):
                    for g in range(2):
                        vec.wait_ge(*pe_did.at(f"T{lev}", c, g))
                        v.tensor_tensor(TT[g], TT[g], b3(g, 2)[:, 0:4, :], ALU.add).then_inc(*vec_did.tick("T", c, g, lev))

                add_tt(0)
                add_tt(1)
                if not smp:
                    add_tt(2)
                    for lev in (2, 3):
                        for g in range(2):
                            vec.wait_ge(*pe_did.at(f"Y{lev}", c, g))
                            v.tensor_copy(YM[g], b3(g, 1)[:, 0:4, :]).then_inc(*vec_did.tick("Y", c, g, lev))
                        vec.wait_ge(*vec_did.at("T", c, 1, lev))
                        add_tt(lev + 1)
                for g in range(2):
                    vec.wait_ge(*pe_did.at("u", c, g))
                    v.tensor_copy(z[half[1], 8 * g:8 * g + 8:2, :], b3(g, 1)[half[1], 0:4, :])
                    v.tensor_copy(z[half[0], 8 * g + 1:8 * g + 8:2, :], b3(g, 1)[half[0], 0:4, :]).then_inc(*vec_did.tick("u", c, g))
                if smp:
                    continue
                for g in range(2):
                    fs = slice(4 * g, 4 * g + 4)
                    vec.wait_ge(*pe_did.at("y" if c else "ds", c, g))
                    if c:
                        v.tensor_tensor(S[:, fs, :], S[:, fs, :], b3(g, 2)[:, 0:4, :], ALU.add).then_inc(*vec_did.tick("S0", c, g))
                        vec.wait_ge(*vec_did.at("S0", c, g))
                        v.tensor_tensor(S[:, fs, :], S[:, fs, :], bc(pc[:, fs, c], CK), ALU.mult).then_inc(*vec_did.tick("S", c, g))
                    else:
                        v.tensor_tensor(S[:, fs, :], b3(g, 2)[:, 0:4, :], bc(pc[:, fs, c], CK), ALU.mult)\
                            .then_inc(*vec_did.tick("S", c, g))
            vec.wait_ge(*vec_did.at("u", SMP, 1))
            vec.wait_ge(*pe_did.at("y", SMP, 1))
            for f in range(KT):
                if f:
                    vec.wait_ge(*pe_did.at("dss", 2 * f - 2))
                v.tensor_tensor(zmask[0], bcm(z[:, 2 * f, :], NB), bc(k.const("seq"), CK), ALU.mult).then_inc(*vec_did.tick("zm", 2 * f))
                for fd in ([f - 1] if f else []) + ([f] if f == KT - 1 else []):
                    vec.wait_ge(*pe_did.at("dss", 2 * fd + 1))
                    sf = SS[:, fd * NB:(fd + 1) * NB, :]
                    v.tensor_tensor(sf, sf, k.ps[:, fd % 4, :].rearrange("p (a b) -> p a b", a=NB), ALU.add)\
                        .then_inc(*vec_did.tick("SS0", fd))
                    vec.wait_ge(*vec_did.at("SS0", fd))
                    v.tensor_tensor(sf, sf, bc(pc[:, fd, 4:12], CK), ALU.mult).then_inc(*vec_did.tick("SS", fd))

        @block.gpsimd
        def _(pool):
            pool.wait_ge(*vec_did.at("u", SMP, 1))
            pool.wait_ge(*pe_did.at("y", SMP, 1))
            for f in range(KT):
                if f:
                    pool.wait_ge(*pe_did.at("dss", 2 * f - 1))
                nc.gpsimd.tensor_tensor(zmask[1], bcm(z[:, 2 * f + 1, :], NB), bc(k.const("seq"), CK), ALU.mult)\
                    .then_inc(*pool_did.tick("zm", 2 * f + 1))


def stage_rwkv_output(k, j):
    nc = k.nc
    act_did, pe_did, vec_did, pool_did = k.tallies("act", "pe", "vec", "pool")
    p0 = k.panel
    k.panel += 4
    Y, BON, G = (k.at(RW[n], KT, T) for n in ("K", "R", "G"))
    flat = lambda a: a.rearrange("p a b -> p (a b)")
    SQ, RS = k.at(RW["AR"], KT, T), k.at(RW["BK"], KT, T)
    par = lambda n: bc(k.param(f"{n}{j}", 0, KT), T)
    allbanks = k.ps[:, :, 0:T]
    with nc.Block() as block:
        @block.sync
        def _(sp):
            k.load_panels(sp, pe_did, p0, 4)

        @block.tensor
        def _(pe):
            for i in range(KT):
                ins = nc.tensor.matmul(k.bank(i, T), k.const("mean64"), Y[:, i, :], start=True, stop=True)
            ins.then_inc(*pe_did.tick("mean"))
            pe.wait_ge(*act_did.at("sq"))
            for i in range(KT):
                ins = nc.tensor.matmul(k.bank(i, T), k.const("mean64"), SQ[:, i, :], start=True, stop=True)
            ins.then_inc(*pe_did.tick("var"))
            pe.wait_ge(*act_did.at("root"))
            out_project_pe(k, pe, pe_did, vec_did, p0, lambda i: Y[:, i, :], KT, lambda e, i: e.wait_ge(*vec_did.at("gated", i)))

        @block.scalar
        def _(act):
            act.wait_ge(*vec_did.at("centred"))
            nc.scalar.activation(flat(SQ), flat(Y), ACT.Square).then_inc(*act_did.tick("sq"))
            act.wait_ge(*pe_did.at("var"))
            nc.scalar.activation(RS, allbanks, ACT.Sqrt, bias=k.eps(1)).then_inc(*act_did.tick("root"))

        @block.vector
        def _(vec):
            v = nc.vector
            vec.wait_ge(*pe_did.at("mean"))
            v.tensor_tensor(Y, Y, allbanks, ALU.subtract).then_inc(*vec_did.tick("centred"))
            vec.wait_ge(*act_did.at("root"))
            v.reciprocal(RS, RS).then_inc(*vec_did.tick("rs"))
            vec.wait_ge(*vec_did.at("rs"))
            v.tensor_tensor(Y, Y, RS, ALU.mult).then_inc(*vec_did.tick("n"))
            vec.wait_ge(*vec_did.at("n"))
            for i in range(KT):
                v.tensor_scalar(Y[:, i, :], Y[:, i, :], k.param(f"lnx_w{j}", i), k.param(f"lnx_b{j}", i), ALU.mult, ALU.add)\
                    .then_inc(*vec_did.tick("w", i))
            for i in range(KT):
                vec.wait_ge(*vec_did.at("w", i))
                v.tensor_tensor(Y[:, i, :], Y[:, i, :], BON[:, i, :], ALU.add).then_inc(*vec_did.tick("b", i))
            for i in range(KT):
                vec.wait_ge(*vec_did.at("b", i))
                v.tensor_tensor(Y[:, i, :], Y[:, i, :], G[:, i, :], ALU.mult).then_inc(*vec_did.tick("gated", i))
            out_project_vec(k, vec, pe_did, vec_did)


HEADS = 16
ML, _o = {}, 0
for _n, _s in (("WUK", 2048), ("WUKT", 2048), ("WUV", 2048), ("CN", 2 * T), ("KPE", T), ("QN", KT * T), ("QP", 4 * T),
               ("OT", KT * T), ("KN", KT * TP), ("VT", 2 * C), ("REST", 0)):
    ML[_n] = _o
    _o += _s
ML_END = _o
HEAD_ROWS = [(h, h // 2, slice(64 * (h % 2), 64 * (h % 2) + 64)) for h in range(HEADS)]


def stage_mla_project(k, l):
    nc, io = k.nc, k.io
    act_did, pe_did, vec_did = k.tallies("act", "pe", "vec")
    landed = k.sem("mla_weights")
    stored = k.sem("mla_stored")
    p0 = k.panel
    k.panel += 7
    wuk, wuv = k.at(ML["WUK"], 2, C), k.at(ML["WUV"], 2, C)
    CN, KPE, QN, QP = k.at(ML["CN"], 2, T), k.at(ML["KPE"], T), k.at(ML["QN"], KT, T), k.at(ML["QP"], 4, T)
    KN, VT = k.at(ML["KN"], KT, TP), k.at(ML["VT"], 2, C)
    o = ML["REST"]
    QA = k.at(o, 4, T)
    CA = k.at(o + 4 * T, 2, T)
    KA = k.at(o + 6 * T, T)
    SQ = k.at(o + 7 * T, KT, T)
    RQ = k.at(o + 15 * T, KT, T)
    RP = k.at(o + 23 * T, 4, T)
    SK = k.at(o + 27 * T, KT, TP)
    RK = k.at(o + 27 * T + 2048, KT, TP)
    r3 = k.at(o + 27 * T + 4096, 3, T)
    SP4 = k.at(ML["OT"], 4, T)
    sw = k.at(ML["OT"] + 4 * T, 4, T)
    flat = lambda a: a.rearrange("p a b -> p (a b)")
    x = k.normed
    kinds = [("qa", m) for m in range(4)] + [("c", m) for m in range(2)] + [("kp", 0)]
    kinds += [("qn", m) for m in range(8)] + [("qp", m) for m in range(4)] + [("kn", m) for m in range(8)]
    kinds += [("v", m) for m in range(4)]

    with nc.Block() as block:
        @block.sync
        def _(sp):
            sp.dma_start(flat(wuk), io["w_uk"]).then_inc(landed, 16)
            sp.dma_start(flat(k.at(ML["WUKT"], 8, 256)), io["w_ukT"]).then_inc(landed, 16)
            sp.dma_start(flat(wuv), io["w_uv"]).then_inc(landed, 16)
            k.load_panels(sp, pe_did, p0, 7)
            sp.wait_ge(*vec_did.at("cn", 1))
            sp.dma_start(io["ckv"], flat(CN)).then_inc(stored, 16)
            sp.wait_ge(*vec_did.at("kpe"))
            sp.dma_start(io["kpe"], KPE[0:32, :]).then_inc(stored, 16)
            sp.wait_ge(stored, 32)

        @block.tensor
        def _(pe):
            mm = nc.tensor.matmul
            norm_pe(k, pe, act_did, pe_did, flat(SQ))
            pe.wait_ge(*vec_did.at("rs"))
            for n, (what, m) in enumerate(kinds):
                if what == "qn" and m == 0:
                    pe.wait_ge(*act_did.at("sqa"))
                    for i in range(4):
                        mm(k.bank(4, T), k.const("mean512"), SQ[:, i, :], start=i == 0, stop=i == 3)
                    for i in range(2):
                        mm(k.bank(5, T), k.const("mean256"), SQ[:, 4 + i, :], start=i == 0, stop=i == 1)
                    mm(k.bank(6, T), k.const("mean32"), SQ[:, 6, :], start=True, stop=True).then_inc(*pe_did.tick("lat"))
                    pe.wait_ge(*vec_did.at("kpn"))
                    mm(k.bank(7, T), k.const("perm"), KA, start=True, stop=True).then_inc(*pe_did.tick("kperm"))
                    pe.wait_ge(*vec_did.at("qan", 3))
                    pe.wait_ge(landed, 48)
                if n >= 4:
                    pe.wait_ge(*act_did.at("t", n - 4))
                out = k.bank(n % 4, T)
                also = []
                if what in ("qa", "c", "kp"):
                    p = p0 + {"qa": m // 2, "c": 2, "kp": 3}[what]
                    if m % 2 == 0:
                        k.wait_panel(pe, p)
                    for i in range(8):
                        if n == 0:
                            pe.wait_ge(*vec_did.at("x", i))
                        ins = mm(out, k.tile(p, (m % 2) * 8 + i), x[:, i * T:(i + 1) * T], start=i == 0, stop=i == 7)
                    also = [("panel", p)]
                elif what in ("qn", "qp"):
                    p = p0 + (4 + m // 4 if what == "qn" else 6)
                    if m % 4 == 0:
                        k.wait_panel(pe, p)
                    for i in range(4):
                        ins = mm(out, k.tile(p, (m % 4) * 4 + i), QA[:, i, :], start=i == 0, stop=i == 3)
                    also = [("panel", p)]
                elif what == "kn":
                    if m == 0:
                        pe.wait_ge(*vec_did.at("cn", 1))
                    for i in range(2):
                        ins = mm(out[:, 0:TP], wuk[:, i, m * P:(m + 1) * P], CN[:, i, 0:TP], start=i == 0, stop=i == 1)
                else:
                    t, half = m // 2, m % 2
                    for i in range(2):
                        ins = mm(k.bank(n % 4), CN[:, i, t * P:(t + 1) * P], wuv[:, i, half * 512:half * 512 + 512],
                                 start=i == 0, stop=i == 1)
                ins.then_inc(*pe_did.tick("t", n, also=also))
            pe.wait_ge(*act_did.at("sqn"))
            pe.wait_ge(*vec_did.at("kpe"))
            for i in range(KT):
                ins = mm(k.bank(i, T), k.const("mean64"), SQ[:, i, :], start=True, stop=True)
            ins.then_inc(*pe_did.tick("qstat"))
            pe.wait_ge(*act_did.at("sqp"))
            pe.wait_ge(*act_did.at("rootq"))
            for i in range(4):
                mm(k.bank(i, T), k.const("mean32"), SP4[:, i, :], start=True, stop=True)
            for i in range(KT):
                ins = mm(k.ps[:, 4 + i // 2, (i % 2) * TP:(i % 2 + 1) * TP], k.const("mean64"), SK[:, i, :], start=True, stop=True)
            ins.then_inc(*pe_did.tick("kstat"))
            pe.wait_ge(*vec_did.at("qpn"))
            for i in range(4):
                ins = mm(k.bank(i, T), k.const("perm"), QP[:, i, :], start=True, stop=True)
            ins.then_inc(*pe_did.tick("qperm"))

        @block.scalar
        def _(act):
            s = nc.scalar
            norm_act(k, act, act_did, pe_did, flat(SQ), r3[:, 0, :])
            for n, (what, m) in enumerate(kinds):
                act.wait_ge(*pe_did.at("t", n))
                b = k.bank(n % 4, T)
                dst = {"qa": lambda: QA[:, m, :], "c": lambda: CA[:, m, :], "kp": lambda: KA, "qn": lambda: QN[:, m, :],
                       "qp": lambda: QP[:, m, :], "kn": lambda: KN[:, m, :],
                       "v": lambda: VT[:, m // 2, (m % 2) * 512:(m % 2) * 512 + 512]}[what]()
                src = b[:, 0:TP] if what == "kn" else k.bank(n % 4) if what == "v" else b
                s.activation(dst, src, ACT.Copy).then_inc(*act_did.tick("t", n))
                if what == "kp":
                    act.wait_ge(*act_did.at("t", n))
                    s.activation(SQ[:, 0:4, :], QA, ACT.Square)
                    s.activation(SQ[:, 4:6, :], CA, ACT.Square)
                    s.activation(SQ[:, 6, :], KA, ACT.Square).then_inc(*act_did.tick("sqa"))
                    act.wait_ge(*pe_did.at("lat"))
                    act.wait_ge(*vec_did.at("x", KT - 1))
                    s.activation(r3, k.ps[:, 4:7, 0:T], ACT.Sqrt, bias=k.eps(0)).then_inc(*act_did.tick("rlat"))
            act.wait_ge(*act_did.at("t", len(kinds) - 1))
            s.activation(flat(SQ), flat(QN), ACT.Square).then_inc(*act_did.tick("sqn"))
            s.activation(flat(SP4), flat(QP), ACT.Square)
            s.activation(flat(SK), flat(KN), ACT.Square).then_inc(*act_did.tick("sqp"))
            act.wait_ge(*pe_did.at("qstat"))
            s.activation(RQ, k.ps[:, :, 0:T], ACT.Sqrt, bias=k.eps(0)).then_inc(*act_did.tick("rootq"))
            act.wait_ge(*pe_did.at("kstat"))
            s.activation(RP, k.ps[:, 0:4, 0:T], ACT.Sqrt, bias=k.eps(0))
            s.activation(flat(RK), k.ps[:, 4:8, :].rearrange("p a b -> p (a b)"), ACT.Sqrt, bias=k.eps(0))\
                .then_inc(*act_did.tick("rootk"))

        @block.vector
        def _(vec):
            v = nc.vector
            norm_vec(k, vec, act_did, vec_did, r3[:, 0, :], f"norm_mix{l}")
            vec.wait_ge(*act_did.at("rlat"))
            v.reciprocal(r3, r3).then_inc(*vec_did.tick("r3"))
            vec.wait_ge(*vec_did.at("r3"))
            v.scalar_tensor_tensor(KA, KA, k.param("kr"), r3[:, 2, :], ALU.mult, ALU.mult).then_inc(*vec_did.tick("kpn"))
            for i in range(4):
                v.scalar_tensor_tensor(QA[:, i, :], QA[:, i, :], k.param("q_norm", i), r3[:, 0, :], ALU.mult, ALU.mult)\
                    .then_inc(*vec_did.tick("qan", i))
            for i in range(2):
                v.scalar_tensor_tensor(CN[:, i, :], CA[:, i, :], k.param("kv_norm", i), r3[:, 1, :], ALU.mult, ALU.mult)\
                    .then_inc(*vec_did.tick("cn", i))
            vec.wait_ge(*vec_did.at("kpn"))
            v.tensor_tensor(KPE, KA, k.const("cos"), ALU.mult).then_inc(*vec_did.tick("kc"))
            vec.wait_ge(*pe_did.at("kperm"))
            v.tensor_tensor(sw[:, 0, :], k.bank(7, T), k.const("sin"), ALU.mult).then_inc(*vec_did.tick("ks"))
            vec.wait_ge(*vec_did.at("ks"))
            v.tensor_tensor(KPE, KPE, sw[:, 0, :], ALU.add).then_inc(*vec_did.tick("kpe"))
            vec.wait_ge(*act_did.at("rootq"))
            v.reciprocal(RQ, RQ).then_inc(*vec_did.tick("rq"))
            vec.wait_ge(*vec_did.at("rq"))
            v.tensor_tensor(QN, QN, RQ, ALU.mult).then_inc(*vec_did.tick("qn0"))
            vec.wait_ge(*act_did.at("rootk"))
            v.reciprocal(RP, RP).then_inc(*vec_did.tick("rp"))
            vec.wait_ge(*vec_did.at("rp"))
            v.scalar_tensor_tensor(QP, QP, k.param("qr"), RP, ALU.mult, ALU.mult).then_inc(*vec_did.tick("qpn"))
            v.reciprocal(RK, RK).then_inc(*vec_did.tick("rk"))
            vec.wait_ge(*vec_did.at("rk"))
            v.tensor_tensor(KN, KN, RK, ALU.mult).then_inc(*vec_did.tick("kn"))
            v.tensor_scalar(flat(QN), flat(QN), k.param("qn"), k.param("kn"), ALU.mult, ALU.mult).then_inc(*vec_did.tick("qn"))
            vec.wait_ge(*pe_did.at("qperm"))
            v.tensor_tensor(sw, k.ps[:, 0:4, 0:T], bcm(k.const("sin"), 4), ALU.mult).then_inc(*vec_did.tick("qs"))
            v.tensor_tensor(QP, QP, bcm(k.const("cos"), 4), ALU.mult).then_inc(*vec_did.tick("qc"))
            vec.wait_ge(*vec_did.at("qc"))
            v.tensor_tensor(QP, QP, sw, ALU.add).then_inc(*vec_did.tick("qp"))


def stage_mla_prompt(k):
    nc = k.nc
    act_did, pe_did, vec_did, pool_did = k.tallies("act", "pe", "vec", "pool")
    KPE, QN, QP = k.at(ML["KPE"], T), k.at(ML["QN"], KT, T), k.at(ML["QP"], 4, T)
    KN, VT, OT = k.at(ML["KN"], KT, TP), k.at(ML["VT"], 2, C), k.at(ML["OT"], KT, T)
    o = ML["REST"]
    S = [k.at(o + 1024 * i, 4, 256) for i in range(2)]
    PT = [k.at(o + 2048 + 1024 * i, 8, P) for i in range(2)]
    st = k.at(o + 4096, 8, 16)
    QM = [k.at(o + 4096 + 128 + 512 * i, 4, P) for i in range(2)]
    NG = 8

    def head(g, i):
        h = (g % 4) * 4 + (i % 2) * 2 + i // 2
        return h, h // 2, slice(64 * (h % 2), 64 * (h % 2) + 64)

    with nc.Block() as block:
        @block.tensor
        def _(pe):
            mm = nc.tensor.matmul

            def scores(g):
                qt = g // 4
                nk = (qt + 1) * P
                if g >= 2:
                    pe.wait_ge(*vec_did.at("s", g - 2))
                pe.wait_ge(*pool_did.at("qm", g))
                for i in range(4):
                    h, f, r = head(g, i)
                    out = k.ps[:, (g % 2) * 2 + i // 2, (i % 2) * 256:(i % 2) * 256 + nk]
                    mm(out, QN[r, f, qt * P:(qt + 1) * P], KN[r, f, 0:nk], start=True, stop=False)
                    ins = mm(out, QM[g % 2][:, h % 4, :], KPE[:, 0:nk], start=False, stop=True)
                ins.then_inc(*pe_did.tick("s", g))

            def values(g):
                qt = g // 4
                pe.wait_ge(*vec_did.at("p", g))
                if g:
                    pe.wait_ge(*act_did.at("pt", g - 1))
                for i in range(4):
                    for kt in range(qt + 1):
                        ins = nc.tensor.transpose(k.ps[:, 4 + i // 2, ((i % 2) * 2 + kt) * P:((i % 2) * 2 + kt + 1) * P],
                                                  S[g % 2][:, i, kt * P:(kt + 1) * P], k.const("ident"))
                ins.then_inc(*pe_did.tick("pt", g))
                pe.wait_ge(*act_did.at("pt", g))
                if g >= 2:
                    pe.wait_ge(*act_did.at("o", g - 2))
                for i in range(4):
                    h, f, r = head(g, i)
                    for kt in range(qt + 1):
                        ins = mm(k.ps[r, 6 + g % 2, (i % 2) * P:(i % 2 + 1) * P], VT[:, kt, h * 64:h * 64 + 64],
                                 PT[g % 2][:, 2 * i + kt, :], start=kt == 0, stop=kt == qt)
                ins.then_inc(*pe_did.tick("o", g))

            for g in range(NG + 1):
                if g < NG:
                    scores(g)
                if g:
                    values(g - 1)

        @block.gpsimd
        def _(pool):
            nc.gpsimd.memset(QM[0], 0.0)
            nc.gpsimd.memset(QM[1], 0.0).then_inc(*pool_did.tick("zero"))
            pool.wait_ge(*pool_did.at("zero"))
            for g in range(NG):
                if g >= 2:
                    pool.wait_ge(*pe_did.at("s", g - 2))
                for a in range(4):
                    rows = slice(32 * a, 32 * a + 32)
                    ins = nc.gpsimd.tensor_copy(QM[g % 2][rows, a, :], QP[rows, g % 4, (g // 4) * P:(g // 4 + 1) * P])
                ins.then_inc(*pool_did.tick("qm", g))

        @block.vector
        def _(vec):
            v = nc.vector
            for g in range(NG):
                qt = g // 4
                Sg = S[g % 2]
                ps = k.ps[:, (g % 2) * 2:(g % 2) * 2 + 2, :].rearrange("p a b -> p (a b)").rearrange("p (a b) -> p a b", a=4)
                vec.wait_ge(*pe_did.at("s", g))
                if g >= 2:
                    vec.wait_ge(*pe_did.at("pt", g - 2))
                v.tensor_tensor(Sg[:, :, qt * P:(qt + 1) * P], ps[:, :, qt * P:(qt + 1) * P], bcm(k.const("causal"), 4), ALU.add)
                if qt:
                    v.tensor_copy(Sg[:, :, 0:P], ps[:, :, 0:P])
                v.tensor_copy(st[:, g, 12:13], ps[:, 0, 0:1]).then_inc(*vec_did.tick("s", g))
                vec.wait_ge(*vec_did.at("s", g))
                v.tensor_reduce(st[:, g, 0:4], Sg[:, :, 0:(qt + 1) * P], AX, ALU.max).then_inc(*vec_did.tick("m", g))
                vec.wait_ge(*vec_did.at("m", g))
                v.tensor_scalar(st[:, g, 4:8], st[:, g, 0:4], -MLA_SCALE, None, ALU.mult).then_inc(*vec_did.tick("nm", g))
                vec.wait_ge(*act_did.at("e", g, 3))
                v.reciprocal(st[:, g, 12:16], st[:, g, 8:12]).then_inc(*vec_did.tick("rd", g))
                vec.wait_ge(*vec_did.at("rd", g))
                v.tensor_tensor(Sg[:, :, 0:(qt + 1) * P], Sg[:, :, 0:(qt + 1) * P], bc(st[:, g, 12:16], (qt + 1) * P), ALU.mult)\
                    .then_inc(*vec_did.tick("p", g))

        @block.scalar
        def _(act):
            s = nc.scalar

            def exps(g):
                n = (g // 4 + 1) * P
                act.wait_ge(*vec_did.at("nm", g))
                for i in range(4):
                    s.activation(S[g % 2][:, i, 0:n], S[g % 2][:, i, 0:n], ACT.Exp, bias=st[:, g, 4 + i:5 + i], scale=MLA_SCALE,
                                 accum_out=st[:, g, 8 + i:9 + i]).then_inc(*act_did.tick("e", g, i))

            def out(g):
                act.wait_ge(*pe_did.at("pt", g))
                if g >= 2:
                    act.wait_ge(*pe_did.at("o", g - 2))
                for kt in range(g // 4 + 1):
                    ins = s.activation(PT[g % 2][:, kt::2, :],
                                       k.ps[:, 4:6, :].rearrange("p a b -> p (a b)").rearrange("p (a b) -> p a b", a=8)[:, kt::2, :],
                                       ACT.Copy)
                ins.then_inc(*act_did.tick("pt", g))
                act.wait_ge(*pe_did.at("o", g))
                f = (g % 4) * 2
                s.activation(OT[:, f:f + 2, (g // 4) * P:(g // 4 + 1) * P],
                             k.ps[:, 6 + g % 2, 0:256].rearrange("p (a b) -> p a b", a=2), ACT.Copy).then_inc(*act_did.tick("o", g))

            for g in range(NG + 1):
                if g < NG:
                    exps(g)
                if g:
                    out(g - 1)


def stage_mla_sample(k):
    nc, io = k.nc, k.io
    act_did, pe_did, vec_did, pool_did = k.tallies("act", "pe", "vec", "pool")
    landed = [k.sem("pages_a"), k.sem("pages_b")]
    wuk, wukT = k.at(ML["WUK"], 2, C), k.at(ML["WUKT"], KT, 256)
    CN, KPE, QN, QP = k.at(ML["CN"], 2, T), k.at(ML["KPE"], T), k.at(ML["QN"], KT, T), k.at(ML["QP"], 4, T)
    o = ML["KN"]
    pages = k.at(o, 16, 640)
    o += 16 * 640
    SQ = [k.at(o + 1024 * i, HEADS, 64) for i in range(2)]
    o += 2048
    QL = k.at(o, 2, NB, P)
    o += 2048
    QX = k.at(o, NB, P)
    o += 1024
    OL = k.at(ML_OL, 2, HEADS, 64)
    o = ML_SMALL
    mx, diag, rden, cnew_a, cnew_b, ss = (k.at(o + 256 * i, 256) for i in range(6))
    m1 = ss[:, 128:129]
    cnew = [cnew_a, cnew_b]
    S = [k.normed[:, 1152 * i:1152 * (i + 1)].rearrange("p (a b) -> p a b", a=9) for i in range(2)]

    with nc.Block() as block:
        @block.sync
        def _(sp):
            for b in range(NB):
                if b >= 2:
                    sp.wait_ge(*pe_did.at("pv", b - 2))
                for kt in range(NPG):
                    page = sp.value_load(k.table[0:1, b * NPG + kt:b * NPG + kt + 1], min_val=0, max_val=POOL - 1)
                    sp.dma_start(pages[:, (b % 2) * NPG + kt, :],
                                 io["pages"][bass.ds(page, 1), :, :].rearrange("a p n -> (a p) n")).then_inc(landed[b % 2], 16)

        @block.gpsimd
        def _(pool):
            nc.gpsimd.memset(QX, 0.0).then_inc(*pool_did.tick("zero"))
            for i in range(2):
                nc.gpsimd.memset(S[i][:, 8, :], NEG).then_inc(*pool_did.tick("neg", i))

        @block.tensor
        def _(pe):
            mm = nc.tensor.matmul
            for rc in range(2):
                for h, f, r in HEAD_ROWS:
                    ins = mm(k.ps[:, 2 * rc + h % 2, f * 64:(f + 1) * 64], wukT[r, f, rc * P:(rc + 1) * P],
                             QN[r, f, TP:T], start=True, stop=True)
            ins.then_inc(*pe_did.tick("ql"))
            pe.wait_ge(*act_did.at("ql"))
            pe.wait_ge(*vec_did.at("qx"))

            def tile(b, kt):
                n = b * 9 + kt
                if kt == 0:
                    pe.wait_ge(landed[b % 2], 16 * NPG * (b // 2 + 1))
                if kt < NPG:
                    pg = pages[:, (b % 2) * NPG + kt, :]
                    ct, kp, m = [pg[:, 256:384], pg[:, 384:512]], pg[:, 512:640], P
                else:
                    cs = slice(TP + TS * b, TP + TS * b + TS)
                    ct, kp, m = [CN[:, 0, cs], CN[:, 1, cs]], KPE[:, cs], TS
                if n >= 2:
                    pe.wait_ge(*act_did.at("sq", n - 2))
                    pe.wait_ge(*vec_did.at("s", n - 2))
                for half in range(2):
                    for rc in range(2):
                        ins = mm(k.ps[0:m, 2 * (n % 2) + half, :], ct[rc], wuk[:, rc, half * 512:half * 512 + 512],
                                 start=rc == 0, stop=rc == 1)
                ins.then_inc(*pe_did.tick("kraw", n))
                sc = k.ps[0:m, 4 + n % 2, :]
                for rc in range(2):
                    mm(sc[:, 0:P], ct[rc], QL[:, rc, b, :], start=rc == 0, stop=rc == 1)
                mm(sc[:, P:2 * P], kp, QX[:, b, :], start=True, stop=True).then_inc(*pe_did.tick("s", n))

            def turn(b):
                pe.wait_ge(*vec_did.at("mx", b))
                pe.wait_ge(*act_did.at("cn", b))
                nc.tensor.transpose(k.ps[:, 6, 0:P], mx[:, 0:P], k.const("ident")).then_inc(*pe_did.tick("mt", b))

            def turn_new(b):
                if b:
                    pe.wait_ge(*vec_did.at("sub", b - 1))
                for rc in range(2):
                    ins = nc.tensor.transpose(k.ps[0:TS, 6, 256 + P * rc:256 + P * rc + P],
                                              CN[:, rc, TP + TS * b:TP + TS * b + TS], k.const("ident"))
                ins.then_inc(*pe_did.tick("cn", b))

            def spread(b):
                pe.wait_ge(*vec_did.at("diag", b))
                mm(k.ps[:, 6, P:2 * P], k.const("ones"), diag[:, 0:P], start=True, stop=True).then_inc(*pe_did.tick("mb", b))

            def values(b):
                pe.wait_ge(*act_did.at("e", b))
                if b:
                    pe.wait_ge(*vec_did.at("ol", b - 1))
                s = S[b % 2]
                for part in range(3):
                    for kt in range(9):
                        rows = slice(0, P if kt < 8 else TS)
                        lhs = k.const("ones") if part == 2 else \
                            pages[:, (b % 2) * NPG + kt, part * P:(part + 1) * P] if kt < 8 else cnew[b % 2][:, part * P:(part + 1) * P]
                        ins = mm(k.ps[:, 7, part * P:(part + 1) * P], lhs[rows, :], s[rows, kt, :], start=kt == 0, stop=kt == 8)
                ins.then_inc(*pe_did.tick("pv", b))

            for b in range(NB + 1):
                for kt in range(9):
                    if b < NB:
                        tile(b, kt)
                    if b < NB and kt == 5:
                        turn_new(b)
                    if b and kt == 1:
                        turn(b - 1)
                    if b and kt == 3:
                        spread(b - 1)
                    if b and kt == 6:
                        values(b - 1)

        @block.scalar
        def _(act):
            s = nc.scalar
            act.wait_ge(*pe_did.at("ql"))
            for rc in range(2):
                for par in range(2):
                    ins = s.activation(QL[:, rc, :, :].rearrange("p b (h q) -> p h b q", h=HEADS)[:, par::2, :, :],
                                       k.ps[:, 2 * rc + par, :].rearrange("p (f b q) -> p f b q", f=KT, b=NB), ACT.Copy)
            ins.then_inc(*act_did.tick("ql"))

            def root(n):
                m = P if n % 9 < NPG else TS
                act.wait_ge(*vec_did.at("ss", n))
                s.activation(ss[0:m, 32 + 16 * (n % 2):48 + 16 * (n % 2)], ss[0:m, 16 * (n % 2):16 * (n % 2) + 16], ACT.Sqrt,
                             bias=k.eps(2, slice(0, m))).then_inc(*act_did.tick("root", n))

            for b in range(NB + 1):
                for kt in range(9):
                    if b == NB and kt == 0:
                        root(NB * 9 - 1)
                    if b < NB:
                        n = b * 9 + kt
                        m = P if kt < NPG else TS
                        if n:
                            root(n - 1)
                        act.wait_ge(*pe_did.at("kraw", n))
                        if n >= 2:
                            act.wait_ge(*vec_did.at("ss", n - 2))
                        s.activation(SQ[n % 2][0:m, :, :].rearrange("p a b -> p (a b)"),
                                     k.ps[0:m, 2 * (n % 2):2 * (n % 2) + 2, :].rearrange("p a b -> p (a b)"), ACT.Square)\
                            .then_inc(*act_did.tick("sq", n))
                    if b < NB and kt == 6:
                        act.wait_ge(*pe_did.at("cn", b))
                        s.activation(cnew[b % 2][0:TS, :], k.ps[0:TS, 6, 256:512], ACT.Copy).then_inc(*act_did.tick("cn", b))
                    if b and kt == 4:
                        act.wait_ge(*vec_did.at("sub", b - 1))
                        sb = S[(b - 1) % 2]
                        s.activation(sb.rearrange("p a b -> p (a b)"), sb.rearrange("p a b -> p (a b)"), ACT.Exp, scale=MLA_SCALE)\
                            .then_inc(*act_did.tick("e", b - 1))

        @block.vector
        def _(vec):
            v = nc.vector
            vec.wait_ge(*pool_did.at("zero"))
            for a in range(4):
                rows = slice(32 * a, 32 * a + 32)
                ins = v.tensor_copy(QX[rows, :, :].rearrange("p b (g a q) -> p g a b q", g=4, a=4)[:, :, a, :, :],
                                    QP[rows, :, TP:T].rearrange("p g (b q) -> p g b q", b=NB))
            ins.then_inc(*vec_did.tick("qx"))
            vec.wait_ge(*pool_did.at("neg", 1))
            for b in range(NB + 1):
                for kt in range(9):
                    if b < NB:
                        n = b * 9 + kt
                        m = P if kt < NPG else TS
                        s1, rk = ss[0:m, 16 * (n % 2):16 * (n % 2) + 16], ss[0:m, 32 + 16 * (n % 2):48 + 16 * (n % 2)]
                        vec.wait_ge(*act_did.at("sq", n))
                        v.tensor_reduce(s1, SQ[n % 2][0:m, :, :], AX, ALU.add).then_inc(*vec_did.tick("ss", n))
                        vec.wait_ge(*act_did.at("root", n))
                        v.reciprocal(rk, rk).then_inc(*vec_did.tick("rk", n))
                        vec.wait_ge(*vec_did.at("rk", n))
                        vec.wait_ge(*pe_did.at("s", n))
                        if kt == 0 and b >= 2:
                            vec.wait_ge(*pe_did.at("pv", b - 2))
                        d = S[b % 2][0:m, kt, :]
                        v.scalar_tensor_tensor(d.rearrange("p (h q) -> p h q", h=HEADS),
                                               k.ps[0:m, 4 + n % 2, 0:P].rearrange("p (h q) -> p h q", h=HEADS), 8.0,
                                               bc(rk, TS), ALU.mult, ALU.mult).then_inc(*vec_did.tick("s0", n))
                        vec.wait_ge(*vec_did.at("s0", n))
                        v.tensor_tensor(d, d, k.ps[0:m, 4 + n % 2, P:2 * P], ALU.add).then_inc(*vec_did.tick("s", n))
                        if kt == 8:
                            vec.wait_ge(*vec_did.at("s", n))
                            dh = d.rearrange("p (h q) -> p h q", h=HEADS)
                            v.tensor_tensor(dh, dh, bcm(k.const("new8", slice(0, TS)), HEADS), ALU.add).then_inc(*vec_did.tick("new", b))
                            vec.wait_ge(*vec_did.at("new", b))
                            v.tensor_reduce(mx[:, 0:P], S[b % 2].rearrange("p k c -> p c k"), AX, ALU.max)\
                                .then_inc(*vec_did.tick("mx", b))
                    if b and kt == 1:
                        vec.wait_ge(*pe_did.at("mt", b - 1))
                        v.tensor_reduce(m1[:, 0:1], k.ps[:, 6, 0:P], AX, ALU.max).then_inc(*vec_did.tick("m1", b - 1))
                        vec.wait_ge(*vec_did.at("m1", b - 1))
                        v.tensor_scalar(diag[:, 0:P], k.const("ident"), m1[:, 0:1], None, ALU.mult).then_inc(*vec_did.tick("diag", b - 1))
                    if b and kt == 3:
                        vec.wait_ge(*pe_did.at("mb", b - 1))
                        sb = S[(b - 1) % 2]
                        v.tensor_tensor(sb, sb, bcm(k.ps[:, 6, P:2 * P], 9), ALU.subtract).then_inc(*vec_did.tick("sub", b - 1))
                    if b and kt == 7:
                        vec.wait_ge(*pe_did.at("pv", b - 1))
                        v.reciprocal(rden[:, 0:P], k.ps[:, 7, 256:384]).then_inc(*vec_did.tick("rd", b - 1))
                        vec.wait_ge(*vec_did.at("rd", b - 1))
                        for rc in range(2):
                            ins = v.tensor_tensor(OL[:, rc, :, (b - 1) * TS:b * TS],
                                                  k.ps[:, 7, rc * P:(rc + 1) * P].rearrange("p (h q) -> p h q", h=HEADS),
                                                  rden[:, 0:P].rearrange("p (h q) -> p h q", h=HEADS), ALU.mult)
                        ins.then_inc(*vec_did.tick("ol", b - 1))


ML_OL = ML["KN"] + 16 * 640 + 2048 + 2048 + 1024
ML_SMALL = ML_OL + 2048
assert ML_SMALL + 6 * 256 <= 33400, ML_SMALL


def stage_mla_output(k):
    nc = k.nc
    act_did, pe_did, vec_did = k.tallies("act", "pe", "vec")
    p0 = k.panel
    k.panel += 4
    wuv, OL, OT = k.at(ML["WUV"], 2, C), k.at(ML_OL, 2, HEADS, 64), k.at(ML["OT"], KT, T)
    with nc.Block() as block:
        @block.sync
        def _(sp):
            k.load_panels(sp, pe_did, p0, 4)

        @block.tensor
        def _(pe):
            for h, f, r in HEAD_ROWS:
                for rc in range(2):
                    ins = nc.tensor.matmul(k.ps[r, 7, f * 64:(f + 1) * 64], wuv[:, rc, h * 64:(h + 1) * 64], OL[:, rc, h, :],
                                           start=rc == 0, stop=rc == 1)
            ins.then_inc(*pe_did.tick("uv"))
            out_project_pe(k, pe, pe_did, vec_did, p0, lambda i: OT[:, i, :], KT, lambda e, i: e.wait_ge(*act_did.at("uv")))

        @block.scalar
        def _(act):
            act.wait_ge(*pe_did.at("uv"))
            nc.scalar.activation(OT[:, :, TP:T], k.ps[:, 7, :].rearrange("p (a b) -> p a b", a=KT), ACT.Copy)\
                .then_inc(*act_did.tick("uv"))

        @block.vector
        def _(vec):
            out_project_vec(k, vec, pe_did, vec_did)


MH = 32
MT = 16
MB, _o = {}, 0
for _n, _s in (("XBC", 24 * T), ("ZS", MT * T), ("Y", MT * T), ("AC", T), ("DT", T), ("EA", T), ("TE", T), ("TM", 9 * MH),
               ("EE", 10 * MH), ("REST", 0)):
    MB[_n] = _o
    _o += _s


def stage_mamba_project(k, l):
    nc, io = k.nc, k.io
    act_did, pe_did, vec_did, pool_did = k.tallies("act", "pe", "vec", "pool")
    landed = k.sem("conv_in")
    stored = k.sem("conv_stored")
    p0 = k.panel
    k.panel += 21
    XBC, ZS, DT = k.at(MB["XBC"], 24, T), k.at(MB["ZS"], MT, T), k.at(MB["DT"], T)
    o = MB["REST"]
    NS = 3
    rw = TP + 3 + NB * 11
    raw = [k.at(o + rw * i, rw) for i in range(NS)]
    o += rw * NS
    acc = [k.at(o + T * i, T) for i in range(NS)]
    o += T * NS
    cin = k.at(o, 24, 24)
    o += 576
    cout = k.at(o, 24, 27)
    o += 648
    SQ = k.at(o, KT * T)
    o += KT * T
    rs = k.at(o, T)
    x = k.normed
    rawp = lambda i: raw[i % NS][:, 0:TP + 3]
    raws = lambda i: raw[i % NS][:, TP + 3:rw].rearrange("p (b t) -> p b t", b=NB)
    accs = lambda i: acc[i % NS][:, TP:T].rearrange("p (b t) -> p b t", b=NB)
    ntile = 16 + 24 + 1

    with nc.Block() as block:
        @block.sync
        def _(sp):
            sp.dma_start(cin.rearrange("p a b -> p (a b)"), io["conv_in"]).then_inc(landed, 16)
            k.load_panels(sp, pe_did, p0, 21)

        @block.tensor
        def _(pe):
            norm_pe(k, pe, act_did, pe_did, SQ)
            for n in range(ntile):
                p = p0 + n // 2
                if n % 2 == 0:
                    k.wait_panel(pe, p)
                if n >= 4:
                    pe.wait_ge(*act_did.at("t", n - 4))
                m = P if n < 40 else MH
                for i in range(KT):
                    if n == 0:
                        pe.wait_ge(*vec_did.at("x", i))
                    ins = nc.tensor.matmul(k.bank(n % 4, T)[0:m, :], k.tile(p, (n % 2) * 8 + i)[:, 0:m], x[:, i * T:(i + 1) * T],
                                           start=i == 0, stop=i == KT - 1)
                ins.then_inc(*pe_did.tick("t", n, also=[("panel", p)]))

        @block.scalar
        def _(act):
            s = nc.scalar
            norm_act(k, act, act_did, pe_did, SQ, rs)
            for n in range(ntile):
                act.wait_ge(*pe_did.at("t", n))
                b = k.bank(n % 4, T)
                if n < 16:
                    s.activation(ZS[:, n, :], b, ACT.Silu).then_inc(*act_did.tick("t", n))
                elif n < 40:
                    i = n - 16
                    if i >= NS:
                        act.wait_ge(*vec_did.at("conv", i - NS))
                        act.wait_ge(*pool_did.at("out", i - NS))
                    s.activation(rawp(i)[:, 3:TP + 3], b[:, 0:TP], ACT.Copy)
                    s.activation(raws(i)[:, :, 3:11], b[:, TP:T].rearrange("p (b t) -> p b t", b=NB), ACT.Copy)\
                        .then_inc(*act_did.tick("t", n))
                else:
                    s.activation(DT[0:MH, :], b[0:MH, :], ACT.Identity, bias=k.param("dt_bias")[0:MH, :]).then_inc(*act_did.tick("t", n))
                if n >= 17:
                    i = n - 17
                    act.wait_ge(*vec_did.at("conv", i))
                    s.activation(XBC[:, i, :], acc[i % NS], ACT.Silu, bias=k.param("conv_b", i)).then_inc(*act_did.tick("xbc", i))

        @block.gpsimd
        def _(pool):
            for i in range(NS):
                nc.gpsimd.memset(raw[i][:, 0:3], 0.0).then_inc(*pool_did.tick("zero", i))
            for i in range(24):
                pool.wait_ge(*act_did.at("t", 16 + i))
                nc.gpsimd.tensor_copy(cout[:, i, 0:3], rawp(i)[:, TP:TP + 3])
                nc.gpsimd.tensor_copy(cout[:, i, 3:27].rearrange("p (b t) -> p b t", b=NB), raws(i)[:, :, 8:11])\
                    .then_inc(*pool_did.tick("out", i))
            pool.wait_ge(*pool_did.at("out", 23))
            nc.gpsimd.dma_start(io["conv_out"], cout.rearrange("p a b -> p (a b)")).then_inc(stored, 16)
            pool.wait_ge(stored, 16)

        @block.vector
        def _(vec):
            v = nc.vector
            norm_vec(k, vec, act_did, vec_did, rs, f"norm_mix{l}")
            vec.wait_ge(landed, 16)
            vec.wait_ge(*pool_did.at("zero", NS - 1))
            for i in range(24):
                if i >= NS:
                    vec.wait_ge(*act_did.at("xbc", i - NS))
                    vec.wait_ge(*vec_did.at("conv", i - NS))
                v.tensor_copy(raws(i)[:, :, 0:3], cin[:, i, :].rearrange("p (b t) -> p b t", b=NB)).then_inc(*vec_did.tick("pad", i))
                vec.wait_ge(*vec_did.at("pad", i))
                vec.wait_ge(*act_did.at("t", 16 + i))
                for j in range(4):
                    w = k.param("conv_w", j * 24 + i)
                    if j:
                        vec.wait_ge(*vec_did.at("tap", i, j - 1))
                        v.scalar_tensor_tensor(acc[i % NS][:, 0:TP], rawp(i)[:, j:j + TP], w, acc[i % NS][:, 0:TP], ALU.mult, ALU.add)
                        ins = v.scalar_tensor_tensor(accs(i), raws(i)[:, :, j:j + TS], w, accs(i), ALU.mult, ALU.add)
                    else:
                        v.tensor_scalar(acc[i % NS][:, 0:TP], rawp(i)[:, 0:TP], w, None, ALU.mult)
                        ins = v.tensor_scalar(accs(i), raws(i)[:, :, 0:TS], w, None, ALU.mult)
                    ins.then_inc(*vec_did.tick("tap", i, j, also=[("conv", i)] if j == 3 else []))


def stage_mamba_decay(k):
    nc = k.nc
    act_did, pe_did, vec_did = k.tallies("act", "pe", "vec")
    AC, DT, EA, TE = (k.at(MB[n], T, rows=MH) for n in ("AC", "DT", "EA", "TE"))
    TM = k.at(MB["TM"], 9, MH)
    EE = k.at(MB["EE"], 10, MH)
    EAB = k.at(MB["Y"], MT, T)
    o = MB["REST"]
    t1, ends, dg, A = k.at(o, T, rows=MH), k.at(o + T, 10, rows=MH), k.at(o + T + 16, 10, MH, rows=MH), k.at(o + 2 * T + 64, 1, rows=MH)
    t2 = k.at(o + 3 * T, T, rows=MH)
    with nc.Block() as block:
        @block.scalar
        def _(act):
            s = nc.scalar
            s.activation(A, k.param("a_log")[0:MH, :], ACT.Exp)
            s.activation(t1, DT, ACT.Abs).then_inc(*act_did.tick("abs"))
            act.wait_ge(*act_did.at("abs"))
            s.activation(t2, t1, ACT.Exp, scale=-1.0).then_inc(*act_did.tick("e"))
            act.wait_ge(*act_did.at("e"))
            s.activation(t1, t2, ACT.Ln, bias=1.0).then_inc(*act_did.tick("ln"))
            act.wait_ge(*vec_did.at("ac"))
            s.activation(EA, AC, ACT.Exp).then_inc(*act_did.tick("ea"))
            act.wait_ge(*vec_did.at("te"))
            s.activation(TE, TE, ACT.Exp).then_inc(*act_did.tick("te"))
            act.wait_ge(*pe_did.at("ee"))
            s.activation(EE, k.ps[:, 7, 0:10 * MH].rearrange("p (a b) -> p a b", a=10), ACT.Exp).then_inc(*act_did.tick("ee"))
            for f in range(MT):
                act.wait_ge(*pe_did.at("eab", f))
                s.activation(EAB[:, f, :], k.bank(f % 4, T), ACT.Copy).then_inc(*act_did.tick("eab", f))

        @block.vector
        def _(vec):
            v = nc.vector
            vec.wait_ge(*act_did.at("ln"))
            v.scalar_tensor_tensor(DT, DT, 0.0, t1, ALU.max, ALU.add).then_inc(*vec_did.tick("dt"))
            vec.wait_ge(*vec_did.at("dt"))
            v.tensor_scalar(t2, DT, A, -1.0, ALU.mult, ALU.mult).then_inc(*vec_did.tick("da"))
            vec.wait_ge(*vec_did.at("da"))
            v.tensor_tensor_scan(AC, k.const("reset_m", slice(0, MH)), t2, 0.0, ALU.mult, ALU.add).then_inc(*vec_did.tick("ac"))
            vec.wait_ge(*vec_did.at("ac"))
            v.tensor_copy(ends[:, 0:2], AC[:, P - 1:TP:P])
            v.tensor_copy(ends[:, 2:10], AC[:, TP + TS - 1::TS]).then_inc(*vec_did.tick("ends"))
            vec.wait_ge(*vec_did.at("ends"))
            v.tensor_tensor(dg, bcm(k.const("ident", slice(0, MH))[:, 0:MH], 10), bc(ends, MH), ALU.mult).then_inc(*vec_did.tick("dg"))
            v.tensor_tensor(TE[:, 0:TP].rearrange("p (a b) -> p a b", a=2), bc(ends[:, 0:2], P),
                            AC[:, 0:TP].rearrange("p (a b) -> p a b", a=2), ALU.subtract)
            v.tensor_tensor(TE[:, TP:T].rearrange("p (a b) -> p a b", a=NB), bc(ends[:, 2:10], TS),
                            AC[:, TP:T].rearrange("p (a b) -> p a b", a=NB), ALU.subtract).then_inc(*vec_did.tick("te"))
            vec.wait_ge(*pe_did.at("tm"))
            for i in range(3):
                v.tensor_copy(TM[:, 3 * i:3 * i + 2, :], k.ps[:, 6, 96 * i:96 * i + 64].rearrange("p (a b) -> p a b", a=2))
                ins = v.tensor_copy(TM[0:64, 3 * i + 2, :], k.ps[0:64, 6, 96 * i + 64:96 * i + 96])
            ins.then_inc(*vec_did.tick("tm"))

        @block.tensor
        def _(pe):
            mm = nc.tensor.matmul
            pe.wait_ge(*vec_did.at("dg"))
            mm(k.bank(7, T), k.const("ones")[0:MH, :], dg.rearrange("p a b -> p (a b)"), start=True, stop=True)\
                .then_inc(*pe_did.tick("ee"))
            pe.wait_ge(*act_did.at("te"))
            for i, src in enumerate((DT, AC, TE)):
                for c in range(3):
                    n = P if c < 2 else 64
                    ins = nc.tensor.transpose(k.ps[0:n, 6, 96 * i + 32 * c:96 * i + 32 * c + 32], src[:, c * P:c * P + n],
                                              k.const("ident")[0:MH, 0:MH])
            ins.then_inc(*pe_did.tick("tm"))
            for f in range(MT):
                if f >= 4:
                    pe.wait_ge(*act_did.at("eab", f - 4))
                for h in (2 * f, 2 * f + 1):
                    r = slice(64 * (h % 2), 64 * (h % 2) + 64)
                    ins = mm(k.bank(f % 4, T)[r, :], k.const("ident")[0:MH, h:h + 1].to_broadcast([MH, 64]), EA, start=True, stop=True)
                ins.then_inc(*pe_did.tick("eab", f))


def stage_mamba_scan(k):
    nc, io = k.nc, k.io
    act_did, pe_did, vec_did, pool_did = k.tallies("act", "pe", "vec", "pool")
    state_in = [k.sem("ssm_in_a"), k.sem("ssm_in_b")]
    state_out = [k.sem("ssm_out_a"), k.sem("ssm_out_b")]
    prompt_out = k.sem("ssm_prompt_out")
    XBC, Y, AC = k.at(MB["XBC"], 24, T), k.at(MB["Y"], MT, T), k.at(MB["AC"], T, rows=MH)
    TM, EE = k.at(MB["TM"], 9, MH), k.at(MB["EE"], 10, MH)
    o = MB["REST"]
    XDT, XDW, HT = (k.at(o + 2048 * i, MH, 64) for i in range(3))
    HB = [k.at(o + 2048 * (3 + i), MH, 64) for i in range(2)]
    o += 2048 * 5
    SEG = [k.at(o + 512 * i, 4, P) for i in range(2)]
    CB, BT = k.at(o + 1024, 4, P), k.at(o + 1536, 4, P)
    YT = k.at(o + 2048, 2, P)
    YI = k.normed[:, 0:1024].rearrange("p (a b) -> p a b", a=MT)
    BM = [k.normed[:, 1024 + 512 * i:1536 + 512 * i].rearrange("p (a b) -> p a b", a=4) for i in range(2)]
    flat = lambda a: a.rearrange("p a b -> p (a b)")
    span = [(0, P), (P, P), (TP, 64)]

    with nc.Block() as block:
        @block.sync
        def _(sp):
            for b in range(2):
                sp.dma_start(flat(HB[b]), io["ssm"][b]).then_inc(state_in[b], 16)
            sp.wait_ge(*vec_did.at("HT", 1))
            sp.dma_start(io["ssm_prompt"], flat(HT)).then_inc(prompt_out, 16)
            for b in range(NB):
                sp.wait_ge(*vec_did.at("HB", b))
                sp.dma_start(io["ssm_sample"][b], flat(HB[b % 2])).then_inc(state_out[b % 2], 16)
                if b + 2 < NB:
                    sp.wait_ge(state_out[b % 2], 16 * (b // 2 + 1))
                    sp.dma_start(flat(HB[b % 2]), io["ssm"][b + 2]).then_inc(state_in[b % 2], 16)
            sp.wait_ge(prompt_out, 16)
            for q in state_out:
                sp.wait_ge(q, 16 * NB // 2)

        @block.tensor
        def _(pe):
            mm = nc.tensor.matmul
            for c in range(3):
                t0, n = span[c]
                tok = slice(t0, t0 + n)
                if c:
                    pe.wait_ge(*vec_did.at("y", c - 1, 7))
                    if c < 3:
                        pe.wait_ge(*vec_did.at("HT", c - 1))
                for f in range(MT):
                    ins = nc.tensor.transpose(k.ps[0:n, f // 4, (f % 4) * P:(f % 4 + 1) * P], XBC[:, f, tok], k.const("ident"))
                ins.then_inc(*pe_did.tick("xt", c))
                for g in range(4):
                    ins = nc.tensor.transpose(k.ps[0:n, 4, g * P:(g + 1) * P], XBC[:, 16 + g, tok], k.const("ident"))
                ins.then_inc(*pe_did.tick("bt", c))
                for g in range(4):
                    ins = mm(k.ps[0:n, 5, g * P:g * P + n], XBC[:, 16 + g, tok], XBC[:, 20 + g, tok], start=True, stop=True)
                ins.then_inc(*pe_did.tick("cb", c))

                def seg(q):
                    if q >= 2:
                        pe.wait_ge(*vec_did.at("seg", c, q - 2))
                    for i in range(4):
                        h = 4 * q + i
                        ins = mm(k.ps[0:n, 6 + q % 2, i * P:i * P + n], k.const("ident")[0:MH, h:h + 1].to_broadcast([MH, n]),
                                 AC[:, tok], start=True, stop=True)
                    ins.then_inc(*pe_did.tick("seg", c, q))

                def outputs(q):
                    if q == 0:
                        pe.wait_ge(*vec_did.at("xdt", c))
                    if q >= 2:
                        pe.wait_ge(*vec_did.at("y", c, q - 2))
                    if c == 1:
                        for i in range(2):
                            f = 2 * q + i
                            mm(k.ps[:, 2 + q % 2, i * P:i * P + n], flat(HT)[:, f * P:(f + 1) * P], XBC[:, 20 + q // 2, tok],
                               start=True, stop=True)
                    pe.wait_ge(*pool_did.at("m", c, q))
                    for i in range(4):
                        r = slice(64 * (i % 2), 64 * (i % 2) + 64)
                        ins = mm(k.ps[r, q % 2, (i // 2) * P:(i // 2) * P + n], XDT[0:n, 4 * q + i, :], SEG[q % 2][0:n, i, 0:n],
                                 start=True, stop=True)
                    ins.then_inc(*pe_did.tick("y", c, q))

                for q in range(9):
                    if q < 8:
                        seg(q)
                    if q:
                        outputs(q - 1)
                if c < 2:
                    pe.wait_ge(*pool_did.at("xdw", c))
                    pe.wait_ge(*act_did.at("bt", c))
                    pe.wait_ge(*vec_did.at("seg", c, 7))
                    for g in range(4):
                        ins = mm(k.bank(4 + g), BT[0:n, g, :], flat(XDW)[0:n, 512 * g:512 * (g + 1)], start=True, stop=True)
                    ins.then_inc(*pe_did.tick("h", c))
            pe.wait_ge(*pool_did.at("xdw", 2))
            pe.wait_ge(*act_did.at("bt", 2))
            pe.wait_ge(*vec_did.at("y", 2, 7))
            pe.wait_ge(*vec_did.at("cb", 2))
            for b in range(NB):
                cols = slice(TP + TS * b, TP + TS * b + TS)
                pe.wait_ge(state_in[b % 2], 16 * (b // 2 + 1))
                for f in range(MT):
                    ins = mm(k.ps[:, 4 + f // 8, (f % 8) * 64 + TS * b:(f % 8) * 64 + TS * b + TS], flat(HB[b % 2])[:, f * P:(f + 1) * P],
                             XBC[:, 20 + f // 4, cols], start=True, stop=True)
                ins.then_inc(*pe_did.tick("ys", b))
                pe.wait_ge(*vec_did.at("bm", b))
                if b:
                    pe.wait_ge(*vec_did.at("HB", b - 1))
                for g in range(4):
                    ins = mm(k.bank(g), BM[b % 2][0:64, g, :], flat(XDW)[0:64, 512 * g:512 * (g + 1)], start=True, stop=True)
                ins.then_inc(*pe_did.tick("hb", b))

        @block.scalar
        def _(act):
            s = nc.scalar
            for c in range(3):
                _, n = span[c]
                act.wait_ge(*pe_did.at("bt", c))
                s.activation(flat(BT)[0:n, :], k.bank(4)[0:n, :], ACT.Copy).then_inc(*act_did.tick("bt", c))
                for q in range(8):
                    act.wait_ge(*vec_did.at("seg", c, q))
                    s.activation(SEG[q % 2][0:n, :, 0:n], SEG[q % 2][0:n, :, 0:n], ACT.Exp).then_inc(*act_did.tick("e", c, q))

        @block.gpsimd
        def _(pool):
            g_ = nc.gpsimd
            for c in range(3):
                _, n = span[c]
                pool.wait_ge(*vec_did.at("xdt", c))
                g_.tensor_tensor(XDW[0:n], XDT[0:n], bc(TM[0:n, 6 + c, :], 64), ALU.mult).then_inc(*pool_did.tick("xdw", c))
                pool.wait_ge(*vec_did.at("cb", c))
                for q in range(8):
                    pool.wait_ge(*act_did.at("e", c, q))
                    m = SEG[q % 2][0:n, :, 0:n]
                    g_.tensor_tensor(m, m, bcm(CB[0:n, q // 2, 0:n], 4), ALU.mult).then_inc(*pool_did.tick("m", c, q))
            for b in range(NB):
                pool.wait_ge(*pe_did.at("ys", b))
                g_.tensor_tensor(HB[b % 2], HB[b % 2], bc(EE[:, 2 + b, :], 64), ALU.mult).then_inc(*pool_did.tick("hb", b))

        @block.vector
        def _(vec):
            v = nc.vector
            for c in range(3):
                t0, n = span[c]
                vec.wait_ge(*pe_did.at("xt", c))
                if c:
                    vec.wait_ge(*pe_did.at("h", c - 1))
                v.tensor_tensor(XDT[0:n], k.ps[0:n, 0:4, :].rearrange("p a (h d) -> p (a h) d", d=64), bc(TM[0:n, c, :], 64), ALU.mult)\
                    .then_inc(*vec_did.tick("xdt", c))
                vec.wait_ge(*pe_did.at("cb", c))
                v.tensor_tensor(CB[0:n, :, 0:n], k.ps[0:n, 5, :].rearrange("p (g i) -> p g i", g=4)[:, :, 0:n],
                                bcm(k.const("tril_p" if c < 2 else "tril_s", slice(0, n)), 4), ALU.mult).then_inc(*vec_did.tick("cb", c))

                def seg(q):
                    vec.wait_ge(*pe_did.at("seg", c, q))
                    if q >= 2:
                        vec.wait_ge(*pe_did.at("y", c, q - 2))
                    for i in range(4):
                        ins = v.tensor_scalar(SEG[q % 2][0:n, i, 0:n], k.ps[0:n, 6 + q % 2, i * P:i * P + n],
                                              TM[0:n, 3 + c, 4 * q + i:4 * q + i + 1], 0.0, ALU.subtract, ALU.min)
                    ins.then_inc(*vec_did.tick("seg", c, q))

                def outputs(q):
                    vec.wait_ge(*pe_did.at("y", c, q))
                    tok = slice(t0, t0 + n)
                    if c == 1:
                        if q:
                            vec.wait_ge(*vec_did.at("y", c, q - 1))
                        v.tensor_tensor(YT, Y[:, 2 * q:2 * q + 2, tok], k.ps[:, 2 + q % 2, 0:256].rearrange("p (a b) -> p a b", a=2),
                                        ALU.mult).then_inc(*vec_did.tick("yt", q))
                        vec.wait_ge(*vec_did.at("yt", q))
                    for i in range(2):
                        f = 2 * q + i
                        dst = YI[:, f, :] if c == 2 else Y[:, f, tok]
                        ins = v.scalar_tensor_tensor(dst, XBC[:, f, tok], k.param("d_skip", f), k.ps[:, q % 2, i * P:i * P + n],
                                                     ALU.mult, ALU.add)
                    if c == 1:
                        ins.then_inc(*vec_did.tick("yd", q))
                        vec.wait_ge(*vec_did.at("yd", q))
                        ins = v.tensor_tensor(Y[:, 2 * q:2 * q + 2, tok], Y[:, 2 * q:2 * q + 2, tok], YT, ALU.add)
                    ins.then_inc(*vec_did.tick("y", c, q))

                for q in range(9):
                    if q < 8:
                        seg(q)
                    if q:
                        outputs(q - 1)
                if c < 2:
                    vec.wait_ge(*pe_did.at("h", c))
                    if c:
                        v.tensor_tensor(HT, HT, bc(EE[:, c, :], 64), ALU.mult).then_inc(*vec_did.tick("H0"))
                        vec.wait_ge(*vec_did.at("H0"))
                        v.tensor_tensor(flat(HT), flat(HT), flat(k.ps[:, 4:8, :]), ALU.add).then_inc(*vec_did.tick("HT", c))
                    else:
                        v.tensor_copy(flat(HT), flat(k.ps[:, 4:8, :])).then_inc(*vec_did.tick("HT", c))
            vec.wait_ge(*act_did.at("bt", 2))
            for b in range(NB):
                if b >= 2:
                    vec.wait_ge(*pe_did.at("hb", b - 2))
                v.tensor_scalar(flat(BM[b % 2])[0:64, :], flat(BT)[0:64, :], k.const("seq", slice(0, 64))[:, b:b + 1], None, ALU.mult)\
                    .then_inc(*vec_did.tick("bm", b))
                vec.wait_ge(*pe_did.at("hb", b))
                vec.wait_ge(*pool_did.at("hb", b))
                v.tensor_tensor(flat(HB[b % 2]), flat(HB[b % 2]), flat(k.ps[:, 0:4, :]), ALU.add).then_inc(*vec_did.tick("HB", b))
            ys = k.ps[:, 4:6, :].rearrange("p a (f t) -> p (a f) t", t=64)
            v.tensor_tensor(Y[:, :, TP:T], Y[:, :, TP:T], ys, ALU.mult).then_inc(*vec_did.tick("ysm"))
            vec.wait_ge(*vec_did.at("ysm"))
            v.tensor_tensor(Y[:, :, TP:T], Y[:, :, TP:T], YI, ALU.add).then_inc(*vec_did.tick("yfin"))


def stage_mamba_output(k):
    nc = k.nc
    act_did, pe_did, vec_did = k.tallies("act", "pe", "vec")
    p0 = k.panel
    k.panel += 8
    ZS, Y = k.at(MB["ZS"], MT, T), k.at(MB["Y"], MT, T)
    SQ, RS = k.at(MB["XBC"], MT, T), k.at(MB["REST"], 4, T)
    with nc.Block() as block:
        @block.sync
        def _(sp):
            k.load_panels(sp, pe_did, p0, 8)

        @block.vector
        def _(vec):
            v = nc.vector
            for g in range(4):
                fs = slice(4 * g, 4 * g + 4)
                v.tensor_tensor(Y[:, fs, :], Y[:, fs, :], ZS[:, fs, :], ALU.mult).then_inc(*vec_did.tick("z", g))
            for g in range(4):
                vec.wait_ge(*act_did.at("root", g))
                v.reciprocal(RS[:, g, :], RS[:, g, :]).then_inc(*vec_did.tick("rs", g))
                vec.wait_ge(*vec_did.at("rs", g))
                for f in range(4 * g, 4 * g + 4):
                    v.scalar_tensor_tensor(Y[:, f, :], Y[:, f, :], k.param("m_norm", f), RS[:, g, :], ALU.mult, ALU.mult)\
                        .then_inc(*vec_did.tick("n", f))
            out_project_vec(k, vec, pe_did, vec_did)

        @block.scalar
        def _(act):
            for g in range(4):
                fs = slice(4 * g, 4 * g + 4)
                act.wait_ge(*vec_did.at("z", g))
                nc.scalar.activation(SQ[:, fs, :], Y[:, fs, :], ACT.Square).then_inc(*act_did.tick("sq", g))
            for g in range(4):
                act.wait_ge(*pe_did.at("mean", g))
                nc.scalar.activation(RS[:, g, :], k.bank(4 + g, T), ACT.Sqrt, bias=k.eps(0)).then_inc(*act_did.tick("root", g))

        @block.tensor
        def _(pe):
            for g in range(4):
                pe.wait_ge(*act_did.at("sq", g))
                for i in range(4):
                    ins = nc.tensor.matmul(k.bank(4 + g, T), k.const("mean512"), SQ[:, 4 * g + i, :], start=i == 0, stop=i == 3)
                ins.then_inc(*pe_did.tick("mean", g))
            out_project_pe(k, pe, pe_did, vec_did, p0, lambda i: Y[:, i, :], MT, lambda e, i: e.wait_ge(*vec_did.at("n", i)))


def stage_store(k):
    nc = k.nc
    stored = k.sem("y_stored")
    with nc.Block() as block:
        @block.sync
        def _(sp):
            sp.dma_start(k.io["y"], k.hidden[:, :, :].rearrange("p a b -> p (a b)")).then_inc(stored, 16)
            sp.wait_ge(stored, 16)


INPUTS = {
    "x": (P, KT * T), "consts": CONSTS.shape, "params": (P, NPARAM), "panels": (PANELS, P, 16 * P),
    "shift": (2, P, KT * NB), "wkv": (2, P, KT * NB * CK), "w_uk": (P, 2048), "w_ukT": (P, 2048), "w_uv": (P, 2048),
    "pages": (POOL, P, 640), "conv_in": (P, 576), "ssm": (NB, P, 2048), "page_table": (1, NB * NPG),
}
OUTPUTS = {
    "y": (P, KT * T), "ckv": (P, 2 * T), "kpe": (32, T), "shift_out": (2, P, KT * 9), "wkv_prompt": (2, P, 512),
    "wkv_sample": (2, P, KT * NB * CK), "conv_out": (P, 648), "ssm_prompt": (P, 2048), "ssm_sample": (NB, P, 2048),
}


def build(nc, old):
    io = {}
    for name, shape in INPUTS.items():
        io[name] = nc.dram_tensor(f"in_{name}", list(shape), I32 if name == "page_table" else F32, kind="ExternalInput").ap()
    for name, shape in OUTPUTS.items():
        io[name] = nc.dram_tensor(f"out_{name}", list(shape), F32, kind="ExternalOutput").ap()
    with ExitStack() as ctx:
        k = Kit(nc, ctx, io, old)
        stage_load(k)
        for l in range(DEPTH):
            if l % 3 == 0:
                stage_rwkv_project(k, l, l // 3)
                stage_rwkv_prepare(k, l // 3)
                stage_rwkv_scan(k, l // 3)
                stage_rwkv_output(k, l // 3)
            elif l % 3 == 1:
                stage_mla_project(k, l)
                stage_mla_prompt(k)
                stage_mla_sample(k)
                stage_mla_output(k)
            else:
                stage_mamba_project(k, l)
                stage_mamba_decay(k)
                stage_mamba_scan(k)
                stage_mamba_output(k)
            stage_ffn(k, l)
        stage_store(k)
        assert k.panel == PANELS, (k.panel, PANELS)
    return k.new


def to_tiles(w):
    kk, m = -(-w.shape[0] // P) * P, -(-w.shape[1] // P) * P
    full = np.zeros((kk, m), np.float32)
    full[:w.shape[0], :w.shape[1]] = w
    return full.reshape(kk // P, P, m // P, P).transpose(0, 2, 1, 3)


def pack_panels(d):
    out = []

    def panel(tiles):
        tiles = list(tiles) + [np.zeros((P, P), np.float32)] * (16 - len(tiles))
        out.append(np.stack(tiles).transpose(1, 0, 2).reshape(P, 16 * P))

    def columns(w):
        t = to_tiles(w)
        per = 16 // t.shape[0]
        for m in range(0, t.shape[1], per):
            panel([t[i, mm] for mm in range(m, min(m + per, t.shape[1])) for i in range(t.shape[0])])

    def deep(w):
        t = to_tiles(w)
        for m in range(0, 8, 2):
            for q in range(4):
                panel([t[8 * q + i, m + mm] for mm in range(2) for i in range(8)])

    for l in range(DEPTH):
        if l % 3 == 0:
            j = l // 3
            for p in range(3):
                columns(d["rwkv_w_rkv"][j, p])
            g1, g2 = d["rwkv_g1"][j], d["rwkv_g2"][j]
            v1 = d["rwkv_v1"][j - 1] if j else np.zeros((C, 32), np.float32)
            v2 = d["rwkv_v2"][j - 1] if j else np.zeros((32, C), np.float32)
            wa = to_tiles(np.concatenate([d["rwkv_w1"][j], d["rwkv_a1"][j]], 1))
            ga = to_tiles(np.ascontiguousarray(g1[:, 0:P]))
            gb = to_tiles(np.concatenate([g1[:, P:160], v1], 1))
            wa2 = to_tiles(np.concatenate([d["rwkv_w2"][j], d["rwkv_a2"][j]], 0))
            ga2 = to_tiles(np.ascontiguousarray(g2[0:P]))
            gb2 = to_tiles(np.concatenate([g2[P:160], v2], 0))
            panel([wa[i, 0] for i in range(8)] + [ga[i, 0] for i in range(8)])
            panel([gb[i, 0] for i in range(8)] + [wa2[0, m] for m in range(8)])
            panel([ga2[0, m] for m in range(8)] + [gb2[0, m] for m in range(8)])
            columns(d["rwkv_w_o"][j])
        elif l % 3 == 1:
            w = d["mla_w_in"][0]
            columns(w[:, 0:512])
            columns(w[:, 512:768])
            columns(np.tile(w[:, 768:800], (1, 4)))
            uq = d["mla_w_uq"][0]
            columns(uq[:, :, 0:64].reshape(512, C))
            columns(uq[:, :, 64:96].reshape(512, 512))
            columns(d["mla_w_o"][0])
        else:
            columns(d["mamba_w_in"][0])
            columns(d["mamba_w_o"][0])
        columns(d["ffn_w1"][l])
        deep(d["ffn_w2"][l])
    assert len(out) == PANELS, (len(out), PANELS)
    return np.stack(out)


def feature_major(a):
    return a.T.reshape(-1, P, a.shape[0]).transpose(1, 0, 2)


def pack_params(d):
    out = np.zeros((P, NPARAM), np.float32)

    def put(name, a, i=0):
        a = np.asarray(a).reshape(-1, P).T
        c, _ = PARAM_COLS[name]
        out[:, c + i:c + i + a.shape[1]] = a

    for l in range(DEPTH):
        put(f"norm_mix{l}", d["norm_mix"][l])
        put(f"norm_ffn{l}", d["norm_ffn"][l])
    for j in range(2):
        put(f"mu{j}", d["rwkv_mu"][j])
        for n in ("w0", "a0", "k_k", "k_a", "r_k", "lnx_w", "lnx_b"):
            put(f"{n}{j}", d[f"rwkv_{n}"][j])
    put("v01", d["rwkv_v0"][0])
    put("q_norm", d["mla_q_norm"][0])
    put("kv_norm", d["mla_kv_norm"][0])
    put("qn", np.tile(d["mla_qn_norm"][0], 2))
    put("kn", np.tile(d["mla_kn_norm"][0], 2))
    put("qr", np.tile(d["mla_qr_norm"][0], 4))
    put("kr", np.tile(d["mla_kr_norm"][0], 4))
    put("conv_w", d["mamba_conv_w"][0])
    put("conv_b", d["mamba_conv_b"][0])
    for name in ("dt_bias", "a_log"):
        out[0:MH, PARAM_COLS[name][0]] = d[f"mamba_{name}"][0]
    put("d_skip", np.repeat(d["mamba_d"][0], 64))
    put("m_norm", d["mamba_norm"][0])
    return out


def kernel(**inputs):
    import concourse.bacc as bacc
    from concourse.bass_utils import run_bass_kernel_spmd

    d = {n: np.asarray(a) for n, a in inputs.items()}
    counts = build(bacc.Bacc("TRN2", target_bir_lowering=False, num_devices=1), None)
    nc = bacc.Bacc("TRN2", target_bir_lowering=False, num_devices=1)
    build(nc, counts)

    tokens = np.concatenate([d["x_prompt"].reshape(TP, C), d["x_sample"].reshape(NB * TS, C)], 0)
    ck, kp = d["cache_mla_ckv"][0], d["cache_mla_kpe"][0]
    ckT = ck.transpose(0, 2, 1).reshape(POOL, 2, P, PAGE).transpose(0, 2, 1, 3).reshape(POOL, P, 256)
    uk = d["mla_w_uk"][0].reshape(256, C)
    rows = lambda w: w.reshape(2, P, C).transpose(1, 0, 2).reshape(P, 2 * C)
    a = {
        "x": feature_major(tokens).reshape(P, -1),
        "consts": CONSTS,
        "params": pack_params(d),
        "panels": pack_panels(d),
        "shift": np.stack([feature_major(s).reshape(P, -1) for s in d["state_rwkv_shift"]]),
        "wkv": d["state_rwkv_wkv"].reshape(2, NB, KT, 2, CK, CK).transpose(0, 3, 5, 2, 1, 4).reshape(2, P, -1),
        "w_uk": rows(uk),
        "w_ukT": uk.T.reshape(KT, P, 256).transpose(1, 0, 2).reshape(P, -1),
        "w_uv": rows(d["mla_w_uv"][0].reshape(256, C)),
        "pages": np.concatenate([ck, ckT, np.tile(kp.transpose(0, 2, 1), (1, 4, 1))], 2),
        "conv_in": d["state_conv"][0].reshape(NB, 3, 24, P).transpose(3, 2, 0, 1).reshape(P, -1),
        "ssm": d["state_ssm"][0].transpose(0, 3, 1, 2).reshape(NB, P, -1),
        "page_table": d["page_table"].reshape(1, -1),
    }
    r = run_bass_kernel_spmd(nc, [{f"in_{n}": np.ascontiguousarray(v) for n, v in a.items()}], core_ids=[0]).results[0]
    r = {n[4:]: v for n, v in r.items()}

    token_major = lambda t, n: t.reshape(-1, n, T).transpose(2, 1, 0).reshape(T, -1)
    y = token_major(r["y"], KT)
    ckv = token_major(r["ckv"], 2)
    kpe = r["kpe"].T
    sh = r["shift_out"].reshape(2, P, KT, 9).transpose(0, 3, 2, 1).reshape(2, 9, C)
    wp = r["wkv_prompt"].reshape(2, 2, CK, KT, CK).transpose(0, 3, 1, 4, 2).reshape(2, 1, 16, CK, CK)
    ws = r["wkv_sample"].reshape(2, 2, CK, KT, NB, CK).transpose(0, 4, 3, 1, 5, 2).reshape(2, NB, 16, CK, CK)
    co = r["conv_out"].reshape(P, 24, 9, 3).transpose(2, 3, 1, 0).reshape(9, 3, 24 * P)
    sp = r["ssm_prompt"].reshape(P, MH, 64).transpose(1, 2, 0)
    ss = r["ssm_sample"].reshape(NB, P, MH, 64).transpose(0, 2, 3, 1)
    out = (y[:TP].reshape(1, TP, C), y[TP:].reshape(NB, TS, C),
           ckv[:TP].reshape(1, 1, TP, 256), kpe[:TP].reshape(1, 1, TP, 32),
           ckv[TP:].reshape(1, NB, TS, 256), kpe[TP:].reshape(1, NB, TS, 32),
           wp, sh[:, 0:1], ws, sh[:, 1:9],
           sp[None, None], co[0:1][None], ss[None], co[1:9][None])
    return tuple(np.ascontiguousarray(o) for o in out)
```
